# Optimizing a Trainium2 kernel written in Bass

```python
import math
import jax
import jax.numpy as jnp
from jax import lax
import numpy as np

D_MODEL = 1024
BATCH = 1
SEQ = 128
DEPTH = 1
DEC_BATCH = 1
DEC_SEQ = 1024
PAST_LEN = 256

GRID_W = 64
MIX_WIDTH = D_MODEL
POOL_WIDTH = MIX_WIDTH // 4
POOL_WINDOWS = (2, 4, 8, 16)
N_POOL_GROUPS = len(POOL_WINDOWS)
POOL_GROUP = POOL_WIDTH // N_POOL_GROUPS
NA_WIDTH = MIX_WIDTH // 2
NA_HEAD_DIM = 64
NA_HEADS = NA_WIDTH // NA_HEAD_DIM
NA_ROWS = 8
NA_COLS = 16
Q_BLOCK = 128
DN_WIDTH = MIX_WIDTH - POOL_WIDTH - NA_WIDTH
DN_HEAD_DIM = 64
DN_HEADS = DN_WIDTH // DN_HEAD_DIM
DN_CONV = 4
DN_CHUNK = 64
N_EXPERTS = 16
N_EXPERT_GROUPS = 4
EXPERTS_PER_GROUP = N_EXPERTS // N_EXPERT_GROUPS
TOP_K = 2
D_EXPERT = 512
IN_SIZES = (POOL_WIDTH, NA_WIDTH, NA_WIDTH, NA_WIDTH, 3 * DN_WIDTH, DN_WIDTH, 2 * DN_HEADS, 2 * DN_HEADS)
IN_WIDTH = sum(IN_SIZES)
EPS = 1e-6
F32 = jnp.float32

kernel_name = 'hybrid_pool_natten_deltanet_moe_diffusion_step'

def _rms_norm(x, g):
    xf = x.astype(F32)
    y = xf * lax.rsqrt(jnp.mean(xf * xf, axis=-1, keepdims=True) + EPS)
    return (y * g.astype(F32)).astype(x.dtype)

def _l2norm(x):
    return x * lax.rsqrt(jnp.sum(x * x, axis=-1, keepdims=True) + EPS)

def _heads(t, n):
    b, l, _ = t.shape
    return t.reshape(b, l, n, -1).transpose(0, 2, 1, 3)

def _split_cols(t, sizes):
    out, start = [], 0
    for s in sizes:
        out.append(t[..., start:start + s])
        start += s
    return out

def _multi_scale_pool(u):
    b, l, _ = u.shape
    uf = u.astype(F32)
    csum = jnp.pad(jnp.cumsum(uf, axis=1), ((0, 0), (1, 0), (0, 0)))
    t = jnp.arange(l)
    means = []
    for gi, win in enumerate(POOL_WINDOWS):
        lo = jnp.clip(t - win // 2, 0, l)
        hi = jnp.clip(t + win - win // 2, 0, l)
        cg = csum[:, :, gi * POOL_GROUP:(gi + 1) * POOL_GROUP]
        means.append((cg[:, hi] - cg[:, lo]) / (hi - lo).astype(F32)[None, :, None])
    return (jnp.concatenate(means, axis=-1) - uf).astype(u.dtype)

def _context_attention(q, k, v):
    b, h, s, d = q.shape
    nb = s // Q_BLOCK
    qb = q.reshape(b, h, nb, Q_BLOCK, d).transpose(2, 0, 1, 3, 4)
    scale = d ** -0.5

    def block(qi):
        sc = jnp.einsum('bhqd,bhkd->bhqk', qi, k).astype(F32) * scale
        p = jax.nn.softmax(sc, axis=-1).astype(v.dtype)
        return jnp.einsum('bhqk,bhkd->bhqd', p, v)

    o = lax.map(block, qb)
    return o.transpose(1, 2, 0, 3, 4).reshape(b, h, s, d)

def _neighbourhood_attention(q, k, v, k_ctx, v_ctx, rpb):
    b, h, l, d = q.shape
    rows = l // GRID_W
    kh = min(NA_ROWS, rows)
    n_loc = kh * GRID_W
    scale = d ** -0.5
    qg = q.reshape(b, h, rows, GRID_W, d)
    kg = k.reshape(b, h, rows, GRID_W, d)
    vg = v.reshape(b, h, rows, GRID_W, d)
    col = jnp.arange(GRID_W)
    col_start = jnp.clip(col - NA_COLS // 2, 0, GRID_W - NA_COLS)
    in_win = (col[None, :] >= col_start[:, None]) & (col[None, :] < col_start[:, None] + NA_COLS)
    dc_idx = jnp.clip(col[None, :] - col[:, None] + NA_COLS - 1, 0, 2 * NA_COLS - 2)
    rpb_cols = rpb.astype(F32)[:, :, dc_idx]

    def one_row(r):
        r0 = jnp.clip(r - kh // 2, 0, rows - kh)
        kb = lax.dynamic_slice_in_dim(kg, r0, kh, axis=2).reshape(b, h, n_loc, d)
        vb = lax.dynamic_slice_in_dim(vg, r0, kh, axis=2).reshape(b, h, n_loc, d)
        qr = lax.dynamic_index_in_dim(qg, r, axis=2, keepdims=False)
        dr_idx = r0 + jnp.arange(kh) - r + NA_ROWS - 1
        bias = jnp.take(rpb_cols, dr_idx, axis=1)
        bias = jnp.where(in_win[None, None], bias, -jnp.inf)
        bias = bias.transpose(0, 2, 1, 3).reshape(h, GRID_W, n_loc)
        s_loc = jnp.einsum('bhqd,bhkd->bhqk', qr, kb).astype(F32) * scale + bias
        s_ctx = jnp.einsum('bhqd,bhpd->bhqp', qr, k_ctx).astype(F32) * scale
        p = jax.nn.softmax(jnp.concatenate([s_loc, s_ctx], axis=-1), axis=-1).astype(v.dtype)
        return (jnp.einsum('bhqk,bhkd->bhqd', p[..., :n_loc], vb)
                + jnp.einsum('bhqp,bhpd->bhqd', p[..., n_loc:], v_ctx.astype(v.dtype)))

    o = lax.map(one_row, jnp.arange(rows))
    return o.transpose(1, 2, 0, 3, 4).reshape(b, h, l, d)

def _short_conv(u, w):
    kw, c = w.shape
    lo = (kw - 1) // 2
    return lax.conv_general_dilated(u, w[:, None, :].astype(u.dtype), window_strides=(1,),
                                    padding=[(lo, kw - 1 - lo)], dimension_numbers=('NWC', 'WIO', 'NWC'),
                                    feature_group_count=c)

def _gated_delta_chunked(q, k, v, g, beta, s0):
    b, h, l, dk = k.shape
    dv = v.shape[-1]
    n = l // DN_CHUNK
    c = DN_CHUNK
    q, k, v = [t.reshape(b, h, n, c, -1) for t in (q, k, v)]
    beta = beta.reshape(b, h, n, c)
    g = jnp.cumsum(g.reshape(b, h, n, c), axis=-1)
    i = jnp.arange(c)
    causal = i[:, None] >= i[None, :]
    strict = i[:, None] > i[None, :]
    decay = jnp.where(causal, jnp.exp(jnp.where(causal, g[..., :, None] - g[..., None, :], 0.0)), 0.0)
    kb = k * beta[..., None]
    lmat = jnp.where(strict, jnp.einsum('bhnid,bhnjd->bhnij', kb, k) * decay, 0.0)
    a = lmat + jnp.eye(c, dtype=F32)
    u = lax.linalg.triangular_solve(a, v * beta[..., None], left_side=True, lower=True, unit_diagonal=True)
    w = lax.linalg.triangular_solve(a, kb * jnp.exp(g)[..., None], left_side=True, lower=True, unit_diagonal=True)
    attn = jnp.einsum('bhnid,bhnjd->bhnij', q, k) * decay
    q_dec = q * jnp.exp(g)[..., None]
    k_dec = k * jnp.exp(g[..., -1:] - g)[..., None]
    g_last = jnp.exp(g[..., -1])

    def step(state, xs):
        u_c, w_c, attn_c, q_c, k_c, gl_c = xs
        v_new = u_c - jnp.einsum('bhik,bhkv->bhiv', w_c, state)
        o_c = jnp.einsum('bhik,bhkv->bhiv', q_c, state) + jnp.einsum('bhij,bhjv->bhiv', attn_c, v_new)
        state = state * gl_c[..., None, None] + jnp.einsum('bhik,bhiv->bhkv', k_c, v_new)
        return state, o_c

    xs = tuple(jnp.moveaxis(t, 2, 0) for t in (u, w, attn, q_dec, k_dec, g_last))
    s_fin, o = lax.scan(step, s0.astype(F32), xs)
    return jnp.moveaxis(o, 0, 2).reshape(b, h, l, dv), s_fin

def _bidir_deltanet(qkv, z, b_raw, a_raw, conv_w, a_log, dt_bias, norm_g, s0_fwd, s0_bwd):
    b, l, _ = qkv.shape
    qkv = jax.nn.silu(_short_conv(qkv, conv_w))
    q, k, v = [_heads(t, DN_HEADS).astype(F32) for t in jnp.split(qkv, 3, axis=-1)]
    q = _l2norm(q) * DN_HEAD_DIM ** -0.5
    k = _l2norm(k)
    beta = jax.nn.sigmoid(b_raw.astype(F32)).reshape(b, l, 2, DN_HEADS).transpose(2, 0, 3, 1)
    a_in = a_raw.astype(F32).reshape(b, l, 2, DN_HEADS).transpose(2, 0, 3, 1)
    g = -jnp.exp(a_log.astype(F32))[:, None, :, None] * jax.nn.softplus(a_in + dt_bias.astype(F32)[:, None, :, None])
    o_f, s_f = _gated_delta_chunked(q, k, v, g[0], beta[0], s0_fwd)
    flip = lambda t: jnp.flip(t, axis=2)
    o_b, s_b = _gated_delta_chunked(flip(q), flip(k), flip(v), flip(g[1]), flip(beta[1]), s0_bwd)
    o = (o_f + flip(o_b)).transpose(0, 2, 1, 3)
    o = _rms_norm(o, norm_g) * jax.nn.silu(z.astype(F32).reshape(b, l, DN_HEADS, DN_HEAD_DIM))
    return o.reshape(b, l, DN_WIDTH), s_f, s_b

def _mixers(h, lp, ctx):
    b, l, _ = h.shape
    u_pool, q_na, k_na, v_na, qkv_dn, z_dn, b_dn, a_dn = _split_cols(h @ lp['w_in'], IN_SIZES)
    pooled = _multi_scale_pool(u_pool).reshape(b, l, N_POOL_GROUPS, POOL_GROUP)
    o_pool = jnp.einsum('blgc,gce->blge', pooled, lp['w_pool']).reshape(b, l, POOL_WIDTH) * lp['pool_scale']
    qn = _rms_norm(_heads(q_na, NA_HEADS), lp['q_norm'])
    kn = _rms_norm(_heads(k_na, NA_HEADS), lp['k_norm'])
    vn = _heads(v_na, NA_HEADS)
    if ctx is None:
        o_na = _context_attention(qn, kn, vn)
        s0 = jnp.zeros((b, 2, DN_HEADS, DN_HEAD_DIM, DN_HEAD_DIM), F32)
    else:
        o_na = _neighbourhood_attention(qn, kn, vn, ctx[0], ctx[1], lp['rpb'])
        s0 = ctx[2]
    o_na = o_na.transpose(0, 2, 1, 3).reshape(b, l, NA_WIDTH)
    o_dn, s_f, s_b = _bidir_deltanet(qkv_dn, z_dn, b_dn, a_dn, lp['conv'], lp['a_log'], lp['dt_bias'],
                                     lp['dn_norm'], s0[:, 0], s0[:, 1])
    mix = jnp.concatenate([o_pool, o_na.astype(h.dtype), o_dn.astype(h.dtype)], axis=-1) @ lp['w_out']
    new_ctx = (kn, vn, jnp.stack([s_f, s_b], axis=1)) if ctx is None else None
    return mix, new_ctx

def _moe(h, w_router, b_router, w_gate, w_up, w_down):
    b, l, d = h.shape
    t = h.reshape(-1, d)
    scores = jax.nn.sigmoid((t @ w_router).astype(F32))
    sel = scores + b_router.astype(F32)
    grp = jnp.sum(lax.top_k(sel.reshape(-1, N_EXPERT_GROUPS, EXPERTS_PER_GROUP), 2)[0], axis=-1)
    best = jnp.argmax(grp, axis=-1)
    in_group = (jnp.arange(N_EXPERTS) // EXPERTS_PER_GROUP)[None, :] == best[:, None]
    _, idx = lax.top_k(jnp.where(in_group, sel, -jnp.inf), TOP_K)
    w_sel = jnp.take_along_axis(scores, idx, axis=-1)
    w_sel = w_sel / jnp.sum(w_sel, axis=-1, keepdims=True)
    gates = jnp.sum(jax.nn.one_hot(idx, N_EXPERTS, dtype=F32) * w_sel[..., None], axis=1)
    hid = jax.nn.silu(jnp.einsum('td,edf->tef', t, w_gate)) * jnp.einsum('td,edf->tef', t, w_up)
    hid = hid * gates.astype(hid.dtype)[..., None]
    return jnp.einsum('tef,efd->td', hid, w_down).reshape(b, l, d)

def _layer(x, cond, lp, w_router, b_router, ctx):
    mod = (jax.nn.silu(cond) @ lp['w_ada'] + lp['b_ada'])[:, None, :]
    sh1, sc1, g1, sh2, sc2, g2 = jnp.split(mod, 6, axis=-1)
    h = _rms_norm(x, lp['norm1']) * (1 + sc1) + sh1
    mix, new_ctx = _mixers(h, lp, ctx)
    x = x + g1 * mix
    h = _rms_norm(x, lp['norm2']) * (1 + sc2) + sh2
    x = x + g2 * _moe(h, w_router, b_router, lp['w_gate'], lp['w_up'], lp['w_down'])
    return x, new_ctx

def setup_inputs(seed: int = 0) -> dict:
    key = jax.random.key(seed)
    ks = jax.random.split(key, 32)
    nrm = lambda k, shape, s: jax.random.normal(k, shape, F32) * s
    d = D_MODEL
    dt = jnp.exp(jax.random.uniform(ks[20], (DEPTH, 2, DN_HEADS), F32, math.log(1e-3), math.log(1e-1)))
    return {
        'x_prompt': nrm(ks[0], (BATCH, SEQ, d), 1.0),
        'x_sample': nrm(ks[1], (DEC_BATCH, DEC_SEQ, d), 1.0),
        'cache_na_k': nrm(ks[2], (DEC_BATCH, DEPTH, NA_HEADS, PAST_LEN, NA_HEAD_DIM), 1.0),
        'cache_na_v': nrm(ks[3], (DEC_BATCH, DEPTH, NA_HEADS, PAST_LEN, NA_HEAD_DIM), 1.0),
        'state_dn': nrm(ks[4], (DEC_BATCH, DEPTH, 2, DN_HEADS, DN_HEAD_DIM, DN_HEAD_DIM), DN_HEAD_DIM ** -0.5),
        'c': nrm(ks[5], (DEC_BATCH, d), 1.0),
        'c_ctx': nrm(ks[6], (d,), 1.0),
        'norm1_g': 1.0 + nrm(ks[7], (DEPTH, d), 0.1),
        'norm2_g': 1.0 + nrm(ks[8], (DEPTH, d), 0.1),
        'w_ada': nrm(ks[9], (DEPTH, d, 6 * d), 0.5 * d ** -0.5),
        'b_ada': nrm(ks[10], (DEPTH, 6 * d), 0.01),
        'w_in': nrm(ks[11], (DEPTH, d, IN_WIDTH), d ** -0.5),
        'w_out': nrm(ks[12], (DEPTH, MIX_WIDTH, d), MIX_WIDTH ** -0.5),
        'w_pool': nrm(ks[13], (DEPTH, N_POOL_GROUPS, POOL_GROUP, POOL_GROUP), POOL_GROUP ** -0.5),
        'pool_scale': 1.0 + nrm(ks[14], (DEPTH, POOL_WIDTH), 0.1),
        'q_norm_g': 1.0 + nrm(ks[15], (DEPTH, NA_HEAD_DIM), 0.1),
        'k_norm_g': 1.0 + nrm(ks[16], (DEPTH, NA_HEAD_DIM), 0.1),
        'rpb': nrm(ks[17], (DEPTH, NA_HEADS, 2 * NA_ROWS - 1, 2 * NA_COLS - 1), 0.1),
        'dn_conv_w': nrm(ks[18], (DEPTH, DN_CONV, 3 * DN_WIDTH), DN_CONV ** -0.5),
        'dn_a_log': jnp.log(jax.random.uniform(ks[19], (DEPTH, 2, DN_HEADS), F32, 1.0, 16.0)),
        'dn_dt_bias': dt + jnp.log(-jnp.expm1(-dt)),
        'dn_norm_g': 1.0 + nrm(ks[21], (DEPTH, DN_HEAD_DIM), 0.1),
        'w_router': nrm(ks[22], (d, N_EXPERTS), d ** -0.5),
        'b_router': nrm(ks[23], (N_EXPERTS,), 0.01),
        'w_gate': nrm(ks[24], (DEPTH, N_EXPERTS, d, D_EXPERT), d ** -0.5),
        'w_up': nrm(ks[25], (DEPTH, N_EXPERTS, d, D_EXPERT), d ** -0.5),
        'w_down': nrm(ks[26], (DEPTH, N_EXPERTS, D_EXPERT, d), D_EXPERT ** -0.5),
    }

def reference(x_prompt, x_sample, cache_na_k, cache_na_v, state_dn, c, c_ctx, norm1_g, norm2_g, w_ada, b_ada,
              w_in, w_out, w_pool, pool_scale, q_norm_g, k_norm_g, rpb, dn_conv_w, dn_a_log, dn_dt_bias, dn_norm_g,
              w_router, b_router, w_gate, w_up, w_down):
    y_prompt = x_prompt
    y_sample = x_sample
    new_k, new_v, new_s = [], [], []
    for l in range(DEPTH):
        lp = {'norm1': norm1_g[l], 'norm2': norm2_g[l], 'w_ada': w_ada[l], 'b_ada': b_ada[l],
              'w_in': w_in[l], 'w_out': w_out[l], 'w_pool': w_pool[l], 'pool_scale': pool_scale[l],
              'q_norm': q_norm_g[l], 'k_norm': k_norm_g[l], 'rpb': rpb[l], 'conv': dn_conv_w[l],
              'a_log': dn_a_log[l], 'dt_bias': dn_dt_bias[l], 'dn_norm': dn_norm_g[l],
              'w_gate': w_gate[l], 'w_up': w_up[l], 'w_down': w_down[l]}
        y_prompt, (k_l, v_l, s_l) = _layer(y_prompt, c_ctx[None, :], lp, w_router, b_router, None)
        new_k.append(k_l)
        new_v.append(v_l)
        new_s.append(s_l)
        y_sample, _ = _layer(y_sample, c, lp, w_router, b_router,
                             (cache_na_k[:, l], cache_na_v[:, l], state_dn[:, l]))
    new_cache_na_k = jnp.stack(new_k, axis=1)
    new_cache_na_v = jnp.stack(new_v, axis=1)
    new_state_dn = jnp.stack(new_s, axis=1)
    return (y_prompt, y_sample, new_cache_na_k, new_cache_na_v, new_state_dn)


_drawn_inputs = setup_inputs


def setup_inputs(seed=0):
    import zlib

    import numpy as np

    out = dict(_drawn_inputs(seed))
    spreads = {}
    factors = {'state_dn': 6.904, 'q_norm_g': 5.658, 'rpb': 8.0, 'dn_norm_g': 2.764}
    for name, (base, spread) in spreads.items():
        noise = np.random.default_rng([zlib.crc32(name.encode()), seed]).standard_normal(out[name].shape)
        drawn = base * np.exp(spread * noise) if base else spread * noise
        out[name] = jnp.asarray(drawn.astype(out[name].dtype))
    for name, factor in factors.items():
        out[name] = (out[name] * factor).astype(out[name].dtype)
    return out
```

```python
import concourse.bass as bass
from concourse import mybir

F32 = mybir.dt.float32
U32 = mybir.dt.uint32
ALU = mybir.AluOpType
ACT = mybir.ActivationFunctionType
AX = mybir.AxisListType

P = 128
D = 1024
KD = D // P
CTX, LAT = 128, 1024
N_TOK = CTX + LAT
NT = N_TOK // P
POOL_W, NA_W, DN_W = 256, 512, 256
HEAD = 64
NA_H, DN_H = NA_W // HEAD, DN_W // HEAD
IN_W = POOL_W + 3 * NA_W + 3 * DN_W + DN_W + 4 * DN_H
PAST = 256
N_EXP, GRP, TOP = 16, 4, 2
FF = 512
EPS = 1e-6
NEG = -1e30
GRID = 64
RPB_W = 31
RPB_REP = 66
RPB_ROW = RPB_REP * RPB_W

POOL_PAD = 8
POOL_CTX = POOL_PAD
POOL_LAT = POOL_CTX + CTX + POOL_PAD
POOL_ROW = POOL_LAT + LAT + POOL_PAD
CONV_CTX = 1
CONV_LAT = CONV_CTX + CTX + 2 + 1
CONV_ROW = CONV_LAT + LAT + 2

CAP = 256
OVER = (2 * N_TOK - 2 * CAP) // P
SLOTS = N_EXP * CAP + OVER * P

COL_POOL = 0
COL_Q = COL_POOL + POOL_W
COL_K = COL_Q + NA_W
COL_V = COL_K + NA_W
COL_DN = COL_V + NA_W
COL_Z = COL_DN + 3 * DN_W

CST = {}
_at = 0
for _name, _n in (("ident", P), ("tri_f", P), ("tri_b", P), ("block", P), ("strict_f", P), ("strict_b", P),
                  ("level_f", 6 * P), ("level_b", 6 * P), ("colmask", GRID), ("before", P), ("ones", P),
                  ("grid16", 16), ("token", NT), ("over_id", OVER)):
    CST[_name] = (_at, _n)
    _at += _n
CST_W = _at


class Store:
    pass


def views(nc, s):
    arena = nc.alloc_sbuf_tensor("arena", [P, s.WORDS], F32)
    s.arena = arena

    def view(at, *shape):
        n = 1
        for x in shape:
            n *= x
        assert at + n <= s.WORDS, (at, n)
        v = arena[:, at:at + n]
        if len(shape) == 2:
            v = v.rearrange("p (a b) -> p a b", a=shape[0])
        elif len(shape) == 3:
            v = v.rearrange("p (a b c) -> p a b c", a=shape[0], b=shape[1])
        return v

    s.view = view
    s.cst = view(0, CST_W)
    cst = lambda name, *shape: view(CST[name][0], *(shape or (CST[name][1],)))
    s.ident, s.tri_f, s.tri_b, s.block = cst("ident"), cst("tri_f"), cst("tri_b"), cst("block")
    s.strict_f, s.strict_b = cst("strict_f"), cst("strict_b")
    s.level_f, s.level_b = cst("level_f", 6, P), cst("level_b", 6, P)
    s.colmask, s.before, s.ones = cst("colmask"), cst("before"), cst("ones")
    s.grid16, s.token, s.over_id = cst("grid16"), cst("token"), cst("over_id")
    at = CST_W
    s.mod_a1 = view(at, KD, 2); at += 16
    s.mod_b1 = view(at, KD, 2); at += 16
    s.gain1 = view(at, KD); at += 8
    s.gain2 = view(at, KD); at += 8
    s.epsc = view(at, 1); at += 1
    s.zero = view(at, 1); at += 1
    s.ss = view(at, NT); at += NT
    s.rstd = view(at, NT); at += NT
    s.qgain = view(at, 1); at += 1
    s.kgain = view(at, 1); at += 1
    s.pscale = view(at, 2); at += 2
    assert at <= 3072, at
    B = 3072
    s.silu = view(B, KD, 2)
    s.cond = view(B + 16, KD, 2)
    s.mod = view(B + 32, 6 * D)
    s.ada_ring = [view(B + 32 + 6 * D + i * 4096, KD, 512) for i in range(4)]
    s.b_ada = view(B + 32 + 6 * D + 4 * 4096, 6 * D)
    s.hT = view(B, KD, N_TOK)
    s.pool_fm = view(12288, 2, POOL_ROW)
    s.qkv_fm = view(14656, 6, CONV_ROW)
    s.q_tm = view(21604, NT, NA_W)
    s.k_tm = view(26212, NT, NA_W)
    s.v_tm = view(30820, NT, NA_W)
    s.zba = view(35428, NT, DN_W + 4 * DN_H)
    s.w_ring = [view(37876 + 4096 * i, KD * 512) for i in range(2)]
    s.x_all = view(21604, NT, D)
    s.xn_ring = [view(46068 + 1024 * i, D) for i in range(3)]
    s.junk = view(49140, D)
    s.zero_rows = view(50164, D)
    s.qT = view(37876, 4, N_TOK)
    s.kT = view(42484, 4, N_TOK)
    s.kcT = view(47092, 4, PAST)
    s.vc_tm = view(48116, 2, NA_W)
    s.kc_tm = view(49140, 2, NA_W)
    s.sq_ring = [view(50164 + 512 * i, 512) for i in range(2)]
    s.qk_ss = view(51188, 2 * NT * NA_H)
    s.qk_r = view(51332, 2 * NT * NA_H)
    s.kgain_row = view(51476, HEAD)
    s.kn_ctx = view(51540, NA_W)
    s.bias = [view(21604 + 896 * i, 14, GRID) for i in range(2)]
    s.bias_mid = [view(23396 + 576 * i, 9, GRID) for i in range(2)]
    s.weights = [view(24548 + 832 * i, 832) for i in range(2)]
    s.wT = [view(26212 + 896 * i, 7 * P) for i in range(2)]
    s.at_m1, s.at_max, s.at_nm, s.at_sum, s.at_inv = [view(28004 + 4 * i, 4) for i in range(5)]
    s.o_na = view(3072, NT, NA_W)
    s.o_dn = view(7680, NT, DN_W)
    s.qkv_tm = view(21604, NT, 3 * DN_W)
    at = 28516
    s.taps = view(at, 6, 4); at += 24
    s.a_log = view(at, 8); at += 8
    s.dt_bias = view(at, 8); at += 8
    s.a_in, s.a_abs, s.g, s.cum, s.g_rest, s.beta, s.beta_eg, s.dn_ss = [view(at + NT * 8 * i, NT, 8) for i in range(8)]
    at += 8 * NT * 8
    s.dn_sq = [view(at + 512 * i, 512) for i in range(2)]; at += 1024
    s.S_ctx = view(at, 2, 4, HEAD); at += 512
    s.S_lat = view(at, 2, 4, HEAD); at += 512
    s.fin_r = view(at, NT * DN_H); at += 36
    s.dn_gain = view(at, HEAD); at += 64
    s.kb, s.vb, s.kg, s.kd, s.su, s.vn = [[view(at + 512 * j + 256 * i, 256) for i in range(2)] for j in range(6)]
    at += 6 * 512
    assert at <= 35428, at
    s.conv = view(37876, 6, CONV_ROW - 3)
    at = 37876
    (s.sqT, s.skT, s.skbT, s.pos, s.neg, s.dec, s.decT, s.eb, s.L, s.LT, s.attT, s.X, s.Z,
     s.Y) = [[view(at + 1024 * j + 512 * i, 512) for i in range(2)] for j in range(14)]
    at += 14 * 1024
    s.swT = [view(14656 + 512 * i, 512) for i in range(2)]
    s.sqd = [view(15680 + 512 * i, 512) for i in range(2)]
    s.sqT, s.skT, s.skbT, s.swT, s.sqd = [[v[0:HEAD, :] for v in pair] for pair in (s.sqT, s.skT, s.skbT, s.swT, s.sqd)]
    assert at <= 53120, at
    s.oT = view(21604, KD, N_TOK)
    s.pool_a = view(37876, 2, POOL_ROW)
    s.pool_b = view(40244, 2, POOL_ROW)
    s.pooled = view(42612, 2, POOL_ROW)
    s.pool_rc = view(44980, 2, POOL_ROW)
    s.w_pool = view(47348, 2, HEAD)
    s.w_out = view(37876, KD, D)
    s.g1_row = view(46068, 2, D)
    s.xr_ring = [view(48116 + D * i, D) for i in range(2)]
    s.x1 = view(B, NT, D)
    s.h2T = view(12288, KD, N_TOK)
    s.a2_row = view(21604, 2, D)
    s.b2_row = view(23652, 2, D)
    s.n2_row = view(25700, D)
    s.w_router = view(26724, KD, N_EXP)
    s.junk2 = view(26852, D)
    s.h2_ring = [view(27876 + D * i, D) for i in range(3)]
    s.zero_slots = view(30948, SLOTS // P).bitcast(U32)
    at = 52000
    s.b_router = view(at, N_EXP); at += 16
    s.slot_idx = view(at, SLOTS // P).bitcast(U32); at += SLOTS // P
    s.slot_hi, s.slot_lo, s.token_id = [view(at + NT * i, NT).bitcast(U32) for i in range(3)]; at += 3 * NT
    s.w_hi, s.w_lo = [view(at + NT * i, NT) for i in range(2)]; at += 2 * NT
    s.over_table = view(at, OVER + 1).bitcast(U32); at += OVER + 1
    assert at <= 52736
    at = 31000
    s.route = {}
    for name in ("score", "sel", "rank", "tmp", "mask", "weight", "off", "slot"):
        s.route[name] = view(at, NT * N_EXP); at += NT * N_EXP
    for name in ("gsum", "grank", "gtmp", "gmask"):
        s.route[name] = view(at, NT * 4); at += NT * 4
    for name in ("wsum", "hi", "lo"):
        s.route[name] = view(at, NT); at += NT
    for name in ("total", "over", "o16", "cum"):
        s.route[name] = view(at, N_EXP); at += N_EXP
    s.over_cmp = view(at, OVER, N_EXP)
    s.we_ring = [view(12288 + 4096 * i, 4096) for i in range(6)]
    s.hg = [view(36864 + 2048 * i, 2, D) for i in range(2)]
    s.hgT = [view(40960 + 2048 * i, KD, CAP) for i in range(2)]
    s.hid = [view(45056 + 1024 * i, 4, CAP) for i in range(2)]
    s.sg = [view(47104 + 256 * i, CAP) for i in range(2)]
    s.y_ring = [view(47616 + 1024 * i, D) for i in range(3)]
    s.further_gate = view(50688, 4, P)
    s.further_idx = view(51200, 1).bitcast(U32)
    s.g2_row = view(12288, 2, D)
    s.y_hi = [view(14336 + D * i, D) for i in range(2)]
    s.y_lo = [view(16384 + D * i, D) for i in range(2)]
    s.big_a = view(37876, NT * DN_W)
    s.big_b = view(37876 + NT * DN_W, NT * DN_W)


def stage_modulation(nc, s, d):
    sem = s.sem
    loaded, exp_done = sem("small_loaded"), sem("cond_exp_done")
    ada_in = [sem(f"ada_in{i}") for i in range(4)]
    silu_done, rows_done, copied = sem("silu_done"), sem("mod_rows_done"), sem("mod_rows_copied")
    stored, turned, chain = sem("mod_rows_stored"), sem("mod_turned"), sem("mod_chain")
    w_ada = d["w_ada"][0].rearrange("(k p) n -> p k n", p=P)
    NB = 6 * D // 512
    with nc.Block() as block:
        @block.sync
        def _(sp):
            sp.dma_start(s.cst, d["consts"]).then_inc(loaded, 16)
            with nc.allow_non_contiguous_dma(reason="small vectors onto partitions"):
                sp.dma_start(s.cond[:, :, 0], d["c_ctx"].rearrange("(k p) -> p k", p=P)).then_inc(loaded, 16)
                sp.dma_start(s.cond[:, :, 1], d["c"][0].rearrange("(k p) -> p k", p=P)).then_inc(loaded, 16)
                sp.dma_start(s.gain1, d["norm1_g"][0].rearrange("(k p) -> p k", p=P)).then_inc(loaded, 16)
                for h in range(2):
                    rows = slice(h * HEAD, (h + 1) * HEAD)
                    sp.dma_start(s.qgain[rows, :], d["q_norm_g"].rearrange("a b -> b a")).then_inc(loaded, 16)
                    sp.dma_start(s.kgain[rows, :], d["k_norm_g"].rearrange("a b -> b a")).then_inc(loaded, 16)
                sp.dma_start(s.pscale, d["pool_scale"][0].rearrange("(k p) -> p k", p=P)).then_inc(loaded, 16)
            for i in range(2):
                sp.dma_start(s.b_ada[i:i + 1, :], d["b_ada"]).then_inc(loaded, 16)
            for n in range(NB):
                if n >= 4:
                    sp.wait_ge(rows_done, n - 3)
                sp.dma_start(s.ada_ring[n % 4], w_ada[:, :, n * 512:(n + 1) * 512]).then_inc(ada_in[n % 4], 16)
            sp.dma_start(d["rpb_rows"].rearrange("r (n w) -> r n w", w=RPB_W),
                         d["rpb"][0].rearrange("h r w -> (h r) w").unsqueeze(1).to_broadcast([NA_H * 15, RPB_REP, RPB_W])).then_inc(stored, 16)
            sp.wait_ge(copied, NB)
            sp.dma_start(d["mod_rows"], s.mod[0:2, :]).then_inc(stored, 16)
            sp.wait_ge(stored, 32)

        @block.scalar
        def _(act):
            act.wait_ge(loaded, 16 * 11)
            nc.scalar.activation(s.silu, s.cond, ACT.Silu).then_inc(silu_done, 1)

        @block.vector
        def _(dve):
            nc.vector.memset(s.epsc, EPS)
            for n in range(NB):
                dve.wait_ge(rows_done, n + 1)
                if n == 0:
                    dve.wait_ge(loaded, 16 * 11)
                cols = slice(n * 512, (n + 1) * 512)
                nc.vector.tensor_tensor(s.mod[0:2, cols], s.bank[n % 2][0:2, :], s.b_ada[0:2, cols],
                                        ALU.add).then_inc(copied, 1)
            nc.vector.tensor_scalar(s.qgain, s.qgain, HEAD ** -0.5, None, ALU.mult)
            dve.wait_ge(turned, 1)
            tr = s.bank[2][:, 0:32].rearrange("p (v k c) -> p v k c", v=2, k=KD)
            nc.vector.tensor_copy(s.mod_b1, tr[:, 0])
            for c in range(2):
                nc.vector.scalar_tensor_tensor(s.mod_a1[:, :, c], tr[:, 1, :, c], 1.0, s.gain1, ALU.add, ALU.mult)

        @block.tensor
        def _(pe):
            pe.wait_ge(silu_done, 1)
            for n in range(NB):
                pe.wait_ge(ada_in[n % 4], 16 * (n // 4 + 1))
                if n >= 2:
                    pe.wait_ge(copied, n - 1)
                for k in range(KD):
                    mm = nc.tensor.matmul(s.bank[n % 2][0:2, :], s.silu[:, k, :], s.ada_ring[n % 4][:, k, :],
                                          start=(k == 0), stop=(k == KD - 1))
                mm.then_inc(rows_done, 1)
            pe.wait_ge(copied, NB)
            for v in range(2):
                for k in range(KD):
                    at = (v * KD + k) * 2
                    tr = nc.tensor.transpose(s.bank[2][:, at:at + 2], s.mod[0:2, v * D + k * P:v * D + (k + 1) * P],
                                             s.ident[0:2, 0:2])
            tr.then_inc(turned, 1)


def stage_norm1(nc, s, d):
    sem = s.sem
    x_in = [sem(f"x_in{i}") for i in range(NT)]
    squared, std_done, rstd_done = sem("n1_squared"), sem("n1_std_done"), sem("n1_rstd_done")
    xn_ready, turned, act_out, dve_out = sem("xn_ready"), sem("xn_turned"), sem("n1_act_out"), sem("n1_dve_out")

    def place(t):
        return [s.bank[2 * (t % 2)], s.bank[2 * (t % 2) + 1]]

    with nc.Block() as block:
        @block.sync
        def _(sp):
            for t in range(NT):
                src = d["x_prompt"][0] if t == 0 else d["x_sample"][0, (t - 1) * P:t * P, :]
                sp.dma_start(s.x_all[:, t, :], src).then_inc(x_in[t], 16)

        @block.scalar
        def _(act):
            for t in range(NT):
                act.wait_ge(x_in[t], 16)
                nc.scalar.activation(s.junk, s.x_all[:, t, :], ACT.Square, accum_out=s.ss[:, t:t + 1]).then_inc(squared, 1)
                act.wait_ge(squared, t + 1)
            nc.scalar.activation(s.rstd, s.ss, ACT.Sqrt, bias=s.epsc, scale=1.0 / D).then_inc(std_done, 1)
            for t in range(NT):
                act.wait_ge(turned, t + 1)
                c = 0 if t == 0 else 1
                for k in range(KD // 2):
                    ps = place(t)[k // 4][:, (k % 4) * P:(k % 4 + 1) * P]
                    nc.scalar.activation(s.hT[:, k, t * P:(t + 1) * P], ps, ACT.Identity, bias=s.mod_b1[:, k, c:c + 1],
                                         scale=s.mod_a1[:, k, c:c + 1]).then_inc(act_out, 1)

        @block.vector
        def _(dve):
            dve.wait_ge(std_done, 1)
            nc.vector.reciprocal(s.rstd, s.rstd).then_inc(rstd_done, 1)
            dve.wait_ge(rstd_done, 1)

            def scale_rows(t):
                if t >= 3:
                    dve.wait_ge(turned, t - 2)
                nc.vector.tensor_scalar(s.xn_ring[t % 3], s.x_all[:, t, :], s.rstd[:, t:t + 1], None,
                                        ALU.mult).then_inc(xn_ready, 1)

            scale_rows(0)
            scale_rows(1)
            for t in range(NT):
                if t + 2 < NT:
                    scale_rows(t + 2)
                dve.wait_ge(turned, t + 1)
                c = 0 if t == 0 else 1
                for k in range(KD // 2, KD):
                    ps = place(t)[k // 4][:, (k % 4) * P:(k % 4 + 1) * P]
                    nc.vector.tensor_scalar(s.hT[:, k, t * P:(t + 1) * P], ps, s.mod_a1[:, k, c:c + 1],
                                            s.mod_b1[:, k, c:c + 1], ALU.mult, ALU.add).then_inc(dve_out, 1)

        @block.tensor
        def _(pe):
            for t in range(NT):
                pe.wait_ge(xn_ready, t + 1)
                if t >= 2:
                    pe.wait_ge(act_out, 4 * (t - 1))
                    pe.wait_ge(dve_out, 4 * (t - 1))
                for k in range(KD):
                    tr = nc.tensor.transpose(place(t)[k // 4][:, (k % 4) * P:(k % 4 + 1) * P],
                                             s.xn_ring[t % 3][:, k * P:(k + 1) * P], s.ident)
                tr.then_inc(turned, 1)


def stage_project(nc, s, d):
    sem = s.sem
    w_in_v = d["w_in"][0].rearrange("(k p) n -> p k n", p=P)
    groups = [(COL_POOL, POOL_W, "fm"), (COL_DN, 384, "fm"), (COL_DN + 384, 384, "fm"), (COL_Q, 512, "q"),
              (COL_K, 512, "k"), (COL_V, 512, "v"), (COL_Z, DN_W + 4 * DN_H, "zba")]
    w_loaded = [sem(f"w_in_loaded{i}") for i in range(2)]
    product, act_out, dve_out, padded, v_stored = sem("proj_product"), sem("proj_act_out"), sem("proj_dve_out"), sem("proj_padded"), s.out_sem["v_stored"]
    rows_zeroed = sem("rows_zeroed")
    tm_dst = {"q": s.q_tm, "k": s.k_tm, "v": s.v_tm, "zba": s.zba}

    units = []
    for g, (col, width, kind) in enumerate(groups):
        mine = []
        if kind == "fm":
            for c in range(width // P):
                if g == 0:
                    row, ctx_at, lat_at = s.pool_fm[:, c], POOL_CTX, POOL_LAT
                else:
                    row, ctx_at, lat_at = s.qkv_fm[:, (g - 1) * 3 + c], CONV_CTX, CONV_LAT
                mine.append((g, (c * P, P), (0, P), row[:, ctx_at:ctx_at + CTX]))
                for half in range(2):
                    mine.append((g, (c * P, P), (P + 512 * half, 512), row[:, lat_at + 512 * half:lat_at + 512 * (half + 1)]))
        else:
            for t in range(NT):
                mine.append((g, None, (t * P, P), tm_dst[kind][:, t, :]))
        units += mine
    last_of = {u[0]: i for i, u in enumerate(units)}
    widths = [w for _, w, _ in groups]

    def out_of(i):
        g, wc, (t0, n), _ = units[i]
        return s.bank[i % 4][:, 0:(n if wc else widths[g])]

    def w_view(g):
        return s.w_ring[g % 2][:, 0:KD * widths[g]].rearrange("p (k n) -> p k n", k=KD)

    with nc.Block() as block:
        @block.sync
        def _(sp):
            for g, (col, width, _) in enumerate(groups):
                if g >= 2:
                    sp.wait_ge(product, last_of[g - 2] + 1)
                sp.dma_start(w_view(g), w_in_v[:, :, col:col + width]).then_inc(w_loaded[g % 2], 16)
            last_v = last_of[5]
            sp.wait_ge(act_out, last_v // 2 + 1)
            sp.wait_ge(dve_out, last_v // 2 + 1)
            sp.dma_start(d["out_v"][0, 0].rearrange("h p d -> p h d"),
                         s.v_tm[:, 0, :].rearrange("p (h d) -> p h d", h=NA_H)).then_inc(v_stored, 16)
            sp.wait_ge(v_stored, 16)

        @block.gpsimd
        def _(pool):
            for at, n in ((0, POOL_PAD), (POOL_CTX + CTX, POOL_PAD), (POOL_LAT + LAT, POOL_PAD)):
                nc.gpsimd.memset(s.pool_fm[:, :, at:at + n], 0.0)
            for at, n in ((0, 1), (CONV_CTX + CTX, 3), (CONV_LAT + LAT, 2)):
                nc.gpsimd.memset(s.qkv_fm[:, :, at:at + n], 0.0)
            nc.gpsimd.memset(s.zero_rows, 0.0).then_inc(padded, 1)
            pool.wait_ge(padded, 1)
            for i in range(OVER):
                pool.dma_start(d["slot_rows"][(N_EXP * CAP) + i * P:(N_EXP * CAP) + (i + 1) * P, :], s.zero_rows).then_inc(rows_zeroed, 16)
            pool.wait_ge(rows_zeroed, 16 * OVER)

        @block.scalar
        def _(act):
            for i in range(0, len(units), 2):
                act.wait_ge(product, i + 1)
                nc.scalar.copy(units[i][3], out_of(i)).then_inc(act_out, 1)

        @block.vector
        def _(dve):
            for i in range(1, len(units), 2):
                dve.wait_ge(product, i + 1)
                nc.vector.tensor_copy(units[i][3], out_of(i)).then_inc(dve_out, 1)

        @block.tensor
        def _(pe):
            for i, (g, wc, (t0, n), _) in enumerate(units):
                if i == 0 or units[i - 1][0] != g:
                    pe.wait_ge(w_loaded[g % 2], 16 * (g // 2 + 1))
                if i >= 4:
                    pe.wait_ge(act_out if i % 2 == 0 else dve_out, (i - 4) // 2 + 1)
                w = w_view(g)
                for k in range(KD):
                    if wc:
                        mm = nc.tensor.matmul(out_of(i), w[:, k, wc[0]:wc[0] + wc[1]], s.hT[:, k, t0:t0 + n],
                                              start=(k == 0), stop=(k == KD - 1))
                    else:
                        mm = nc.tensor.matmul(out_of(i), s.hT[:, k, t0:t0 + n], w[:, k, :],
                                              start=(k == 0), stop=(k == KD - 1))
                mm.then_inc(product, 1)


def stage_heads(nc, s, d):
    sem = s.sem
    cache_in, gain_in = sem("cache_in"), sem("kgain_row_in")
    squared, summed, std_done, r_done = sem("qk_squared"), sem("qk_summed"), sem("qk_std_done"), sem("qk_r_done")
    scaled, turned, out = sem("qk_scaled"), sem("qk_turned"), sem("qk_out")
    kc_turned, kc_out, kn_done, kn_stored = sem("kc_turned"), sem("kc_out"), sem("kn_done"), s.out_sem["kn_stored"]
    tiles = [(t, w) for t in range(NT) for w in range(2)]
    tm = [s.q_tm, s.k_tm]

    with nc.Block() as block:
        @block.sync
        def _(sp):
            for i in range(2):
                rows = slice(i * P, (i + 1) * P)
                sp.dma_start(s.kc_tm[:, i, :].rearrange("p (h d) -> p h d", h=NA_H),
                             d["cache_na_k"][0, 0, :, rows, :].rearrange("h p d -> p h d")).then_inc(cache_in, 16)
                sp.dma_start(s.vc_tm[:, i, :].rearrange("p (h d) -> p h d", h=NA_H),
                             d["cache_na_v"][0, 0, :, rows, :].rearrange("h p d -> p h d")).then_inc(cache_in, 16)
            sp.dma_start(s.kgain_row, d["k_norm_g"].to_broadcast([P, HEAD])).then_inc(gain_in, 16)
            sp.wait_ge(kn_done, 1)
            sp.dma_start(d["out_k"][0, 0].rearrange("h p d -> p h d"),
                         s.kn_ctx.rearrange("p (h d) -> p h d", h=NA_H)).then_inc(kn_stored, 16)
            sp.wait_ge(kn_stored, 16)

        @block.scalar
        def _(act):
            for j, (t, w) in enumerate(tiles):
                if j >= 2:
                    act.wait_ge(summed, j - 1)
                nc.scalar.activation(s.sq_ring[j % 2], tm[w][:, t, :], ACT.Square).then_inc(squared, 1)
            act.wait_ge(summed, len(tiles))
            nc.scalar.activation(s.qk_r, s.qk_ss, ACT.Sqrt, bias=s.epsc, scale=1.0 / HEAD).then_inc(std_done, 1)
            for i in range(2):
                act.wait_ge(kc_turned, i + 1)
                nc.scalar.copy(s.kcT[:, :, i * P:(i + 1) * P], s.bank[4 + i].rearrange("p (a b) -> p a b", a=4)).then_inc(kc_out, 1)
            for j, (t, w) in enumerate(tiles):
                act.wait_ge(turned, j + 1)
                dst = (s.qT, s.kT)[w][:, :, t * P:(t + 1) * P]
                nc.scalar.activation(dst, s.bank[j % 4].rearrange("p (a b) -> p a b", a=4), ACT.Copy,
                                     scale=(s.qgain, s.kgain)[w]).then_inc(out, 1)

        @block.vector
        def _(dve):
            for j, (t, w) in enumerate(tiles):
                dve.wait_ge(squared, j + 1)
                nc.vector.tensor_reduce(s.qk_ss[:, j * NA_H:(j + 1) * NA_H],
                                        s.sq_ring[j % 2].rearrange("p (h d) -> p h d", h=NA_H), AX.X, ALU.add).then_inc(summed, 1)
            dve.wait_ge(std_done, 1)
            nc.vector.reciprocal(s.qk_r, s.qk_r).then_inc(r_done, 1)
            dve.wait_ge(r_done, 1)
            for j, (t, w) in enumerate(tiles):
                x = tm[w][:, t, :].rearrange("p (h d) -> p h d", h=NA_H)
                r = s.qk_r[:, j * NA_H:(j + 1) * NA_H].unsqueeze(2).to_broadcast([P, NA_H, HEAD])
                nc.vector.tensor_tensor(x, x, r, ALU.mult).then_inc(scaled, 1)
                if j == 1:
                    dve.wait_ge(scaled, 2)
                    dve.wait_ge(gain_in, 16)
                    nc.vector.tensor_tensor(s.kn_ctx.rearrange("p (h d) -> p h d", h=NA_H), x,
                                            s.kgain_row.unsqueeze(1).to_broadcast([P, NA_H, HEAD]), ALU.mult).then_inc(kn_done, 1)

        @block.tensor
        def _(pe):
            pe.wait_ge(cache_in, 64)
            for i in range(2):
                for hp in range(4):
                    tr = nc.tensor.transpose(s.bank[4 + i][:, hp * P:(hp + 1) * P], s.kc_tm[:, i, hp * P:(hp + 1) * P], s.ident)
                tr.then_inc(kc_turned, 1)
            for j, (t, w) in enumerate(tiles):
                pe.wait_ge(scaled, j + 1)
                if j >= 4:
                    pe.wait_ge(out, j - 3)
                for hp in range(4):
                    tr = nc.tensor.transpose(s.bank[j % 4][:, hp * P:(hp + 1) * P], tm[w][:, t, hp * P:(hp + 1) * P], s.ident)
                tr.then_inc(turned, 1)


def query_tiles():
    out = []
    rows, kh = LAT // GRID, 8
    for i in range(rows // 2):
        first = [min(max(r - kh // 2, 0), rows - kh) for r in (2 * i, 2 * i + 1)]
        n = first[1] + kh - first[0]
        out.append((1 + i, first[0], n, first[0] - 2 * i + 6))
    out.append((0, None, None, None))
    return out


def stage_attention(nc, s, d):
    sem = s.sem
    bias_in, bias_ready = [sem(f"bias_in{i}") for i in range(2)], sem("bias_ready")
    scored, biased, neg_max, weighted = sem("at_scored"), sem("at_biased"), sem("at_neg_max"), sem("at_weighted")
    turned, act_out, dve_out = sem("at_turned"), sem("at_act_out"), sem("at_dve_out")
    part_max = sem("at_part_max")
    summed, inverse, mixed, chain = sem("at_summed"), sem("at_inverse"), sem("at_mixed"), sem("at_chain")
    tiles = query_tiles()
    units = [(h, q) for h in range(NA_H) for q in range(len(tiles))]
    U, Q = len(units), len(tiles)

    def local(q):
        return 0 if tiles[q][2] is None else tiles[q][2] * GRID

    def width(q):
        return P if tiles[q][2] is None else local(q) + PAST

    def blocks(q):
        t, r0, n, _ = tiles[q]
        if n is None:
            return [(0, P, 0, False)]
        full = [(b * P, min(P, local(q) - b * P), 1 + r0 // 2 + b, False) for b in range((n + 1) // 2)]
        return full + [(local(q) + b * P, P, b, True) for b in range(PAST // P)]

    def scores(u):
        return s.pair[u % 2]

    with nc.Block() as block:
        @block.sync
        def _(sp):
            for h in range(NA_H):
                if h >= 2:
                    sp.wait_ge(biased, Q * (h - 1))
                    sp.wait_ge(bias_ready, h - 1)
                for a in range(2):
                    src = bass.AP(tensor=d["rpb_rows"].tensor, offset=(h * 15 + 1 - a) * RPB_ROW + 15,
                                  ap=[[RPB_W - 1, GRID], [RPB_ROW, 14], [1, GRID]])
                    sp.dma_start(s.bias[h % 2][a * GRID:(a + 1) * GRID], src).then_inc(bias_in[h % 2], 16)

        @block.gpsimd
        def _(pool):
            for h in range(NA_H):
                b, m = s.bias[h % 2], s.bias_mid[h % 2]
                pool.wait_ge(bias_in[h % 2], 32 * (h // 2 + 1))
                nc.gpsimd.tensor_tensor(b, b, s.colmask.unsqueeze(1).to_broadcast([P, 14, GRID]), ALU.add).then_inc(chain, 1)
                pool.wait_ge(chain, 3 * h + 1)
                nc.gpsimd.tensor_copy(m, b[:, 2:11, :]).then_inc(chain, 1)
                pool.wait_ge(chain, 3 * h + 2)
                nc.gpsimd.memset(m[0:GRID, 8, :], NEG)
                nc.gpsimd.memset(m[GRID:P, 0, :], NEG).then_inc(chain, 1)
                pool.wait_ge(chain, 3 * h + 3)
                nc.gpsimd.nop().then_inc(bias_ready, 1)

        @block.scalar
        def _(act):
            def turned_out(u):
                h, q = units[u]
                n = min(len(blocks(q)), 4) * P
                act.wait_ge(turned, u + 1)
                if u >= 2:
                    act.wait_ge(mixed, u - 1)
                nc.scalar.copy(s.wT[u % 2][:, 0:n], s.bank[4][:, 0:n]).then_inc(act_out, 1)

            for u, (h, q) in enumerate(units):
                act.wait_ge(neg_max, u + 1)
                w = s.weights[u % 2][:, 0:width(q)]
                nc.scalar.activation(w, w, ACT.Exp, bias=s.at_nm[:, u % 4:u % 4 + 1],
                                     accum_out=s.at_sum[:, u % 4:u % 4 + 1]).then_inc(weighted, 1)
                if u >= 1:
                    turned_out(u - 1)
            turned_out(U - 1)

        @block.vector
        def _(dve):
            def turned_out(u):
                h, q = units[u]
                n = (len(blocks(q)) - 4) * P
                dve.wait_ge(turned, u + 1)
                if u >= 2:
                    dve.wait_ge(mixed, u - 1)
                if n > 0:
                    nc.vector.tensor_copy(s.wT[u % 2][:, 512:512 + n], s.bank[5][:, 0:n]).then_inc(dve_out, 1)
                else:
                    dve.sem_inc(dve_out, 1)

            def mixed_out(u):
                h, q = units[u]
                dve.wait_ge(mixed, u + 1)
                dve.wait_ge(inverse, u + 1)
                nc.vector.tensor_scalar(s.o_na[:, tiles[q][0], h * HEAD:(h + 1) * HEAD], s.bank[6 + u % 2][:, 0:HEAD],
                                        s.at_inv[:, u % 4:u % 4 + 1], None, ALU.mult).then_inc(summed, 1)

            for u, (h, q) in enumerate(units):
                t, r0, n, m0 = tiles[q]
                dve.wait_ge(scored, u + 1)
                if u >= 2:
                    dve.wait_ge(turned, u - 1)
                if q == 0:
                    dve.wait_ge(bias_ready, h + 1)
                w, L = s.weights[u % 2], local(q)
                mx, nm = s.at_max[:, u % 4:u % 4 + 1], s.at_nm[:, u % 4:u % 4 + 1]
                if n is None:
                    nc.vector.tensor_scalar(w[:, 0:P], scores(u)[:, 0:P], 1.0, None, ALU.mult, ALU.max, accum_out=mx).then_inc(biased, 1)
                else:
                    bias = s.bias_mid[h % 2] if n == 9 else s.bias[h % 2][:, m0:m0 + n, :]
                    m1 = s.at_m1[:, u % 4:u % 4 + 1]
                    nc.vector.tensor_tensor_reduce(out=w[:, 0:L], in0=scores(u)[:, 0:L],
                                                   in1=bias.rearrange("p a b -> p (a b)"), scale=1.0, scalar=NEG,
                                                   op0=ALU.add, op1=ALU.max, accum_out=m1).then_inc(part_max, 1)
                    dve.wait_ge(part_max, h * (Q - 1) + q + 1)
                    nc.vector.tensor_scalar(w[:, L:L + PAST], scores(u)[:, L:L + PAST], 1.0, m1, ALU.mult, ALU.max,
                                            accum_out=mx).then_inc(biased, 1)
                dve.wait_ge(biased, u + 1)
                nc.vector.tensor_scalar(nm, mx, -1.0, None, ALU.mult).then_inc(neg_max, 1)
                if u >= 1:
                    turned_out(u - 1)
                    dve.wait_ge(weighted, u)
                    nc.vector.reciprocal(s.at_inv[:, (u - 1) % 4:(u - 1) % 4 + 1], s.at_sum[:, (u - 1) % 4:(u - 1) % 4 + 1]).then_inc(inverse, 1)
                if u >= 2:
                    mixed_out(u - 2)
            turned_out(U - 1)
            dve.wait_ge(weighted, U)
            nc.vector.reciprocal(s.at_inv[:, (U - 1) % 4:(U - 1) % 4 + 1], s.at_sum[:, (U - 1) % 4:(U - 1) % 4 + 1]).then_inc(inverse, 1)
            mixed_out(U - 2)
            mixed_out(U - 1)

        @block.tensor
        def _(pe):
            def score(u):
                h, q = units[u]
                t, r0, n, _ = tiles[q]
                half, hp = slice((h % 2) * HEAD, (h % 2 + 1) * HEAD), h // 2
                if u >= 2:
                    pe.wait_ge(biased, u - 1)
                qT = s.qT[half, hp, t * P:(t + 1) * P]
                out = scores(u)
                if n is None:
                    mm = nc.tensor.matmul(out[:, 0:P], qT, s.kT[half, hp, 0:CTX], start=True, stop=True)
                else:
                    L, k0 = local(q), CTX + r0 * GRID
                    nc.tensor.matmul(out[:, 0:512], qT, s.kT[half, hp, k0:k0 + 512], start=True, stop=True)
                    if L > 512:
                        nc.tensor.matmul(out[:, 512:L], qT, s.kT[half, hp, k0 + 512:k0 + L], start=True, stop=True)
                    mm = nc.tensor.matmul(out[:, L:L + PAST], qT, s.kcT[half, hp, :], start=True, stop=True)
                mm.then_inc(scored, 1)

            def turn(u):
                h, q = units[u]
                pe.wait_ge(weighted, u + 1)
                if u >= 1:
                    pe.wait_ge(act_out, u)
                    pe.wait_ge(dve_out, u)
                for b, (col, n, _, _) in enumerate(blocks(q)):
                    bank = s.bank[4 + b // 4]
                    tr = nc.tensor.transpose(bank[0:n, (b % 4) * P:(b % 4 + 1) * P], s.weights[u % 2][:, col:col + n], s.ident)
                tr.then_inc(turned, 1)

            def mix(u):
                h, q = units[u]
                pe.wait_ge(act_out, u + 1)
                pe.wait_ge(dve_out, u + 1)
                if u >= 2:
                    pe.wait_ge(summed, u - 1)
                every = blocks(q)
                for b, (_, n, tile, cached) in enumerate(every):
                    v = (s.vc_tm if cached else s.v_tm)[0:n, tile, h * HEAD:(h + 1) * HEAD]
                    mm = nc.tensor.matmul(s.bank[6 + u % 2][:, 0:HEAD], s.wT[u % 2][0:n, b * P:(b + 1) * P], v,
                                          start=(b == 0), stop=(b == len(every) - 1))
                mm.then_inc(mixed, 1)

            score(0)
            for u in range(U):
                if u + 1 < U:
                    score(u + 1)
                turn(u)
                if u >= 1:
                    mix(u - 1)
            mix(U - 1)


def stage_dn_prepare(nc, s, d):
    sem = s.sem
    small_in, chain, conv_done, silu_done = sem("dn_small_in"), sem("dn_chain"), sem("conv_done"), sem("conv_silu_done")
    turned, act_out, dve_out = sem("dn_turned"), sem("dn_act_out"), sem("dn_dve_out")
    squared, summed, std_done, r_done = sem("dn_squared"), sem("dn_ssq"), sem("dn_std"), sem("dn_r")
    sig_done, pre_done, abs_done, exp_done, ln_done, g_done = [sem("dn_" + n) for n in ("sig", "pre", "abs", "exp", "ln", "g")]
    cum_done, ex_in, ex_done = sem("dn_cum"), sem("dn_ex_in"), sem("dn_ex")
    NJ = CONV_ROW - 3
    G2 = 2 * DN_H
    b_raw = s.zba[:, :, DN_W:DN_W + G2]
    a_raw = s.zba[:, :, DN_W + G2:DN_W + 2 * G2]

    def tile_col(t):
        return 0 if t == 0 else CONV_LAT - 1 + (t - 1) * P

    with nc.Block() as block:
        @block.sync
        def _(sp):
            with nc.allow_non_contiguous_dma(reason="conv taps onto partitions"):
                for k in range(4):
                    sp.dma_start(s.taps[:, :, k], d["dn_conv_w"][0, k].rearrange("(c p) -> p c", p=P)).then_inc(small_in, 16)
            sp.dma_start(s.a_log, d["dn_a_log"].rearrange("a b c -> a (b c)").to_broadcast([P, G2])).then_inc(small_in, 16)
            sp.dma_start(s.dt_bias, d["dn_dt_bias"].rearrange("a b c -> a (b c)").to_broadcast([P, G2])).then_inc(small_in, 16)

        @block.vector
        def _(dve):
            done = [0]

            def link(ins):
                done[0] += 1
                ins.then_inc(chain, 1)
                dve.wait_ge(chain, done[0])

            dve.wait_ge(small_in, 96)
            for c in range(6):
                u, out = s.qkv_fm[:, c], s.conv[:, c]
                link(nc.vector.tensor_scalar(out, u[:, 0:NJ], s.taps[:, c, 0:1], None, ALU.mult))
                for k in range(1, 4):
                    ins = nc.vector.scalar_tensor_tensor(out, u[:, k:k + NJ], s.taps[:, c, k:k + 1], out, ALU.mult, ALU.add)
                    if k < 3:
                        link(ins)
                    else:
                        ins.then_inc(conv_done, 1)
            link(nc.vector.tensor_tensor(s.a_in, a_raw, s.dt_bias.unsqueeze(1).to_broadcast([P, NT, G2]), ALU.add))
            link(nc.vector.tensor_scalar(s.a_abs, s.a_in, -1.0, None, ALU.mult))
            nc.vector.tensor_tensor(s.a_abs, s.a_abs, s.a_in, ALU.min).then_inc(abs_done, 1)
            dve.wait_ge(ln_done, 2)
            link(nc.vector.tensor_scalar(s.a_in, s.a_in, 0.0, None, ALU.max))
            link(nc.vector.tensor_tensor(s.a_in, s.a_in, s.a_abs, ALU.add))
            link(nc.vector.tensor_scalar(s.a_log, s.a_log, -1.0, None, ALU.mult))
            nc.vector.tensor_tensor(s.g, s.a_in, s.a_log.unsqueeze(1).to_broadcast([P, NT, G2]), ALU.mult).then_inc(g_done, 1)
            for t in range(NT):
                dve.wait_ge(turned, t + 1)
                nc.vector.tensor_copy(s.qkv_tm[:, t, 512:768], s.bank[2 * (t % 2) + 1][:, 0:256]).then_inc(dve_out, 1)
                dve.wait_ge(squared, t + 1)
                nc.vector.tensor_reduce(s.dn_ss[:, t, :], s.dn_sq[t % 2].rearrange("p (h d) -> p h d", h=8), AX.X,
                                        ALU.add).then_inc(summed, 1)
            dve.wait_ge(std_done, 1)
            nc.vector.reciprocal(s.dn_ss, s.dn_ss).then_inc(r_done, 1)
            dve.wait_ge(r_done, 1)
            nc.vector.tensor_scalar(s.dn_ss[:, :, 0:4], s.dn_ss[:, :, 0:4], HEAD ** -0.5, None, ALU.mult).then_inc(r_done, 1)
            dve.wait_ge(r_done, 2)
            for t in range(NT):
                qk = s.qkv_tm[:, t, 0:512].rearrange("p (h d) -> p h d", h=8)
                nc.vector.tensor_tensor(qk, qk, s.dn_ss[:, t, :].unsqueeze(2).to_broadcast([P, 8, HEAD]), ALU.mult)
            dve.wait_ge(cum_done, 1)
            ps = s.bank[4]
            for dd in range(2):
                nc.vector.tensor_copy(s.cum[:, :, dd * 4:dd * 4 + 4], ps[:, dd * 36:dd * 36 + 36].rearrange("p (t h) -> p t h", h=4)).then_inc(ex_in, 1)
            dve.wait_ge(ex_in, 2)
            nc.vector.tensor_tensor(s.g_rest, ps[:, 72:144].rearrange("p (t h) -> p t h", h=G2), s.cum, ALU.subtract).then_inc(ex_in, 1)
            dve.wait_ge(ex_done, 2)
            nc.vector.tensor_tensor(s.beta_eg, s.beta, s.beta_eg, ALU.mult)

        @block.scalar
        def _(act):
            for c in range(6):
                act.wait_ge(conv_done, c + 1)
                nc.scalar.activation(s.conv[:, c], s.conv[:, c], ACT.Silu).then_inc(silu_done, 1)
            nc.scalar.activation(s.beta, b_raw, ACT.Sigmoid).then_inc(sig_done, 1)
            act.wait_ge(abs_done, 1)
            nc.scalar.activation(s.a_abs, s.a_abs, ACT.Exp).then_inc(exp_done, 1)
            nc.scalar.activation(s.a_log, s.a_log, ACT.Exp).then_inc(ln_done, 1)
            act.wait_ge(exp_done, 1)
            nc.scalar.activation(s.a_abs, s.a_abs, ACT.Ln, bias=1.0).then_inc(ln_done, 1)
            for t in range(NT):
                act.wait_ge(turned, t + 1)
                nc.scalar.copy(s.qkv_tm[:, t, 0:512], s.bank[2 * (t % 2)]).then_inc(act_out, 1)
                act.wait_ge(act_out, t + 1)
                if t >= 2:
                    act.wait_ge(summed, t - 1)
                nc.scalar.activation(s.dn_sq[t % 2], s.qkv_tm[:, t, 0:512], ACT.Square).then_inc(squared, 1)
            act.wait_ge(summed, NT)
            nc.scalar.activation(s.dn_ss, s.dn_ss, ACT.Sqrt, bias=s.epsc).then_inc(std_done, 1)
            act.wait_ge(ex_in, 3)
            nc.scalar.activation(s.beta_eg, s.cum, ACT.Exp).then_inc(ex_done, 1)
            nc.scalar.activation(s.g_rest, s.g_rest, ACT.Exp).then_inc(ex_done, 1)

        @block.tensor
        def _(pe):
            for t in range(NT):
                if t == 0:
                    pe.wait_ge(silu_done, 6)
                if t >= 2:
                    pe.wait_ge(act_out, t - 1)
                    pe.wait_ge(dve_out, t - 1)
                for c in range(6):
                    bank = s.bank[2 * (t % 2) + c // 4]
                    tr = nc.tensor.transpose(bank[:, (c % 4) * P:(c % 4 + 1) * P], s.conv[:, c, tile_col(t):tile_col(t) + P], s.ident)
                tr.then_inc(turned, 1)
            pe.wait_ge(g_done, 1)
            nc.tensor.matmul(s.bank[4][:, 0:36], s.tri_f, s.g[:, :, 0:4], start=True, stop=True)
            nc.tensor.matmul(s.bank[4][:, 36:72], s.tri_b, s.g[:, :, 4:8], start=True, stop=True)
            nc.tensor.matmul(s.bank[4][:, 72:144], s.block, s.g, start=True, stop=True).then_inc(cum_done, 1)


def stage_dn_scan(nc, s, d):
    sem = s.sem
    both = lambda name: [sem(f"{name}_{x}") for x in "fb"]
    state_in, state_out, start = sem("state_in"), s.out_sem["state_out"], sem("dn_start")
    kb_ready, kv_ready, turned, cast, kbt = both("kb_ready"), both("kv_ready"), both("sc_turned"), both("qk_cast"), both("kbt")
    spread, diff, decay, gram, gram_out = both("spread"), both("diff"), both("decay"), both("gram"), both("gram_out")
    inv_ready, y_done, y_ready, dxz = both("inv_ready"), both("y_done"), both("y_ready"), both("dxz")
    wu_done, wu_ready, qd_ready = both("wu_done"), both("wu_ready"), both("qd_ready")
    ws_done, v_ready, step_done, s_ready, o_ready = both("ws_done"), both("v_ready"), both("step_done"), both("s_ready"), both("o_ready")
    chain = sem("scan_chain")
    tile_of = lambda n, r: 0 if n == 0 else (n if r == 0 else NT - n)
    dirs = (0, 1)
    level = (s.level_f, s.level_b)
    strict = (s.strict_f, s.strict_b)
    tri = (s.tri_f, s.tri_b)
    W = 4 * P

    def heads(v, n=P):
        return v.rearrange("p (h a) -> p h a", h=4)

    def over_heads(m):
        return m.unsqueeze(1).to_broadcast([P, 4, P])

    def chunk_order(r):
        return (0, 1) if r == 0 else (1, 0)

    def end_col(r, c):
        return c * HEAD + (HEAD - 1 if r == 0 else 0)

    with nc.Block() as block:
        @block.sync
        def _(sp):
            for r in dirs:
                sp.dma_start(s.S_lat[0:HEAD, r], d["state_dn"][0, 0, r].rearrange("h k v -> k h v")).then_inc(state_in, 16)
            for r in dirs:
                sp.wait_ge(s_ready[r], 2)
                sp.dma_start(d["out_state"][0, 0, r].rearrange("h k v -> k h v"), s.S_ctx[0:HEAD, r]).then_inc(state_out, 16)
            sp.wait_ge(state_out, 32)

        @block.gpsimd
        def _(pool):
            for n in range(NT):
                for r in dirs:
                    t = tile_of(n, r)
                    if n >= 1:
                        pool.wait_ge(turned[r], n)
                    k = heads(s.qkv_tm[:, t, 256:512])
                    v = heads(s.qkv_tm[:, t, 512:768])
                    col = lambda x: x[:, t, r * 4:r * 4 + 4].unsqueeze(2).to_broadcast([P, 4, HEAD])
                    nc.gpsimd.tensor_tensor(heads(s.kb[r]), k, col(s.beta), ALU.mult).then_inc(kb_ready[r], 1)
                    if n >= 1:
                        pool.wait_ge(step_done[r], 2 * n)
                    nc.gpsimd.tensor_tensor(heads(s.vb[r]), v, col(s.beta), ALU.mult)
                    nc.gpsimd.tensor_tensor(heads(s.kg[r]), k, col(s.beta_eg), ALU.mult)
                    nc.gpsimd.tensor_tensor(heads(s.kd[r]), k, col(s.g_rest), ALU.mult).then_inc(kv_ready[r], 1)

        @block.scalar
        def _(act):
            for n in range(NT):
                for r in dirs:
                    b = s.bank[4 * r:4 * r + 4]
                    act.wait_ge(turned[r], n + 1)
                    if n >= 1:
                        act.wait_ge(qd_ready[r], n)
                    nc.scalar.copy(s.sqT[r], b[0][0:HEAD, :]).then_inc(cast[r], 1)
                    nc.scalar.copy(s.skT[r], b[1][0:HEAD, :]).then_inc(cast[r], 1)
                for r in dirs:
                    b = s.bank[4 * r:4 * r + 4]
                    act.wait_ge(diff[r], n + 1)
                    nc.scalar.activation(s.dec[r], s.pos[r], ACT.Exp, scale=-1.0)
                    nc.scalar.activation(s.decT[r], s.neg[r], ACT.Exp).then_inc(decay[r], 1)
                    if n >= 1:
                        act.wait_ge(s_ready[r], 2 * n)
                    nc.scalar.activation(s.eb[r], b[3], ACT.Exp).then_inc(decay[r], 1)
                for r in dirs:
                    b = s.bank[4 * r:4 * r + 4]
                    act.wait_ge(wu_done[r], n + 1)
                    nc.scalar.copy(s.swT[r], b[0][0:HEAD, :])
                    nc.scalar.copy(s.su[r], b[1][:, 0:4 * HEAD]).then_inc(wu_ready[r], 1)

        @block.vector
        def _(dve):
            done = [0]

            def link(ins):
                done[0] += 1
                ins.then_inc(chain, 1)
                dve.wait_ge(chain, done[0])

            nc.vector.memset(s.o_dn, 0.0)
            nc.vector.memset(s.S_ctx, 0.0).then_inc(start, 1)
            dve.wait_ge(start, 1)
            for n in range(NT):
                for r in dirs:
                    t, b = tile_of(n, r), s.bank[4 * r:4 * r + 4]
                    dve.wait_ge(turned[r], n + 1)
                    nc.vector.tensor_copy(s.skbT[r], b[2][0:HEAD, :]).then_inc(kbt[r], 1)
                    dve.wait_ge(spread[r], n + 1)
                    gc = s.cum[:, t, r * 4:r * 4 + 4].unsqueeze(2).to_broadcast([P, 4, P])
                    link(nc.vector.tensor_tensor(heads(s.pos[r]), heads(b[3]), gc, ALU.subtract))
                    link(nc.vector.tensor_scalar(s.neg[r], s.pos[r], 0.0, None, ALU.min))
                    nc.vector.tensor_scalar(s.pos[r], s.pos[r], 0.0, None, ALU.max).then_inc(diff[r], 1)
                for r in dirs:
                    b = s.bank[4 * r:4 * r + 4]
                    dve.wait_ge(decay[r], 2 * n + 1)
                    dve.wait_ge(gram[r], n + 1)
                    link(nc.vector.tensor_tensor(heads(s.dec[r]), heads(s.dec[r]), over_heads(strict[r]), ALU.mult))
                    link(nc.vector.tensor_tensor(s.L[r], b[0], s.dec[r], ALU.mult))
                    link(nc.vector.tensor_tensor(heads(s.dec[r]), heads(s.decT[r]), over_heads(strict[1 - r]), ALU.mult))
                    link(nc.vector.tensor_tensor(s.LT[r], b[1], s.dec[r], ALU.mult))
                    link(nc.vector.tensor_tensor(heads(s.decT[r]), heads(s.decT[r]), over_heads(tri[r]), ALU.mult))
                    nc.vector.tensor_tensor(s.attT[r], b[2], s.decT[r], ALU.mult)
                    link(nc.vector.tensor_tensor(heads(s.X[r]), heads(s.L[r]), over_heads(level[r][:, 0, :]), ALU.mult))
                    link(nc.vector.tensor_tensor(heads(s.Z[r]), heads(s.LT[r]), over_heads(level[1 - r][:, 0, :]), ALU.mult))
                    nc.vector.scalar_tensor_tensor(heads(s.X[r]), heads(s.X[r]), -1.0, over_heads(s.ident), ALU.mult, ALU.add)
                    nc.vector.scalar_tensor_tensor(heads(s.Z[r]), heads(s.Z[r]), -1.0, over_heads(s.ident), ALU.mult, ALU.add).then_inc(inv_ready[r], 1)
                    dve.wait_ge(decay[r], 2 * n + 2)
                    if n >= 1:
                        dve.wait_ge(step_done[r], 2 * n)
                    nc.vector.tensor_tensor(s.sqd[r], s.sqT[r], s.eb[r][0:HEAD, :], ALU.mult).then_inc(qd_ready[r], 1)
                for m in range(1, 6):
                    for r in dirs:
                        b = s.bank[4 * r:4 * r + 4]
                        dve.wait_ge(y_done[r], 5 * n + m)
                        nc.vector.tensor_tensor(heads(s.Y[r]), heads(b[0]), over_heads(level[r][:, m, :]), ALU.mult).then_inc(y_ready[r], 1)
                    for r in dirs:
                        b = s.bank[4 * r:4 * r + 4]
                        dve.wait_ge(dxz[r], 5 * n + m)
                        if m < 5:
                            nc.vector.tensor_tensor(s.X[r], s.X[r], b[1], ALU.subtract)
                        nc.vector.tensor_tensor(s.Z[r], s.Z[r], b[2], ALU.subtract).then_inc(inv_ready[r], 1)
                for r in dirs:
                    if n == 1 and r == 0:
                        dve.wait_ge(state_in, 32)
                for j in range(2):
                    for r in dirs:
                        c = chunk_order(r)[j]
                        rows, b = slice(c * HEAD, (c + 1) * HEAD), s.bank[4 * r:4 * r + 4]
                        S = (s.S_ctx if n == 0 else s.S_lat)[0:HEAD, r]
                        if j == 0:
                            dve.wait_ge(wu_ready[r], n + 1)
                        dve.wait_ge(ws_done[r], 2 * n + j + 1)
                        nc.vector.tensor_tensor(s.vn[r][rows], s.su[r][rows], b[0][rows, 0:4 * HEAD], ALU.subtract).then_inc(v_ready[r], 1)
                    for r in dirs:
                        t = tile_of(n, r)
                        c = chunk_order(r)[j]
                        rows, b = slice(c * HEAD, (c + 1) * HEAD), s.bank[4 * r:4 * r + 4]
                        S = (s.S_ctx if n == 0 else s.S_lat)[0:HEAD, r]
                        gl = heads(s.eb[r])[0:HEAD, :, end_col(r, c)].unsqueeze(2).to_broadcast([HEAD, 4, HEAD])
                        dve.wait_ge(step_done[r], 2 * n + j + 1)
                        link(nc.vector.tensor_tensor(S, S, gl, ALU.mult))
                        nc.vector.tensor_tensor(S, S, b[3][0:HEAD, 0:4 * HEAD].rearrange("p (h v) -> p h v", h=4), ALU.add).then_inc(s_ready[r], 1)
                        o = s.o_dn[rows, t, :]
                        link(nc.vector.tensor_tensor(o, o, b[2][rows, 0:4 * HEAD], ALU.add))
                        nc.vector.tensor_tensor(o, o, b[1][rows, 0:4 * HEAD], ALU.add).then_inc(o_ready[r], 1)
                        dve.wait_ge(o_ready[r], 2 * n + j + 1)

        @block.tensor
        def _(pe):
            for n in range(NT):
                for r in dirs:
                    t, b = tile_of(n, r), s.bank[4 * r:4 * r + 4]
                    pe.wait_ge(kb_ready[r], n + 1)
                    if n == 0 and r == 0:
                        pe.wait_ge(start, 1)
                    if n >= 1:
                        pe.wait_ge(o_ready[r], 2 * n)
                        pe.wait_ge(s_ready[r], 2 * n)
                    for h in range(4):
                        cols = slice(h * P, (h + 1) * P)
                        nc.tensor.transpose(b[0][0:HEAD, cols], s.qkv_tm[:, t, h * HEAD:(h + 1) * HEAD], s.ident)
                        nc.tensor.transpose(b[1][0:HEAD, cols], s.qkv_tm[:, t, 256 + h * HEAD:256 + (h + 1) * HEAD], s.ident)
                        tr = nc.tensor.transpose(b[2][0:HEAD, cols], s.kb[r][:, h * HEAD:(h + 1) * HEAD], s.ident)
                    tr.then_inc(turned[r], 1)
                    for h in range(4):
                        g = s.g[:, t, r * 4 + h:r * 4 + h + 1].to_broadcast([P, P])
                        mm = nc.tensor.matmul(b[3][:, h * P:(h + 1) * P], g, tri[r], start=True, stop=True)
                    mm.then_inc(spread[r], 1)
                for r in dirs:
                    b = s.bank[4 * r:4 * r + 4]
                    pe.wait_ge(cast[r], 2 * n + 2)
                    pe.wait_ge(kbt[r], n + 1)
                    for h in range(4):
                        cols = slice(h * P, (h + 1) * P)
                        nc.tensor.matmul(b[0][:, cols], s.skbT[r][0:HEAD, cols], s.skT[r][0:HEAD, cols], start=True, stop=True)
                        nc.tensor.matmul(b[1][:, cols], s.skT[r][0:HEAD, cols], s.skbT[r][0:HEAD, cols], start=True, stop=True)
                        mm = nc.tensor.matmul(b[2][:, cols], s.skT[r][0:HEAD, cols], s.sqT[r][0:HEAD, cols], start=True, stop=True)
                    mm.then_inc(gram[r], 1)
                for m in range(1, 6):
                    for r in dirs:
                        b = s.bank[4 * r:4 * r + 4]
                        pe.wait_ge(inv_ready[r], 6 * n + m)
                        for h in range(4):
                            cols = slice(h * P, (h + 1) * P)
                            mm = nc.tensor.matmul(b[0][:, cols], s.LT[r][:, cols], s.X[r][:, cols], start=True, stop=True)
                        mm.then_inc(y_done[r], 1)
                    for r in dirs:
                        b = s.bank[4 * r:4 * r + 4]
                        pe.wait_ge(y_ready[r], 5 * n + m)
                        for h in range(4):
                            cols = slice(h * P, (h + 1) * P)
                            if m < 5:
                                nc.tensor.matmul(b[1][:, cols], s.Z[r][:, cols], s.Y[r][:, cols], start=True, stop=True)
                            mm = nc.tensor.matmul(b[2][:, cols], s.Y[r][:, cols], s.Z[r][:, cols], start=True, stop=True)
                        mm.then_inc(dxz[r], 1)
                for r in dirs:
                    b = s.bank[4 * r:4 * r + 4]
                    pe.wait_ge(kv_ready[r], n + 1)
                    pe.wait_ge(inv_ready[r], 6 * n + 6)
                    for h in range(4):
                        cols, hd = slice(h * P, (h + 1) * P), slice(h * HEAD, (h + 1) * HEAD)
                        nc.tensor.matmul(b[0][0:HEAD, cols], s.kg[r][:, hd], s.Z[r][:, cols], start=True, stop=True)
                        mm = nc.tensor.matmul(b[1][:, hd], s.Z[r][:, cols], s.vb[r][:, hd], start=True, stop=True)
                    mm.then_inc(wu_done[r], 1)
                for j in range(2):
                    for r in dirs:
                        c = chunk_order(r)[j]
                        rows, b = slice(c * HEAD, (c + 1) * HEAD), s.bank[4 * r:4 * r + 4]
                        S = (s.S_ctx if n == 0 else s.S_lat)[0:HEAD, r]
                        if j == 0:
                            pe.wait_ge(wu_ready[r], n + 1)
                        if n == 1 and j == 0:
                            pe.wait_ge(state_in, 32)
                        pe.wait_ge(s_ready[r], 2 * n + j) if 2 * n + j else None
                        for h in range(4):
                            hd = slice(h * HEAD, (h + 1) * HEAD)
                            mm = nc.tensor.matmul(b[0][rows, hd], heads(s.swT[r])[0:HEAD, h, rows], S[:, h, :], start=True, stop=True)
                        mm.then_inc(ws_done[r], 1)
                    for r in dirs:
                        c = chunk_order(r)[j]
                        rows, b = slice(c * HEAD, (c + 1) * HEAD), s.bank[4 * r:4 * r + 4]
                        S = (s.S_ctx if n == 0 else s.S_lat)[0:HEAD, r]
                        pe.wait_ge(v_ready[r], 2 * n + j + 1)
                        if j == 0:
                            pe.wait_ge(qd_ready[r], n + 1)
                        else:
                            pe.wait_ge(o_ready[r], 2 * n + 1)
                        for h in range(4):
                            hd = slice(h * HEAD, (h + 1) * HEAD)
                            nc.tensor.matmul(b[2][rows, hd], heads(s.sqd[r])[0:HEAD, h, rows], S[:, h, :], start=True, stop=True)
                            nc.tensor.matmul(b[1][rows, hd], heads(s.attT[r])[rows, h, rows], s.vn[r][rows, hd], start=True, stop=True)
                            mm = nc.tensor.matmul(b[3][0:HEAD, hd], s.kd[r][rows, hd], s.vn[r][rows, hd], start=True, stop=True)
                        mm.then_inc(step_done[r], 1)


def stage_dn_finish(nc, s, d):
    sem = s.sem
    gain_in, squared, summed, std_done, chain, z_done = [sem("fin_" + n) for n in ("gain", "sq", "sum", "std", "chain", "z")]
    o4 = s.o_dn.rearrange("p t (h d) -> p (t h) d", h=DN_H)
    sq4 = s.big_a.rearrange("p (t d) -> p t d", d=HEAD)
    with nc.Block() as block:
        @block.sync
        def _(sp):
            sp.dma_start(s.dn_gain, d["dn_norm_g"].to_broadcast([P, HEAD])).then_inc(gain_in, 16)

        @block.scalar
        def _(act):
            nc.scalar.activation(s.big_a, s.o_dn.rearrange("p t c -> p (t c)"), ACT.Square).then_inc(squared, 1)
            nc.scalar.activation(s.big_b.rearrange("p (t c) -> p t c", t=NT), s.zba[:, :, 0:DN_W], ACT.Silu).then_inc(z_done, 1)
            act.wait_ge(summed, 1)
            nc.scalar.activation(s.fin_r, s.fin_r, ACT.Sqrt, bias=s.epsc, scale=1.0 / HEAD).then_inc(std_done, 1)

        @block.vector
        def _(dve):
            dve.wait_ge(squared, 1)
            nc.vector.tensor_reduce(s.fin_r, sq4, AX.X, ALU.add).then_inc(summed, 1)
            dve.wait_ge(std_done, 1)
            nc.vector.reciprocal(s.fin_r, s.fin_r).then_inc(chain, 1)
            dve.wait_ge(chain, 1)
            nc.vector.tensor_tensor(o4, o4, s.fin_r.unsqueeze(2).to_broadcast([P, NT * DN_H, HEAD]), ALU.mult).then_inc(chain, 1)
            dve.wait_ge(chain, 2)
            dve.wait_ge(gain_in, 16)
            nc.vector.tensor_tensor(o4, o4, s.dn_gain.unsqueeze(1).to_broadcast([P, NT * DN_H, HEAD]), ALU.mult).then_inc(chain, 1)
            dve.wait_ge(chain, 3)
            dve.wait_ge(z_done, 1)
            o = s.o_dn.rearrange("p t c -> p (t c)")
            nc.vector.tensor_tensor(o, o, s.big_b, ALU.mult)


def stage_pool(nc, s, d):
    sem = s.sem
    counts_in, wp_in, chain, pooled, mapped, out = [sem("pool_" + n) for n in ("counts", "w", "chain", "done", "mapped", "out")]
    A, B, R = s.pool_a, s.pool_b, POOL_ROW
    lo, hi = slice(0, HEAD), slice(HEAD, P)
    spans = [(POOL_CTX, 0, CTX), (POOL_LAT, CTX, 512), (POOL_LAT + 512, CTX + 512, 512)]
    units = [(c, sp_) for c in range(2) for sp_ in spans]
    groups = [(lo, 0, A), (hi, 0, B), (lo, 1, A), (hi, 1, B)]

    with nc.Block() as block:
        @block.sync
        def _(sp):
            sp.dma_start(s.pool_rc, d["pool_counts"]).then_inc(counts_in, 16)
            for g in range(4):
                sp.dma_start(s.w_pool[HEAD * (g % 2):HEAD * (g % 2 + 1), g // 2, :], d["w_pool"][0, g]).then_inc(wp_in, 16)

        @block.vector
        def _(dve):
            done = [0]

            def link(ins):
                done[0] += 1
                ins.then_inc(chain, 1)
                dve.wait_ge(chain, done[0])

            u = s.pool_fm
            add = lambda out_, a, b: link(nc.vector.tensor_tensor(out_, a, b, ALU.add))
            add(A[:, :, 1:R], u[:, :, 0:R - 1], u[:, :, 1:R])
            add(B[:, 0, 2:R - 1], A[:, 0, 1:R - 2], A[:, 0, 3:R])
            add(B[:, 1, 2:R - 1], A[:, 1, 1:R - 2], A[:, 1, 3:R])
            add(A[:, 1, 4:R - 3], B[:, 1, 2:R - 5], B[:, 1, 6:R - 1])
            add(B[hi, 1, 8:R - 7], A[hi, 1, 4:R - 11], A[hi, 1, 12:R - 3])
            dve.wait_ge(counts_in, 16)
            body = slice(POOL_CTX, POOL_LAT + LAT)
            for rows, c, buf in groups:
                link(nc.vector.tensor_tensor(buf[rows, c, body], buf[rows, c, body], s.pool_rc[rows, c, body], ALU.mult))
                ins = nc.vector.tensor_tensor(s.pooled[rows, c, body], buf[rows, c, body], u[rows, c, body], ALU.subtract)
            ins.then_inc(pooled, 1)

        @block.tensor
        def _(pe):
            pe.wait_ge(pooled, 1)
            pe.wait_ge(wp_in, 64)
            for i, (c, (at, _, n)) in enumerate(units):
                for half in range(2):
                    rows = slice(half * HEAD, (half + 1) * HEAD)
                    mm = nc.tensor.matmul(s.bank[i][rows, 0:n], s.w_pool[rows, c, :], s.pooled[rows, c, at:at + n], start=True, stop=True)
                mm.then_inc(mapped, 1)

        @block.scalar
        def _(act):
            for i, (c, (_, t0, n)) in enumerate(units):
                act.wait_ge(mapped, i + 1)
                nc.scalar.activation(s.oT[:, c, t0:t0 + n], s.bank[i][:, 0:n], ACT.Copy, scale=s.pscale[:, c:c + 1])


def stage_turn_mix(nc, s, d):
    sem = s.sem
    turned, act_out, dve_out = sem("mix_turned"), sem("mix_act_out"), sem("mix_dve_out")
    with nc.Block() as block:
        @block.tensor
        def _(pe):
            for t in range(NT):
                if t >= 4:
                    pe.wait_ge(act_out, t - 3)
                    pe.wait_ge(dve_out, t - 3)
                for c in range(4):
                    nc.tensor.transpose(s.bank[2 * (t % 4)][:, c * P:(c + 1) * P], s.o_na[:, t, c * P:(c + 1) * P], s.ident)
                for c in range(2):
                    tr = nc.tensor.transpose(s.bank[2 * (t % 4) + 1][:, c * P:(c + 1) * P], s.o_dn[:, t, c * P:(c + 1) * P], s.ident)
                tr.then_inc(turned, 1)

        @block.scalar
        def _(act):
            for t in range(NT):
                act.wait_ge(turned, t + 1)
                nc.scalar.copy(s.oT[:, 2:6, t * P:(t + 1) * P], s.bank[2 * (t % 4)].rearrange("p (a b) -> p a b", a=4)).then_inc(act_out, 1)

        @block.vector
        def _(dve):
            for t in range(NT):
                dve.wait_ge(turned, t + 1)
                nc.vector.tensor_copy(s.oT[:, 6:8, t * P:(t + 1) * P],
                                      s.bank[2 * (t % 4) + 1][:, 0:256].rearrange("p (a b) -> p a b", a=2)).then_inc(dve_out, 1)


def stage_output(nc, s, d):
    sem = s.sem
    w_in, g_in, x_in = sem("w_out_in"), sem("g1_in"), [sem(f"xr_in{i}") for i in range(2)]
    product, gated, added = sem("out_product"), sem("out_gated"), sem("out_added")
    with nc.Block() as block:
        @block.sync
        def _(sp):
            wv = d["w_out"][0].rearrange("(k p) n -> p k n", p=P)
            for half in range(2):
                sp.dma_start(s.w_out[:, :, half * 512:(half + 1) * 512], wv[:, :, half * 512:(half + 1) * 512]).then_inc(w_in, 16)
            for c in range(2):
                sp.dma_start(s.g1_row[:, c, :], d["mod_rows"][c:c + 1, 2 * D:3 * D].to_broadcast([P, D])).then_inc(g_in, 16)
            for t in range(NT):
                if t >= 2:
                    sp.wait_ge(added, t - 1)
                src = d["x_prompt"][0] if t == 0 else d["x_sample"][0, (t - 1) * P:t * P, :]
                sp.dma_start(s.xr_ring[t % 2], src).then_inc(x_in[t % 2], 16)

        @block.tensor
        def _(pe):
            pe.wait_ge(w_in, 32)
            for t in range(NT):
                if t >= 4:
                    pe.wait_ge(gated, t - 3)
                for half in range(2):
                    for k in range(KD):
                        mm = nc.tensor.matmul(s.bank[2 * (t % 4) + half], s.oT[:, k, t * P:(t + 1) * P],
                                              s.w_out[:, k, half * 512:(half + 1) * 512], start=(k == 0), stop=(k == KD - 1))
                mm.then_inc(product, 1)

        @block.vector
        def _(dve):
            dve.wait_ge(g_in, 32)
            for t in range(NT):
                dve.wait_ge(product, t + 1)
                nc.vector.tensor_tensor(s.x1[:, t, :], s.pair[t % 4], s.g1_row[:, min(t, 1), :], ALU.mult).then_inc(gated, 1)
                dve.wait_ge(gated, t + 1)
                dve.wait_ge(x_in[t % 2], 16 * (t // 2 + 1))
                nc.vector.tensor_tensor(s.x1[:, t, :], s.x1[:, t, :], s.xr_ring[t % 2], ALU.add).then_inc(added, 1)


def stage_norm2(nc, s, d):
    sem = s.sem
    rows_in, squared, std_done, rstd_done, chain = [sem("n2_" + n) for n in ("in", "sq", "std", "rstd", "chain")]
    a_done, h_half, h_ready, h_stored = sem("n2_a"), sem("n2_half"), sem("h2_ready"), [sem(f"h2_stored{i}") for i in range(3)]
    turned, act_out, dve_out, zeroed = sem("h2_turned"), sem("h2_act_out"), sem("h2_dve_out"), sem("slots_zeroed")
    zero_set = sem("zero_set")
    logits_done = sem("logits_done")
    with nc.Block() as block:
        @block.sync
        def _(sp):
            for c in range(2):
                sp.dma_start(s.b2_row[:, c, :], d["mod_rows"][c:c + 1, 3 * D:4 * D].to_broadcast([P, D])).then_inc(rows_in, 16)
                sp.dma_start(s.a2_row[:, c, :], d["mod_rows"][c:c + 1, 4 * D:5 * D].to_broadcast([P, D])).then_inc(rows_in, 16)
            sp.dma_start(s.n2_row, d["norm2_g"].to_broadcast([P, D])).then_inc(rows_in, 16)
            sp.dma_start(s.w_router, d["w_router"].rearrange("(k p) e -> p k e", p=P)).then_inc(rows_in, 16)
            sp.wait_ge(zero_set, 1)
            sp.dma_start(d["slot_token"].rearrange("(p a) b -> p (a b)", p=P), s.zero_slots).then_inc(zeroed, 16)
            for t in range(NT):
                sp.wait_ge(h_ready, t + 1)
                sp.dma_start(d["h2_rows"][t * P:(t + 1) * P, :], s.h2_ring[t % 3]).then_inc(h_stored[t % 3], 16)
            for i in range(3):
                sp.wait_ge(h_stored[i], 16 * NT // 3)
            sp.wait_ge(zeroed, 16)

        @block.scalar
        def _(act):
            for t in range(NT):
                nc.scalar.activation(s.junk2, s.x1[:, t, :], ACT.Square, accum_out=s.ss[:, t:t + 1]).then_inc(squared, 1)
                act.wait_ge(squared, t + 1)
            nc.scalar.activation(s.rstd, s.ss, ACT.Sqrt, bias=s.epsc, scale=1.0 / D).then_inc(std_done, 1)
            for t in range(NT):
                act.wait_ge(turned, t + 1)
                nc.scalar.copy(s.h2T[:, 0:4, t * P:(t + 1) * P], s.bank[2 * (t % 2)].rearrange("p (a b) -> p a b", a=4)).then_inc(act_out, 1)

        @block.vector
        def _(dve):
            nc.vector.memset(s.zero_slots, 0).then_inc(zero_set, 1)
            dve.wait_ge(rows_in, 96)
            for c in range(2):
                nc.vector.scalar_tensor_tensor(s.a2_row[:, c, :], s.a2_row[:, c, :], 1.0, s.n2_row, ALU.add, ALU.mult).then_inc(a_done, 1)
            dve.wait_ge(a_done, 2)
            dve.wait_ge(std_done, 1)
            nc.vector.reciprocal(s.rstd, s.rstd).then_inc(rstd_done, 1)
            dve.wait_ge(rstd_done, 1)

            def make(t):
                if t >= 3:
                    dve.wait_ge(h_stored[t % 3], 16 * (t // 3))
                    dve.wait_ge(turned, t - 2)
                c = min(t, 1)
                nc.vector.scalar_tensor_tensor(s.h2_ring[t % 3], s.x1[:, t, :], s.rstd[:, t:t + 1], s.a2_row[:, c, :],
                                               ALU.mult, ALU.mult).then_inc(h_half, 1)
                dve.wait_ge(h_half, t + 1)
                nc.vector.tensor_tensor(s.h2_ring[t % 3], s.h2_ring[t % 3], s.b2_row[:, c, :], ALU.add).then_inc(h_ready, 1)

            make(0)
            for t in range(NT):
                if t + 1 < NT:
                    make(t + 1)
                dve.wait_ge(turned, t + 1)
                nc.vector.tensor_copy(s.h2T[:, 4:8, t * P:(t + 1) * P],
                                      s.bank[2 * (t % 2) + 1].rearrange("p (a b) -> p a b", a=4)).then_inc(dve_out, 1)

        @block.tensor
        def _(pe):
            for t in range(NT):
                pe.wait_ge(h_ready, t + 1)
                if t >= 2:
                    pe.wait_ge(act_out, t - 1)
                    pe.wait_ge(dve_out, t - 1)
                for k in range(KD):
                    tr = nc.tensor.transpose(s.bank[2 * (t % 2) + k // 4][:, (k % 4) * P:(k % 4 + 1) * P],
                                             s.h2_ring[t % 3][:, k * P:(k + 1) * P], s.ident)
                tr.then_inc(turned, 1)
            pe.wait_ge(act_out, NT)
            pe.wait_ge(dve_out, NT)
            pe.wait_ge(rows_in, 96)
            for t in range(NT):
                for k in range(KD):
                    mm = nc.tensor.matmul(s.bank[4][:, t * N_EXP:(t + 1) * N_EXP], s.h2T[:, k, t * P:(t + 1) * P],
                                          s.w_router[:, k, :], start=(k == 0), stop=(k == KD - 1))
            mm.then_inc(logits_done, 1)


def stage_route(nc, s, d):
    sem = s.sem
    b_in, sig_done, chain, mask_ready, counted = [sem("rt_" + n) for n in ("bias", "sig", "chain", "mask", "counted")]
    slots_ready, scattered, read_back = sem("slots_ready"), sem("slots_scattered"), sem("slots_read")
    R = s.route
    with nc.Block() as block:
        @block.sync
        def _(sp):
            sp.dma_start(s.b_router, d["b_router"].rearrange("(a e) -> a e", a=1).to_broadcast([P, N_EXP])).then_inc(b_in, 16)
            sp.wait_ge(scattered, 16 * 2 * NT)
            with nc.allow_non_contiguous_dma(reason="one token number per slot"):
                sp.dma_start(s.slot_idx, d["slot_token"].rearrange("(a p) b -> p (a b)", p=P)).then_inc(read_back, 16)
            sp.wait_ge(read_back, 16)

        @block.scalar
        def _(act):
            nc.scalar.activation(R["score"], s.bank[4][:, 0:NT * N_EXP], ACT.Sigmoid).then_inc(sig_done, 1)

        @block.gpsimd
        def _(pool):
            pool.wait_ge(slots_ready, 1)
            for t in range(NT):
                for which in (s.slot_hi, s.slot_lo):
                    nc.gpsimd.indirect_dma_start(out=d["slot_token"], out_offset=bass.IndirectOffsetOnAxis(ap=which[:, t:t + 1], axis=0),
                                                 in_=s.token_id[:, t:t + 1], in_offset=None).then_inc(scattered, 16)
            pool.wait_ge(scattered, 16 * 2 * NT)

        @block.tensor
        def _(pe):
            pe.wait_ge(mask_ready, 1)
            nc.tensor.matmul(s.bank[5][:, 0:NT * N_EXP], s.before, R["mask"], start=True, stop=True)
            nc.tensor.matmul(s.bank[6][:, 0:NT * N_EXP], s.ones, R["mask"], start=True, stop=True).then_inc(counted, 1)

        @block.vector
        def _(dve):
            done = [0]

            def link(ins):
                done[0] += 1
                ins.then_inc(chain, 1)
                dve.wait_ge(chain, done[0])

            def tt(out, a, b, op):
                link(nc.vector.tensor_tensor(out, a, b, op))

            def rank4(rank, x, tmp):
                link(nc.vector.memset(rank, 0.0))
                n = x.shape[1]
                for j in range(4):
                    if j > 0:
                        tt(tmp[:, :, 0:j], x[:, :, 0:j], x[:, :, j:j + 1].to_broadcast([P, n, j]), ALU.is_lt)
                        tt(rank[:, :, 0:j], rank[:, :, 0:j], tmp[:, :, 0:j], ALU.add)
                    if j < 3:
                        tt(tmp[:, :, j + 1:4], x[:, :, j + 1:4], x[:, :, j:j + 1].to_broadcast([P, n, 3 - j]), ALU.is_le)
                        tt(rank[:, :, j + 1:4], rank[:, :, j + 1:4], tmp[:, :, j + 1:4], ALU.add)

            g4 = lambda v: v.rearrange("p (n e) -> p n e", e=4)
            t16 = lambda v: v.rearrange("p (t e) -> p t e", e=N_EXP)
            dve.wait_ge(b_in, 16)
            dve.wait_ge(sig_done, 1)
            tt(t16(R["sel"]), t16(R["score"]), s.b_router.unsqueeze(1).to_broadcast([P, NT, N_EXP]), ALU.add)
            rank4(g4(R["rank"]), g4(R["sel"]), g4(R["tmp"]))
            link(nc.vector.tensor_scalar(R["mask"], R["rank"], 1.5, None, ALU.is_lt))
            tt(R["tmp"], R["sel"], R["mask"], ALU.mult)
            link(nc.vector.tensor_reduce(R["gsum"], g4(R["tmp"]), AX.X, ALU.add))
            rank4(g4(R["grank"]), g4(R["gsum"]), g4(R["gtmp"]))
            link(nc.vector.tensor_scalar(R["gmask"], R["grank"], 0.5, None, ALU.is_lt))
            link(nc.vector.tensor_tensor(g4(R["mask"]), g4(R["mask"]), R["gmask"].unsqueeze(2).to_broadcast([P, 36, 4]), ALU.mult))
            nc.vector.nop().then_inc(mask_ready, 1)
            tt(R["weight"], R["score"], R["mask"], ALU.mult)
            link(nc.vector.tensor_reduce(R["wsum"], t16(R["weight"]), AX.X, ALU.add))
            link(nc.vector.reciprocal(R["wsum"], R["wsum"]))
            tt(t16(R["weight"]), t16(R["weight"]), R["wsum"].unsqueeze(2).to_broadcast([P, NT, N_EXP]), ALU.mult)
            dve.wait_ge(counted, 1)
            count = t16(s.bank[6][:, 0:NT * N_EXP])
            off = t16(R["off"])
            link(nc.vector.memset(off[:, 0, :], 0.0))
            for t in range(1, NT):
                tt(off[:, t, :], off[:, t - 1, :], count[:, t - 1, :], ALU.add)
            tt(R["total"], off[:, NT - 1, :], count[:, NT - 1, :], ALU.add)
            tt(R["slot"], R["off"], s.bank[5][:, 0:NT * N_EXP], ALU.add)
            link(nc.vector.memset(R["over"], 0.0))
            for k in range((N_TOK - CAP + P - 1) // P):
                link(nc.vector.tensor_scalar(R["o16"], R["total"], CAP + k * P + 0.5, None, ALU.is_gt))
                tt(R["over"], R["over"], R["o16"], ALU.add)
            link(nc.vector.tensor_tensor_scan(R["cum"], s.ones[:, 0:N_EXP], R["over"], 0.0, ALU.mult, ALU.add))
            tt(R["o16"], R["cum"], R["over"], ALU.subtract)
            link(nc.vector.tensor_scalar(R["o16"], R["o16"], float(P), float((N_EXP - 1) * CAP), ALU.mult, ALU.add))
            tt(R["o16"], R["o16"], s.grid16, ALU.subtract)
            link(nc.vector.tensor_scalar(R["tmp"], R["slot"], CAP - 0.5, None, ALU.is_gt))
            tt(t16(R["tmp"]), t16(R["tmp"]), R["o16"].unsqueeze(1).to_broadcast([P, NT, N_EXP]), ALU.mult)
            tt(R["slot"], R["slot"], R["tmp"], ALU.add)
            tt(t16(R["slot"]), t16(R["slot"]), s.grid16.unsqueeze(1).to_broadcast([P, NT, N_EXP]), ALU.add)
            tt(R["slot"], R["slot"], R["mask"], ALU.mult)
            link(nc.vector.tensor_reduce(R["hi"], t16(R["slot"]), AX.X, ALU.max))
            link(nc.vector.tensor_reduce(R["lo"], t16(R["slot"]), AX.X, ALU.add))
            tt(R["lo"], R["lo"], R["hi"], ALU.subtract)
            link(nc.vector.tensor_copy(s.slot_hi, R["hi"]))
            link(nc.vector.tensor_copy(s.slot_lo, R["lo"]))
            link(nc.vector.tensor_copy(s.token_id, s.token))
            nc.vector.nop().then_inc(slots_ready, 1)
            tt(t16(R["tmp"]), t16(R["slot"]), R["hi"].unsqueeze(2).to_broadcast([P, NT, N_EXP]), ALU.is_equal)
            tt(R["rank"], R["weight"], R["tmp"], ALU.mult)
            link(nc.vector.tensor_reduce(s.w_hi, t16(R["rank"]), AX.X, ALU.add))
            tt(R["rank"], R["weight"], R["rank"], ALU.subtract)
            link(nc.vector.tensor_reduce(s.w_lo, t16(R["rank"]), AX.X, ALU.add))
            ex = R["rank"][:, 0:OVER].rearrange("p (a b) -> p a b", b=1)
            wide = s.over_cmp
            link(nc.vector.tensor_tensor(wide, R["cum"].unsqueeze(1).to_broadcast([P, OVER, N_EXP]),
                                         s.over_id.unsqueeze(2).to_broadcast([P, OVER, N_EXP]), ALU.is_le))
            link(nc.vector.tensor_reduce(R["tmp"][:, 0:OVER], wide, AX.X, ALU.add))
            link(nc.vector.tensor_scalar(R["tmp"][:, 0:OVER], R["tmp"][:, 0:OVER], float(N_EXP - 1), None, ALU.min))
            nc.vector.tensor_copy(s.over_table[:, 0:OVER], R["tmp"][:, 0:OVER])
            nc.vector.tensor_copy(s.over_table[:, OVER:OVER + 1], R["cum"][:, N_EXP - 1:N_EXP])


def stage_experts(nc, s, d):
    sem = s.sem
    w_in = [sem(f"we_in{i}") for i in range(6)]
    gathered, turned, act_out, dve_out = [sem(f"gathered{i}") for i in range(2)], sem("hg_turned"), sem("hg_act_out"), sem("hg_dve_out")
    gate_up, silu_done, hid_ready, down_done = sem("gate_up"), sem("hid_silu"), sem("hid_ready"), sem("down_done")
    y_act, y_dve, y_stored = sem("y_act"), sem("y_dve"), [sem(f"y_stored{i}") for i in range(3)]
    kinds = ("w_gate", "w_up", "w_down")
    FB = FF // P

    def place(e, j):
        return (3 * e + j) % 6

    with nc.Block() as block:
        @block.sync
        def _(sp):
            for e in range(N_EXP):
                for j, kind in enumerate(kinds):
                    if e >= 2:
                        if kind == "w_down":
                            sp.wait_ge(down_done, 2 * (e - 1))
                        else:
                            sp.wait_ge(gate_up, FB * (e - 1))
                    src = d[kind][0, e].rearrange("(k p) n -> p k n", p=P)
                    dst = s.we_ring[place(e, j)].rearrange("p (k n) -> p k n", n=src.shape[2])
                    sp.dma_start(dst, src).then_inc(w_in[place(e, j)], 16)

        @block.gpsimd
        def _(pool):
            for e in range(N_EXP):
                if e >= 2:
                    pool.wait_ge(turned, 2 * (e - 1))
                for i in range(2):
                    nc.gpsimd.indirect_dma_start(out=s.hg[e % 2][:, i, :], out_offset=None, in_=d["h2_rows"],
                                                 in_offset=bass.IndirectOffsetOnAxis(ap=s.slot_idx[:, 2 * e + i:2 * e + i + 1], axis=0)
                                                 ).then_inc(gathered[e % 2], 16)

        @block.scalar
        def _(act):
            def turned_out(e):
                for i in range(2):
                    act.wait_ge(turned, 2 * e + i + 1)
                    if e >= 2:
                        act.wait_ge(gate_up, FB * (e - 1))
                    nc.scalar.copy(s.hgT[e % 2][:, 0:4, i * P:(i + 1) * P], s.bank[0].rearrange("p (a b) -> p a b", a=4)).then_inc(act_out, 1)

            turned_out(0)
            for e in range(N_EXP):
                for f in range(FB):
                    u = FB * e + f
                    act.wait_ge(gate_up, u + 1)
                    if u >= 2:
                        act.wait_ge(hid_ready, u - 1)
                    nc.scalar.activation(s.sg[u % 2], s.bank[2 + u % 2][:, 0:CAP], ACT.Silu).then_inc(silu_done, 1)
                if e + 1 < N_EXP:
                    turned_out(e + 1)
                for i in range(2):
                    v = 2 * e + i
                    act.wait_ge(down_done, v + 1)
                    if v >= 3:
                        act.wait_ge(y_stored[v % 3], 16 * (v // 3))
                    nc.scalar.copy(s.y_ring[v % 3][:, 0:512], s.bank[4 + 2 * i]).then_inc(y_act, 1)
                    act.wait_ge(y_act, v + 1)
                    act.wait_ge(y_dve, v + 1)
                    act.dma_start(d["slot_rows"][v * P:(v + 1) * P, :], s.y_ring[v % 3]).then_inc(y_stored[v % 3], 16)
            for i in range(3):
                act.wait_ge(y_stored[i], 16 * len(range(i, 2 * N_EXP, 3)))

        @block.vector
        def _(dve):
            def turned_out(e):
                for i in range(2):
                    dve.wait_ge(turned, 2 * e + i + 1)
                    if e >= 2:
                        dve.wait_ge(gate_up, FB * (e - 1))
                    nc.vector.tensor_copy(s.hgT[e % 2][:, 4:8, i * P:(i + 1) * P], s.bank[1].rearrange("p (a b) -> p a b", a=4)).then_inc(dve_out, 1)

            turned_out(0)
            for e in range(N_EXP):
                for f in range(FB):
                    u = FB * e + f
                    dve.wait_ge(silu_done, u + 1)
                    if e >= 2 and f == 0:
                        dve.wait_ge(down_done, 2 * (e - 1))
                    nc.vector.tensor_tensor(s.hid[e % 2][:, f, :], s.sg[u % 2], s.bank[2 + u % 2][:, CAP:2 * CAP], ALU.mult).then_inc(hid_ready, 1)
                if e + 1 < N_EXP:
                    turned_out(e + 1)
                for i in range(2):
                    v = 2 * e + i
                    dve.wait_ge(down_done, v + 1)
                    if v >= 3:
                        dve.wait_ge(y_stored[v % 3], 16 * (v // 3))
                    nc.vector.tensor_copy(s.y_ring[v % 3][:, 512:1024], s.bank[5 + 2 * i]).then_inc(y_dve, 1)

        @block.tensor
        def _(pe):
            def turn(e):
                for i in range(2):
                    v = 2 * e + i
                    if i == 0:
                        pe.wait_ge(gathered[e % 2], 32 * (e // 2 + 1))
                    if v >= 1:
                        pe.wait_ge(act_out, v)
                        pe.wait_ge(dve_out, v)
                    for k in range(KD):
                        tr = nc.tensor.transpose(s.bank[k // 4][:, (k % 4) * P:(k % 4 + 1) * P], s.hg[e % 2][:, i, k * P:(k + 1) * P], s.ident)
                    tr.then_inc(turned, 1)

            turn(0)
            for e in range(N_EXP):
                pe.wait_ge(act_out, 2 * e + 2)
                pe.wait_ge(dve_out, 2 * e + 2)
                W = [s.we_ring[place(e, j)].rearrange("p (k n) -> p k n", n=(FF, FF, D)[j]) for j in range(3)]
                for j in range(2):
                    pe.wait_ge(w_in[place(e, j)], 16 * (e // 2 + 1))
                for f in range(FB):
                    u = FB * e + f
                    if u >= 2:
                        pe.wait_ge(hid_ready, u - 1)
                    for j in range(2):
                        for k in range(KD):
                            mm = nc.tensor.matmul(s.bank[2 + u % 2][:, j * CAP:(j + 1) * CAP], W[j][:, k, f * P:(f + 1) * P],
                                                  s.hgT[e % 2][:, k, :], start=(k == 0), stop=(k == KD - 1))
                    mm.then_inc(gate_up, 1)
                if e + 1 < N_EXP:
                    turn(e + 1)
                pe.wait_ge(w_in[place(e, 2)], 16 * (e // 2 + 1))
                pe.wait_ge(hid_ready, FB * (e + 1))
                for i in range(2):
                    v = 2 * e + i
                    if e >= 1:
                        pe.wait_ge(y_act, v - 1)
                        pe.wait_ge(y_dve, v - 1)
                    for half in range(2):
                        for f in range(FB):
                            mm = nc.tensor.matmul(s.bank[4 + 2 * i + half], s.hid[e % 2][:, f, i * P:(i + 1) * P],
                                                  W[2][:, f, half * 512:(half + 1) * 512], start=(f == 0), stop=(f == FB - 1))
                    mm.then_inc(down_done, 1)


def stage_further(nc, s, d):
    n_over = nc.values_load(s.over_table[0:1, OVER:OVER + 1], min_val=0, max_val=OVER)
    first = N_EXP * CAP
    FB = FF // P
    Wv = [s.we_ring[j].rearrange("p (k n) -> p k n", n=(FF, FF, D)[j]) for j in range(3)]
    kinds = ("w_gate", "w_up", "w_down")
    sem = s.sem
    idx_in, w_in, rows_in, turned, out = sem("fu_idx"), sem("fu_w"), sem("fu_rows"), sem("fu_turned"), sem("fu_out")
    gate_up, silu_done, hid_ready, down, y_ready, stored = [sem("fu_" + n) for n in ("gate_up", "silu", "hid", "down", "y", "stored")]
    counted = [idx_in, w_in, turned, out, gate_up, silu_done, hid_ready, down, y_ready, stored]
    with nc.If(n_over > 0):
        with nc.Fori(0, OVER) as o:
            with nc.Block() as block:
                @block.sync
                def _(sp):
                    with nc.allow_non_contiguous_dma(reason="one token number per slot"):
                        sp.dma_start(s.further_idx, d["slot_token"][bass.ds(first + o * P, P), :]).then_inc(idx_in, 16)
                    e = sp.value_load(s.over_table[0:1, bass.ds(o, 1)], min_val=0, max_val=N_EXP - 1)
                    for j, kind in enumerate(kinds):
                        src = d[kind][0].rearrange("e (k p) n -> p (e k) n", p=P)
                        k = src.shape[1] // N_EXP
                        sp.dma_start(Wv[j], src[:, bass.ds(e * k, k), :]).then_inc(w_in, 16)
                    sp.wait_ge(y_ready, 4)
                    sp.dma_start(d["slot_rows"][bass.ds(first + o * P, P), :], s.y_ring[0]).then_inc(stored, 16)
                    sp.wait_ge(stored, 16)

                @block.gpsimd
                def _(pool):
                    pool.wait_ge(idx_in, 16)
                    nc.gpsimd.indirect_dma_start(out=s.hg[0][:, 0, :], out_offset=None, in_=d["h2_rows"],
                                                 in_offset=bass.IndirectOffsetOnAxis(ap=s.further_idx, axis=0)).then_inc(rows_in, 16)
                    pool.wait_ge(rows_in, o * 16 + 16)

                @block.tensor
                def _(pe):
                    pe.wait_ge(rows_in, o * 16 + 16)
                    for k in range(KD):
                        tr = nc.tensor.transpose(s.bank[k // 4][:, (k % 4) * P:(k % 4 + 1) * P], s.hg[0][:, 0, k * P:(k + 1) * P], s.ident)
                    tr.then_inc(turned, 1)
                    pe.wait_ge(out, 2)
                    pe.wait_ge(w_in, 48)
                    for f in range(FB):
                        for j in range(2):
                            for k in range(KD):
                                mm = nc.tensor.matmul(s.bank[2 + f][:, j * P:(j + 1) * P], Wv[j][:, k, f * P:(f + 1) * P],
                                                      s.hgT[0][:, k, 0:P], start=(k == 0), stop=(k == KD - 1))
                        mm.then_inc(gate_up, 1)
                    pe.wait_ge(hid_ready, FB)
                    for half in range(2):
                        for f in range(FB):
                            mm = nc.tensor.matmul(s.bank[6 + half], s.hid[0][:, f, 0:P], Wv[2][:, f, half * 512:(half + 1) * 512],
                                                  start=(f == 0), stop=(f == FB - 1))
                    mm.then_inc(down, 1)

                @block.scalar
                def _(act):
                    act.wait_ge(turned, 1)
                    for half in range(2):
                        nc.scalar.copy(s.hgT[0][:, 4 * half:4 * half + 4, 0:P], s.bank[half].rearrange("p (a b) -> p a b", a=4)).then_inc(out, 1)
                    for f in range(FB):
                        act.wait_ge(gate_up, f + 1)
                        nc.scalar.activation(s.further_gate[:, f, :], s.bank[2 + f][:, 0:P], ACT.Silu).then_inc(silu_done, 1)

                @block.vector
                def _(dve):
                    for f in range(FB):
                        dve.wait_ge(silu_done, f + 1)
                        nc.vector.tensor_tensor(s.hid[0][:, f, 0:P], s.further_gate[:, f, :], s.bank[2 + f][:, P:2 * P], ALU.mult).then_inc(hid_ready, 1)
                    dve.wait_ge(down, 1)
                    for half in range(2):
                        nc.vector.tensor_copy(s.y_ring[0][:, half * 512:(half + 1) * 512], s.bank[6 + half]).then_inc(y_ready, 2)
            for one in counted:
                nc.sync.sem_clear(one)
            nc.all_engine_barrier()
    nc.end_ifs()


def stage_combine(nc, s, d):
    sem = s.sem
    g_in, in_hi, in_lo = sem("g2_in"), [sem(f"y_hi{i}") for i in range(2)], [sem(f"y_lo{i}") for i in range(2)]
    chain, ready, stored = sem("cb_chain"), sem("y_ready"), s.out_sem["y_out"]
    with nc.Block() as block:
        @block.sync
        def _(sp):
            for c in range(2):
                sp.dma_start(s.g2_row[:, c, :], d["mod_rows"][c:c + 1, 5 * D:6 * D].to_broadcast([P, D])).then_inc(g_in, 16)
            for t in range(NT):
                sp.wait_ge(ready, t + 1)
                dst = d["out_y_prompt"][0] if t == 0 else d["out_y_sample"][0, (t - 1) * P:t * P, :]
                sp.dma_start(dst, s.x1[:, t, :]).then_inc(stored, 16)
            sp.wait_ge(stored, 16 * NT)

        @block.gpsimd
        def _(pool):
            for t in range(NT):
                if t >= 2:
                    pool.wait_ge(ready, t - 1)
                for buf, idx, got in ((s.y_hi, s.slot_hi, in_hi), (s.y_lo, s.slot_lo, in_lo)):
                    nc.gpsimd.indirect_dma_start(out=buf[t % 2], out_offset=None, in_=d["slot_rows"],
                                                 in_offset=bass.IndirectOffsetOnAxis(ap=idx[:, t:t + 1], axis=0)).then_inc(got[t % 2], 16)

        @block.vector
        def _(dve):
            done = [0]

            def link(ins):
                done[0] += 1
                ins.then_inc(chain, 1)
                dve.wait_ge(chain, done[0])

            dve.wait_ge(g_in, 32)
            for t in range(NT):
                a, b = s.y_hi[t % 2], s.y_lo[t % 2]
                dve.wait_ge(in_hi[t % 2], 16 * (t // 2 + 1))
                link(nc.vector.tensor_scalar(a, a, s.w_hi[:, t:t + 1], None, ALU.mult))
                dve.wait_ge(in_lo[t % 2], 16 * (t // 2 + 1))
                link(nc.vector.scalar_tensor_tensor(a, b, s.w_lo[:, t:t + 1], a, ALU.mult, ALU.add))
                link(nc.vector.tensor_tensor(a, a, s.g2_row[:, min(t, 1), :], ALU.mult))
                nc.vector.tensor_tensor(s.x1[:, t, :], s.x1[:, t, :], a, ALU.add).then_inc(ready, 1)


def constants():
    import numpy as np
    i = np.arange(P)
    same = (i[:, None] // HEAD) == (i[None, :] // HEAD)
    out = {
        "ident": np.eye(P),
        "tri_f": same & (i[:, None] <= i[None, :]),
        "tri_b": same & (i[:, None] >= i[None, :]),
        "block": same,
        "strict_f": same & (i[:, None] > i[None, :]),
        "strict_b": same & (i[:, None] < i[None, :]),
        "before": i[:, None] < i[None, :],
        "ones": np.ones((P, P)),
        "grid16": np.tile(np.arange(16) * CAP, (P, 1)),
        "over_id": np.tile(np.arange(OVER), (P, 1)),
        "token": np.arange(NT)[None, :] * P + i[:, None],
    }
    level = []
    for b in range(6):
        size = 1 << b
        bi, bj = i[:, None] // size, i[None, :] // size
        level.append((bi % 2 == 1) & (bj == bi - 1))
    out["level_f"] = np.concatenate(level, axis=1)
    out["level_b"] = np.concatenate([m.T for m in level], axis=1)
    q = (i % GRID)[:, None]
    k = np.arange(GRID)[None, :]
    start = np.clip(q - 8, 0, GRID - 16)
    out["colmask"] = np.where((k >= start) & (k < start + 16), 0.0, NEG)
    return np.concatenate([np.asarray(out[n], np.float32) for n in CST], axis=1)


def pool_counts():
    import numpy as np
    out = np.ones((P, 2, POOL_ROW), np.float32)
    for g, win in enumerate((2, 4, 8, 16)):
        for at, n in ((POOL_CTX, CTX), (POOL_LAT, LAT)):
            t = np.arange(n)
            count = np.clip(t + win - win // 2, 0, n) - np.clip(t - win // 2, 0, n)
            out[HEAD * (g % 2):HEAD * (g % 2 + 1), g // 2, at:at + n] = 1.0 / count
    return out


STAGES = [stage_modulation, stage_norm1, stage_project, stage_heads, stage_attention,
          stage_dn_prepare, stage_dn_scan, stage_dn_finish, stage_pool, stage_turn_mix, stage_output,
          stage_norm2, stage_route, stage_experts, stage_further, stage_combine]

IN_SHAPES = {
    "x_prompt": (1, CTX, D), "x_sample": (1, LAT, D), "cache_na_k": (1, 1, NA_H, PAST, HEAD),
    "cache_na_v": (1, 1, NA_H, PAST, HEAD), "state_dn": (1, 1, 2, DN_H, HEAD, HEAD), "c": (1, D), "c_ctx": (D,),
    "norm1_g": (1, D), "norm2_g": (1, D), "w_ada": (1, D, 6 * D), "b_ada": (1, 6 * D), "w_in": (1, D, IN_W),
    "w_out": (1, D, D), "w_pool": (1, 4, HEAD, HEAD), "pool_scale": (1, POOL_W), "q_norm_g": (1, HEAD),
    "k_norm_g": (1, HEAD), "dn_conv_w": (1, 4, 3 * DN_W), "dn_a_log": (1, 2, DN_H), "dn_dt_bias": (1, 2, DN_H),
    "dn_norm_g": (1, HEAD), "w_router": (D, N_EXP), "b_router": (N_EXP,), "w_gate": (1, N_EXP, D, FF),
    "w_up": (1, N_EXP, D, FF), "w_down": (1, N_EXP, FF, D),
}


def declare(nc, inputs):
    import numpy as np
    arrays, d = {}, {}
    own = {name: inputs[name] for name in IN_SHAPES}
    own["rpb"] = inputs["rpb"]
    own["consts"] = constants()
    own["pool_counts"] = pool_counts()
    for name, a in own.items():
        a = np.ascontiguousarray(a)
        arrays[f"in_{name}"] = a
        d[name] = nc.dram_tensor(f"in_{name}", a.shape, F32, kind="ExternalInput").ap()
    outs = [("out_y_prompt", (1, CTX, D)), ("out_y_sample", (1, LAT, D)), ("out_k", (1, 1, NA_H, CTX, HEAD)),
            ("out_v", (1, 1, NA_H, CTX, HEAD)), ("out_state", (1, 1, 2, DN_H, HEAD, HEAD))]
    for name, shape in outs:
        d[name] = nc.dram_tensor(name, shape, F32, kind="ExternalOutput").ap()
    d["rpb_rows"] = nc.dram_tensor("rpb_rows", (NA_H * 15, RPB_ROW), F32).ap()
    d["mod_rows"] = nc.dram_tensor("mod_rows", (2, 6 * D), F32).ap()
    d["h2_rows"] = nc.dram_tensor("h2_rows", (N_TOK, D), F32).ap()
    d["slot_token"] = nc.dram_tensor("slot_token", (SLOTS, 1), U32).ap()
    d["slot_rows"] = nc.dram_tensor("slot_rows", (SLOTS, D), F32).ap()
    s = Store()
    s.out_sem = {name: nc.alloc_semaphore(name) for name in ("v_stored", "kn_stored", "state_out", "y_out")}
    s.WORDS = 53120
    views(nc, s)
    psum = nc.alloc_psum_tensor("psum", [P, 8 * 512], F32)
    s.bank = [psum[:, 512 * i:512 * (i + 1)] for i in range(8)]
    s.pair = [psum[:, 1024 * i:1024 * (i + 1)] for i in range(4)]
    return arrays, d, [n for n, _ in outs], s


def run_stage(nc, s, d, stage):
    held = []

    def sem(name):
        held.append(nc.alloc_semaphore(name))
        return held[-1]

    s.sem = sem
    stage(nc, s, d)
    nc.clear_and_free_semaphores(held)
    nc.all_engine_barrier()


def kernel(**inputs):
    import concourse.bacc as bacc
    from concourse.bass_utils import run_bass_kernel_spmd

    nc = bacc.Bacc("TRN2", target_bir_lowering=False, num_devices=1)
    arrays, d, outs, s = declare(nc, inputs)
    for stage in STAGES:
        run_stage(nc, s, d, stage)
    r = run_bass_kernel_spmd(nc, [arrays], core_ids=[0])
    return tuple(r.results[0][name] for name in outs)
```

```python
import concourse.bass as bass
from concourse import mybir

F32 = mybir.dt.float32
U32 = mybir.dt.uint32
F32R = mybir.dt.float32r
ALU = mybir.AluOpType
ACT = mybir.ActivationFunctionType
AX = mybir.AxisListType

P = 128
D = 1024
KD = D // P
CTX, LAT = 128, 1024
N_TOK = CTX + LAT
NT = N_TOK // P
POOL_W, NA_W, DN_W = 256, 512, 256
HEAD = 64
NA_H, DN_H = NA_W // HEAD, DN_W // HEAD
IN_W = POOL_W + 3 * NA_W + 3 * DN_W + DN_W + 4 * DN_H
PAST = 256
N_EXP, GRP, TOP = 16, 4, 2
FF = 512
EPS = 1e-6
NEG = -1e30
GRID = 64
RPB_W = 31
RPB_REP = 66
RPB_ROW = RPB_REP * RPB_W

POOL_PAD = 8
POOL_CTX = POOL_PAD
POOL_LAT = POOL_CTX + CTX + POOL_PAD
POOL_ROW = POOL_LAT + LAT + POOL_PAD
CONV_CTX = 1
CONV_LAT = CONV_CTX + CTX + 2 + 1
CONV_ROW = CONV_LAT + LAT + 2

CAP = 256
UNITS = 6
UNIT_X, UNIT_H = 7, 6
OVER = (2 * N_TOK - 2 * CAP) // P
SLOTS = N_EXP * CAP + OVER * P

COL_POOL = 0
COL_Q = COL_POOL + POOL_W
COL_K = COL_Q + NA_W
COL_V = COL_K + NA_W
COL_DN = COL_V + NA_W
COL_Z = COL_DN + 3 * DN_W

CST = {}
_at = 0
for _name, _n in (("ident", P), ("tri_f", P), ("tri_b", P), ("block", P), ("strict_f", P), ("strict_b", P),
                  ("level_f", 6 * P), ("level_b", 6 * P), ("colmask", GRID), ("before", P), ("ones", P),
                  ("grid16", 16), ("token", NT), ("over_id", OVER)):
    CST[_name] = (_at, _n)
    _at += _n
CST_W = _at


class Store:
    pass


def views(nc, s):
    base = (nc.sbuf_base + 31) // 32 * 32
    arena = nc.alloc_sbuf_tensor("arena", [P, s.WORDS], F32)
    s.arena = arena

    def view(at, *shape):
        n = 1
        for x in shape:
            n *= x
        assert at + n <= s.WORDS, (at, n)
        v = arena[:, at:at + n]
        if len(shape) == 2:
            v = v.rearrange("p (a b) -> p a b", a=shape[0])
        elif len(shape) == 3:
            v = v.rearrange("p (a b c) -> p a b c", a=shape[0], b=shape[1])
        return v

    def parts(name, at, *shape):
        n = 1
        for x in shape:
            n *= x
        v = nc.alloc_sbuf_tensor_at(name, [P, n], F32R, offset=base + 4 * at)[:, :]
        return v.rearrange("p (a b) -> p a b", a=shape[0]) if len(shape) == 2 else v

    s.view = view
    s.cst = view(0, CST_W)
    cst = lambda name, *shape: view(CST[name][0], *(shape or (CST[name][1],)))
    s.ident, s.tri_f, s.tri_b, s.block = cst("ident"), cst("tri_f"), cst("tri_b"), cst("block")
    s.strict_f, s.strict_b = cst("strict_f"), cst("strict_b")
    s.level_f, s.level_b = cst("level_f", 6, P), cst("level_b", 6, P)
    s.colmask, s.before, s.ones = cst("colmask"), cst("before"), cst("ones")
    s.grid16, s.token, s.over_id = cst("grid16"), cst("token"), cst("over_id")
    at = CST_W
    s.mod_a1 = view(at, KD, 2); at += 16
    s.mod_b1 = view(at, KD, 2); at += 16
    s.gain1 = view(at, KD); at += 8
    s.gain2 = view(at, KD); at += 8
    s.epsc = view(at, 1); at += 1
    s.zero = view(at, 1); at += 1
    s.ss = view(at, NT); at += NT
    s.rstd = view(at, NT); at += NT
    s.qgain = view(at, 1); at += 1
    s.kgain = view(at, 1); at += 1
    s.pscale = view(at, 2); at += 2
    assert at <= 3072, at
    B = 3072
    s.silu = view(B, KD, 2)
    s.cond = view(B + 16, KD, 2)
    s.mod = view(B + 32, 6 * D)
    s.ada_ring = [view(B + 32 + 6 * D + i * 4096, KD, 512) for i in range(4)]
    s.b_ada = view(B + 32 + 6 * D + 4 * 4096, 6 * D)
    s.hT = view(B, KD, N_TOK)
    s.pool_fm = view(12288, 2, POOL_ROW)
    s.qkv_fm = view(14656, 6, CONV_ROW)
    s.q_tm = view(21604, NT, NA_W)
    s.k_tm = view(26212, NT, NA_W)
    s.v_tm = view(30820, NT, NA_W)
    s.zba = view(35428, NT, DN_W + 4 * DN_H)
    s.w_ring = [view(37876 + 4096 * i, KD * 512) for i in range(2)]
    s.x_all = view(21604, NT, D)
    s.xn_ring = [view(46068 + 1024 * i, D) for i in range(3)]
    s.junk = view(49140, D)
    s.zero_rows = view(50164, D)
    s.qT = view(37876, 4, N_TOK)
    s.kT = view(42484, 4, N_TOK)
    s.kcT = view(47092, 4, PAST)
    s.vc_tm = view(48116, 2, NA_W)
    s.kc_tm = view(49140, 2, NA_W)
    s.sq_ring = [view(50164 + 512 * i, 512) for i in range(2)]
    s.qk_ss = view(51188, 2 * NT * NA_H)
    s.qk_r = view(51332, 2 * NT * NA_H)
    s.kgain_row = view(51476, HEAD)
    s.kn_ctx = view(51540, NA_W)
    s.bias = [view(21604 + 896 * i, 14, GRID) for i in range(2)]
    s.bias_mid = [view(23396 + 576 * i, 9, GRID) for i in range(2)]
    s.weights = [view(24548 + 832 * i, 832) for i in range(2)]
    s.wT = [view(26212 + 896 * i, 7 * P) for i in range(2)]
    s.at_m1, s.at_max, s.at_nm, s.at_sum, s.at_inv = [view(28004 + 4 * i, 4) for i in range(5)]
    s.o_naT = view(3072, 4, N_TOK)
    s.o_dn = view(7680, NT, DN_W)
    s.qkv_tm = view(21604, NT, 3 * DN_W)
    at = 28516
    s.taps = view(at, 6, 4); at += 24
    s.a_log = view(at, 8); at += 8
    s.dt_bias = view(at, 8); at += 8
    s.a_in, s.a_abs, s.g, s.cum, s.g_rest, s.beta, s.beta_eg, s.dn_ss = [view(at + NT * 8 * i, NT, 8) for i in range(8)]
    at += 8 * NT * 8
    s.dn_sq = [view(at + 512 * i, 512) for i in range(2)]; at += 1024
    s.S_ctx = view(at, 2, 4, HEAD); at += 512
    s.S_lat = view(at, 2, 4, HEAD); at += 512
    s.fin_r = view(at, NT * DN_H); at += 36
    s.dn_gain = view(at, HEAD); at += 64
    s.kb, s.vb, s.kg, s.kd, s.su, s.vn = [[view(at + 512 * j + 256 * i, 256) for i in range(2)] for j in range(6)]
    at += 6 * 512
    assert at <= 35428, at
    s.conv = view(37876, 6, CONV_ROW - 3)
    at = 37876
    (s.sqT, s.skT, s.skbT, s.pos, s.neg, s.dec, s.decT, s.eb, s.L, s.LT, s.attT, s.X, s.Z,
     s.Y) = [[view(at + 1024 * j + 512 * i, 512) for i in range(2)] for j in range(14)]
    at += 14 * 1024
    s.swT = [view(14656 + 512 * i, 512) for i in range(2)]
    s.sqd = [view(15680 + 512 * i, 512) for i in range(2)]
    s.sqT, s.skT, s.skbT, s.swT, s.sqd = [[v[0:HEAD, :] for v in pair] for pair in (s.sqT, s.skT, s.skbT, s.swT, s.sqd)]
    assert at <= 53120, at
    s.o_poolT = view(14656, 2, N_TOK)
    s.o_dnT = view(16960, 2, N_TOK)
    s.pool_a = view(37876, 2, POOL_ROW)
    s.pool_b = view(40244, 2, POOL_ROW)
    s.pooled = view(42612, 2, POOL_ROW)
    s.pool_rc = view(44980, 2, POOL_ROW)
    s.w_pool = view(47348, 2, HEAD)
    s.w_out = view(21604, KD, D)
    s.g1_row = view(31700, 2, D)
    s.xr_ring = [view(33748 + D * i, D) for i in range(2)]
    s.x1 = view(42784, NT, D)
    s.h2T = view(27648, KD, N_TOK)
    s.a2_row = view(36864, 2, D)
    s.b2_row = view(38912, 2, D)
    s.n2_row = view(40960, D)
    s.w_router = view(41984, KD, N_EXP)
    s.junk2 = view(23552, D)
    s.h2_ring = [view(24576 + D * i, D) for i in range(3)]
    s.zero_slots = view(42112, SLOTS // P).bitcast(U32)
    at = 52000
    s.b_router = view(at, N_EXP); at += 16
    s.slot_idx = view(at, SLOTS // P).bitcast(U32); at += SLOTS // P
    s.slot_hi, s.slot_lo, s.token_id = [view(at + NT * i, NT).bitcast(U32) for i in range(3)]; at += 3 * NT
    s.w_hi, s.w_lo = [view(at + NT * i, NT) for i in range(2)]; at += 2 * NT
    s.over_table = view(at, OVER + 1).bitcast(U32); at += OVER + 1
    assert at <= 52736
    at = 27648
    s.route = {}
    for name in ("score", "sel", "rank", "tmp", "mask", "weight", "off", "slot"):
        s.route[name] = view(at, NT * N_EXP); at += NT * N_EXP
    for name in ("gsum", "grank", "gtmp", "gmask"):
        s.route[name] = view(at, NT * 4); at += NT * 4
    for name in ("wsum", "hi", "lo"):
        s.route[name] = view(at, NT); at += NT
    for name in ("total", "over", "o16", "cum"):
        s.route[name] = view(at, N_EXP); at += N_EXP
    s.over_cmp = view(at, OVER, N_EXP)
    s.we_ring = [view(3072 + 4096 * i, 4096) for i in range(6)]
    s.hg = [view(27648 + 2048 * i, 2, D) for i in range(2)]
    s.hgT = [view(31744 + 2048 * i, KD, CAP) for i in range(2)]
    s.hid = [view(35840 + 1024 * i, 4, CAP) for i in range(2)]
    s.sg = [view(37888 + 256 * i, CAP) for i in range(2)]
    s.y_ring = [view(38400 + 1024 * i, D) for i in range(3)]
    s.unit_x = [view(3072 + 2048 * i, 2048) for i in range(UNIT_X)]
    s.unit_low = [parts(f"unit_low{i}", 3072 + 2048 * i, 2048) for i in range(UNIT_X)]
    s.unit_high = [parts(f"unit_high{i}", 17408 + 2048 * i, 2048) for i in range(UNIT_H)]
    s.hg_rows = view(29696, 2, D)
    s.hgT_high = parts("hgT_high", 31744, KD, CAP)
    s.hgT_low = parts("hgT_low", 33792, KD, CAP)
    s.hid_high = parts("hid_high", 35840, 4, CAP)
    s.hid_low = parts("hid_low", 36864, 4, CAP)
    s.hid_whole = [view(38400 + 256 * i, CAP) for i in range(2)]
    s.y_rows = [view(38912 + 1024 * i, D) for i in range(3)]
    s.further_gate = view(41472, 4, P)
    s.further_idx = view(41984, 1).bitcast(U32)
    s.g2_row = view(12288, 2, D)
    s.y_hi = [view(14336 + D * i, D) for i in range(2)]
    s.y_lo = [view(16384 + D * i, D) for i in range(2)]
    s.big_a = view(37876, NT * DN_W)
    s.big_b = view(37876 + NT * DN_W, NT * DN_W)


def stage_modulation(nc, s, d):
    sem = s.sem
    loaded, exp_done = sem("small_loaded"), sem("cond_exp_done")
    ada_in = [sem(f"ada_in{i}") for i in range(4)]
    silu_done, rows_done, copied = sem("silu_done"), sem("mod_rows_done"), sem("mod_rows_copied")
    stored, turned, chain = sem("mod_rows_stored"), sem("mod_turned"), sem("mod_chain")
    w_ada = d["w_ada"][0].rearrange("(k p) n -> p k n", p=P)
    NB = 6 * D // 512
    with nc.Block() as block:
        @block.sync
        def _(sp):
            sp.dma_start(s.cst, d["consts"]).then_inc(loaded, 16)
            with nc.allow_non_contiguous_dma(reason="small vectors onto partitions"):
                sp.dma_start(s.cond[:, :, 0], d["c_ctx"].rearrange("(k p) -> p k", p=P)).then_inc(loaded, 16)
                sp.dma_start(s.cond[:, :, 1], d["c"][0].rearrange("(k p) -> p k", p=P)).then_inc(loaded, 16)
                sp.dma_start(s.gain1, d["norm1_g"][0].rearrange("(k p) -> p k", p=P)).then_inc(loaded, 16)
                for h in range(2):
                    rows = slice(h * HEAD, (h + 1) * HEAD)
                    sp.dma_start(s.qgain[rows, :], d["q_norm_g"].rearrange("a b -> b a")).then_inc(loaded, 16)
                    sp.dma_start(s.kgain[rows, :], d["k_norm_g"].rearrange("a b -> b a")).then_inc(loaded, 16)
                sp.dma_start(s.pscale, d["pool_scale"][0].rearrange("(k p) -> p k", p=P)).then_inc(loaded, 16)
            for i in range(2):
                sp.dma_start(s.b_ada[i:i + 1, :], d["b_ada"]).then_inc(loaded, 16)
            for n in range(NB):
                if n >= 4:
                    sp.wait_ge(rows_done, n - 3)
                sp.dma_start(s.ada_ring[n % 4], w_ada[:, :, n * 512:(n + 1) * 512]).then_inc(ada_in[n % 4], 16)
            sp.dma_start(d["rpb_rows"].rearrange("r (n w) -> r n w", w=RPB_W),
                         d["rpb"][0].rearrange("h r w -> (h r) w").unsqueeze(1).to_broadcast([NA_H * 15, RPB_REP, RPB_W])).then_inc(stored, 16)
            sp.wait_ge(copied, NB)
            sp.dma_start(d["mod_rows"], s.mod[0:2, :]).then_inc(stored, 16)
            sp.wait_ge(stored, 32)

        @block.scalar
        def _(act):
            act.wait_ge(loaded, 16 * 11)
            nc.scalar.activation(s.silu, s.cond, ACT.Silu).then_inc(silu_done, 1)

        @block.vector
        def _(dve):
            nc.vector.memset(s.epsc, EPS)
            for n in range(NB):
                dve.wait_ge(rows_done, n + 1)
                if n == 0:
                    dve.wait_ge(loaded, 16 * 11)
                cols = slice(n * 512, (n + 1) * 512)
                nc.vector.tensor_tensor(s.mod[0:2, cols], s.bank[n % 2][0:2, :], s.b_ada[0:2, cols],
                                        ALU.add).then_inc(copied, 1)
            nc.vector.tensor_scalar(s.qgain, s.qgain, HEAD ** -0.5, None, ALU.mult)
            dve.wait_ge(turned, 1)
            tr = s.bank[2][:, 0:32].rearrange("p (v k c) -> p v k c", v=2, k=KD)
            nc.vector.tensor_copy(s.mod_b1, tr[:, 0])
            for c in range(2):
                nc.vector.scalar_tensor_tensor(s.mod_a1[:, :, c], tr[:, 1, :, c], 1.0, s.gain1, ALU.add, ALU.mult)

        @block.tensor
        def _(pe):
            pe.wait_ge(silu_done, 1)
            for n in range(NB):
                pe.wait_ge(ada_in[n % 4], 16 * (n // 4 + 1))
                if n >= 2:
                    pe.wait_ge(copied, n - 1)
                for k in range(KD):
                    mm = nc.tensor.matmul(s.bank[n % 2][0:2, :], s.silu[:, k, :], s.ada_ring[n % 4][:, k, :],
                                          start=(k == 0), stop=(k == KD - 1))
                mm.then_inc(rows_done, 1)
            pe.wait_ge(copied, NB)
            for v in range(2):
                for k in range(KD):
                    at = (v * KD + k) * 2
                    tr = nc.tensor.transpose(s.bank[2][:, at:at + 2], s.mod[0:2, v * D + k * P:v * D + (k + 1) * P],
                                             s.ident[0:2, 0:2])
            tr.then_inc(turned, 1)


def stage_norm1(nc, s, d):
    sem = s.sem
    x_in = [sem(f"x_in{i}") for i in range(NT)]
    squared, std_done, rstd_done = sem("n1_squared"), sem("n1_std_done"), sem("n1_rstd_done")
    xn_ready, turned, act_out, dve_out = sem("xn_ready"), sem("xn_turned"), sem("n1_act_out"), sem("n1_dve_out")

    def place(t):
        return [s.bank[2 * (t % 2)], s.bank[2 * (t % 2) + 1]]

    with nc.Block() as block:
        @block.sync
        def _(sp):
            for t in range(NT):
                src = d["x_prompt"][0] if t == 0 else d["x_sample"][0, (t - 1) * P:t * P, :]
                sp.dma_start(s.x_all[:, t, :], src).then_inc(x_in[t], 16)

        @block.scalar
        def _(act):
            for t in range(NT):
                act.wait_ge(x_in[t], 16)
                nc.scalar.activation(s.junk, s.x_all[:, t, :], ACT.Square, accum_out=s.ss[:, t:t + 1]).then_inc(squared, 1)
                act.wait_ge(squared, t + 1)
            nc.scalar.activation(s.rstd, s.ss, ACT.Sqrt, bias=s.epsc, scale=1.0 / D).then_inc(std_done, 1)
            for t in range(NT):
                act.wait_ge(turned, t + 1)
                c = 0 if t == 0 else 1
                for k in range(KD // 2):
                    ps = place(t)[k // 4][:, (k % 4) * P:(k % 4 + 1) * P]
                    nc.scalar.activation(s.hT[:, k, t * P:(t + 1) * P], ps, ACT.Identity, bias=s.mod_b1[:, k, c:c + 1],
                                         scale=s.mod_a1[:, k, c:c + 1]).then_inc(act_out, 1)

        @block.vector
        def _(dve):
            dve.wait_ge(std_done, 1)
            nc.vector.reciprocal(s.rstd, s.rstd).then_inc(rstd_done, 1)
            dve.wait_ge(rstd_done, 1)

            def scale_rows(t):
                if t >= 3:
                    dve.wait_ge(turned, t - 2)
                nc.vector.tensor_scalar(s.xn_ring[t % 3], s.x_all[:, t, :], s.rstd[:, t:t + 1], None,
                                        ALU.mult).then_inc(xn_ready, 1)

            scale_rows(0)
            scale_rows(1)
            for t in range(NT):
                if t + 2 < NT:
                    scale_rows(t + 2)
                dve.wait_ge(turned, t + 1)
                c = 0 if t == 0 else 1
                for k in range(KD // 2, KD):
                    ps = place(t)[k // 4][:, (k % 4) * P:(k % 4 + 1) * P]
                    nc.vector.tensor_scalar(s.hT[:, k, t * P:(t + 1) * P], ps, s.mod_a1[:, k, c:c + 1],
                                            s.mod_b1[:, k, c:c + 1], ALU.mult, ALU.add).then_inc(dve_out, 1)

        @block.tensor
        def _(pe):
            for t in range(NT):
                pe.wait_ge(xn_ready, t + 1)
                if t >= 2:
                    pe.wait_ge(act_out, 4 * (t - 1))
                    pe.wait_ge(dve_out, 4 * (t - 1))
                for k in range(KD):
                    tr = nc.tensor.transpose(place(t)[k // 4][:, (k % 4) * P:(k % 4 + 1) * P],
                                             s.xn_ring[t % 3][:, k * P:(k + 1) * P], s.ident)
                tr.then_inc(turned, 1)


def stage_project(nc, s, d):
    sem = s.sem
    w_in_v = d["w_in"][0].rearrange("(k p) n -> p k n", p=P)
    groups = [(COL_POOL, POOL_W, "fm"), (COL_DN, 384, "fm"), (COL_DN + 384, 384, "fm"), (COL_Q, 512, "q"),
              (COL_K, 512, "k"), (COL_V, 512, "v"), (COL_Z, DN_W + 4 * DN_H, "zba")]
    w_loaded = [sem(f"w_in_loaded{i}") for i in range(2)]
    product, act_out, dve_out, padded, v_stored = sem("proj_product"), sem("proj_act_out"), sem("proj_dve_out"), sem("proj_padded"), s.out_sem["v_stored"]
    rows_zeroed = sem("rows_zeroed")
    tm_dst = {"q": s.q_tm, "k": s.k_tm, "v": s.v_tm, "zba": s.zba}

    units = []
    for g, (col, width, kind) in enumerate(groups):
        mine = []
        if kind == "fm":
            for c in range(width // P):
                if g == 0:
                    row, ctx_at, lat_at = s.pool_fm[:, c], POOL_CTX, POOL_LAT
                else:
                    row, ctx_at, lat_at = s.qkv_fm[:, (g - 1) * 3 + c], CONV_CTX, CONV_LAT
                mine.append((g, (c * P, P), (0, P), row[:, ctx_at:ctx_at + CTX]))
                for half in range(2):
                    mine.append((g, (c * P, P), (P + 512 * half, 512), row[:, lat_at + 512 * half:lat_at + 512 * (half + 1)]))
        else:
            for t in range(NT):
                mine.append((g, None, (t * P, P), tm_dst[kind][:, t, :]))
        units += mine
    last_of = {u[0]: i for i, u in enumerate(units)}
    widths = [w for _, w, _ in groups]

    def out_of(i):
        g, wc, (t0, n), _ = units[i]
        return s.bank[i % 4][:, 0:(n if wc else widths[g])]

    def w_view(g):
        return s.w_ring[g % 2][:, 0:KD * widths[g]].rearrange("p (k n) -> p k n", k=KD)

    with nc.Block() as block:
        @block.sync
        def _(sp):
            for g, (col, width, _) in enumerate(groups):
                if g >= 2:
                    sp.wait_ge(product, last_of[g - 2] + 1)
                sp.dma_start(w_view(g), w_in_v[:, :, col:col + width]).then_inc(w_loaded[g % 2], 16)
            last_v = last_of[5]
            sp.wait_ge(act_out, last_v // 2 + 1)
            sp.wait_ge(dve_out, last_v // 2 + 1)
            sp.dma_start(d["out_v"][0, 0].rearrange("h p d -> p h d"),
                         s.v_tm[:, 0, :].rearrange("p (h d) -> p h d", h=NA_H)).then_inc(v_stored, 16)
            sp.wait_ge(v_stored, 16)

        @block.gpsimd
        def _(pool):
            for at, n in ((0, POOL_PAD), (POOL_CTX + CTX, POOL_PAD), (POOL_LAT + LAT, POOL_PAD)):
                nc.gpsimd.memset(s.pool_fm[:, :, at:at + n], 0.0)
            for at, n in ((0, 1), (CONV_CTX + CTX, 3), (CONV_LAT + LAT, 2)):
                nc.gpsimd.memset(s.qkv_fm[:, :, at:at + n], 0.0)
            nc.gpsimd.memset(s.zero_rows, 0.0).then_inc(padded, 1)
            pool.wait_ge(padded, 1)
            for i in range(OVER):
                pool.dma_start(d["slot_rows"][(N_EXP * CAP) + i * P:(N_EXP * CAP) + (i + 1) * P, :], s.zero_rows).then_inc(rows_zeroed, 16)
            pool.wait_ge(rows_zeroed, 16 * OVER)

        @block.scalar
        def _(act):
            for i in range(0, len(units), 2):
                act.wait_ge(product, i + 1)
                nc.scalar.copy(units[i][3], out_of(i)).then_inc(act_out, 1)

        @block.vector
        def _(dve):
            for i in range(1, len(units), 2):
                dve.wait_ge(product, i + 1)
                nc.vector.tensor_copy(units[i][3], out_of(i)).then_inc(dve_out, 1)

        @block.tensor
        def _(pe):
            for i, (g, wc, (t0, n), _) in enumerate(units):
                if i == 0 or units[i - 1][0] != g:
                    pe.wait_ge(w_loaded[g % 2], 16 * (g // 2 + 1))
                if i >= 4:
                    pe.wait_ge(act_out if i % 2 == 0 else dve_out, (i - 4) // 2 + 1)
                w = w_view(g)
                for k in range(KD):
                    if wc:
                        mm = nc.tensor.matmul(out_of(i), w[:, k, wc[0]:wc[0] + wc[1]], s.hT[:, k, t0:t0 + n],
                                              start=(k == 0), stop=(k == KD - 1))
                    else:
                        mm = nc.tensor.matmul(out_of(i), s.hT[:, k, t0:t0 + n], w[:, k, :],
                                              start=(k == 0), stop=(k == KD - 1))
                mm.then_inc(product, 1)


def stage_heads(nc, s, d):
    sem = s.sem
    cache_in, gain_in = sem("cache_in"), sem("kgain_row_in")
    squared, summed, std_done, r_done = sem("qk_squared"), sem("qk_summed"), sem("qk_std_done"), sem("qk_r_done")
    scaled, turned, out = sem("qk_scaled"), sem("qk_turned"), sem("qk_out")
    kc_turned, kc_out, kn_done, kn_stored = sem("kc_turned"), sem("kc_out"), sem("kn_done"), s.out_sem["kn_stored"]
    tiles = [(t, w) for t in range(NT) for w in range(2)]
    tm = [s.q_tm, s.k_tm]

    with nc.Block() as block:
        @block.sync
        def _(sp):
            for i in range(2):
                rows = slice(i * P, (i + 1) * P)
                sp.dma_start(s.kc_tm[:, i, :].rearrange("p (h d) -> p h d", h=NA_H),
                             d["cache_na_k"][0, 0, :, rows, :].rearrange("h p d -> p h d")).then_inc(cache_in, 16)
                sp.dma_start(s.vc_tm[:, i, :].rearrange("p (h d) -> p h d", h=NA_H),
                             d["cache_na_v"][0, 0, :, rows, :].rearrange("h p d -> p h d")).then_inc(cache_in, 16)
            sp.dma_start(s.kgain_row, d["k_norm_g"].to_broadcast([P, HEAD])).then_inc(gain_in, 16)
            sp.wait_ge(kn_done, 1)
            sp.dma_start(d["out_k"][0, 0].rearrange("h p d -> p h d"),
                         s.kn_ctx.rearrange("p (h d) -> p h d", h=NA_H)).then_inc(kn_stored, 16)
            sp.wait_ge(kn_stored, 16)

        @block.scalar
        def _(act):
            for j, (t, w) in enumerate(tiles):
                if j >= 2:
                    act.wait_ge(summed, j - 1)
                nc.scalar.activation(s.sq_ring[j % 2], tm[w][:, t, :], ACT.Square).then_inc(squared, 1)
            act.wait_ge(summed, len(tiles))
            nc.scalar.activation(s.qk_r, s.qk_ss, ACT.Sqrt, bias=s.epsc, scale=1.0 / HEAD).then_inc(std_done, 1)
            for i in range(2):
                act.wait_ge(kc_turned, i + 1)
                nc.scalar.copy(s.kcT[:, :, i * P:(i + 1) * P], s.bank[4 + i].rearrange("p (a b) -> p a b", a=4)).then_inc(kc_out, 1)
            for j, (t, w) in enumerate(tiles):
                act.wait_ge(turned, j + 1)
                dst = (s.qT, s.kT)[w][:, :, t * P:(t + 1) * P]
                nc.scalar.activation(dst, s.bank[j % 4].rearrange("p (a b) -> p a b", a=4), ACT.Copy,
                                     scale=(s.qgain, s.kgain)[w]).then_inc(out, 1)

        @block.vector
        def _(dve):
            for j, (t, w) in enumerate(tiles):
                dve.wait_ge(squared, j + 1)
                nc.vector.tensor_reduce(s.qk_ss[:, j * NA_H:(j + 1) * NA_H],
                                        s.sq_ring[j % 2].rearrange("p (h d) -> p h d", h=NA_H), AX.X, ALU.add).then_inc(summed, 1)
            dve.wait_ge(std_done, 1)
            nc.vector.reciprocal(s.qk_r, s.qk_r).then_inc(r_done, 1)
            dve.wait_ge(r_done, 1)
            for j, (t, w) in enumerate(tiles):
                x = tm[w][:, t, :].rearrange("p (h d) -> p h d", h=NA_H)
                r = s.qk_r[:, j * NA_H:(j + 1) * NA_H].unsqueeze(2).to_broadcast([P, NA_H, HEAD])
                nc.vector.tensor_tensor(x, x, r, ALU.mult).then_inc(scaled, 1)
                if j == 1:
                    dve.wait_ge(scaled, 2)
                    dve.wait_ge(gain_in, 16)
                    nc.vector.tensor_tensor(s.kn_ctx.rearrange("p (h d) -> p h d", h=NA_H), x,
                                            s.kgain_row.unsqueeze(1).to_broadcast([P, NA_H, HEAD]), ALU.mult).then_inc(kn_done, 1)

        @block.tensor
        def _(pe):
            pe.wait_ge(cache_in, 64)
            for i in range(2):
                for hp in range(4):
                    tr = nc.tensor.transpose(s.bank[4 + i][:, hp * P:(hp + 1) * P], s.kc_tm[:, i, hp * P:(hp + 1) * P], s.ident)
                tr.then_inc(kc_turned, 1)
            for j, (t, w) in enumerate(tiles):
                pe.wait_ge(scaled, j + 1)
                if j >= 4:
                    pe.wait_ge(out, j - 3)
                for hp in range(4):
                    tr = nc.tensor.transpose(s.bank[j % 4][:, hp * P:(hp + 1) * P], tm[w][:, t, hp * P:(hp + 1) * P], s.ident)
                tr.then_inc(turned, 1)


def query_tiles():
    out = []
    rows, kh = LAT // GRID, 8
    for i in range(rows // 2):
        first = [min(max(r - kh // 2, 0), rows - kh) for r in (2 * i, 2 * i + 1)]
        n = first[1] + kh - first[0]
        out.append((1 + i, first[0], n, first[0] - 2 * i + 6))
    out.append((0, None, None, None))
    return out


def stage_attention(nc, s, d):
    sem = s.sem
    bias_in, bias_ready = [sem(f"bias_in{i}") for i in range(2)], sem("bias_ready")
    scored, biased, neg_max, weighted = sem("at_scored"), sem("at_biased"), sem("at_neg_max"), sem("at_weighted")
    turned, act_out, dve_out = sem("at_turned"), sem("at_act_out"), sem("at_dve_out")
    part_max = sem("at_part_max")
    inverse, normed, mixed, mixed_read, chain = [sem("at_" + n) for n in ("inverse", "normed", "mixed", "mixed_read", "chain")]
    tiles = query_tiles()
    units = [(h, q) for h in range(NA_H) for q in range(len(tiles))]
    U, Q = len(units), len(tiles)

    def local(q):
        return 0 if tiles[q][2] is None else tiles[q][2] * GRID

    def width(q):
        return P if tiles[q][2] is None else local(q) + PAST

    def blocks(q):
        t, r0, n, _ = tiles[q]
        if n is None:
            return [(0, P, 0, False)]
        full = [(b * P, min(P, local(q) - b * P), 1 + r0 // 2 + b, False) for b in range((n + 1) // 2)]
        return full + [(local(q) + b * P, P, b, True) for b in range(PAST // P)]

    def scores(u):
        return s.pair[u % 3]

    with nc.Block() as block:
        @block.sync
        def _(sp):
            for h in range(NA_H):
                if h >= 2:
                    sp.wait_ge(biased, Q * (h - 1))
                    sp.wait_ge(bias_ready, h - 1)
                for a in range(2):
                    src = bass.AP(tensor=d["rpb_rows"].tensor, offset=(h * 15 + 1 - a) * RPB_ROW + 15,
                                  ap=[[RPB_W - 1, GRID], [RPB_ROW, 14], [1, GRID]])
                    sp.dma_start(s.bias[h % 2][a * GRID:(a + 1) * GRID], src).then_inc(bias_in[h % 2], 16)

        @block.gpsimd
        def _(pool):
            for h in range(NA_H):
                b, m = s.bias[h % 2], s.bias_mid[h % 2]
                pool.wait_ge(bias_in[h % 2], 32 * (h // 2 + 1))
                nc.gpsimd.tensor_tensor(b, b, s.colmask.unsqueeze(1).to_broadcast([P, 14, GRID]), ALU.add).then_inc(chain, 1)
                pool.wait_ge(chain, 3 * h + 1)
                nc.gpsimd.tensor_copy(m, b[:, 2:11, :]).then_inc(chain, 1)
                pool.wait_ge(chain, 3 * h + 2)
                nc.gpsimd.memset(m[0:GRID, 8, :], NEG)
                nc.gpsimd.memset(m[GRID:P, 0, :], NEG).then_inc(chain, 1)
                pool.wait_ge(chain, 3 * h + 3)
                nc.gpsimd.nop().then_inc(bias_ready, 1)

        @block.scalar
        def _(act):
            def turned_out(u):
                h, q = units[u]
                n = min(len(blocks(q)), 4) * P
                act.wait_ge(turned, u + 1)
                if u >= 2:
                    act.wait_ge(mixed, u - 1)
                nc.scalar.copy(s.wT[u % 2][:, 0:n], s.pair[u % 3][:, 0:n]).then_inc(act_out, 1)

            def weigh(u):
                h, q = units[u]
                act.wait_ge(neg_max, u + 1)
                w = s.weights[u % 2][:, 0:width(q)]
                nc.scalar.activation(w, w, ACT.Exp, bias=s.at_nm[:, u % 4:u % 4 + 1],
                                     accum_out=s.at_sum[:, u % 4:u % 4 + 1]).then_inc(weighted, 1)

            def mixed_out(u):
                h, q = units[u]
                half, t = slice((h % 2) * HEAD, (h % 2 + 1) * HEAD), tiles[q][0]
                act.wait_ge(mixed, u + 1)
                nc.scalar.copy(s.o_naT[half, h // 2, t * P:(t + 1) * P], s.bank[6 + u % 2][half, 0:P]).then_inc(mixed_read, 1)

            weigh(0)
            weigh(1)
            for u in range(U):
                turned_out(u)
                if u + 2 < U:
                    weigh(u + 2)
                mixed_out(u)

        @block.vector
        def _(dve):
            def turned_out(u):
                h, q = units[u]
                n = (len(blocks(q)) - 4) * P
                dve.wait_ge(turned, u + 1)
                if u >= 2:
                    dve.wait_ge(mixed, u - 1)
                if n > 0:
                    nc.vector.tensor_copy(s.wT[u % 2][:, 512:512 + n], s.pair[u % 3][:, 512:512 + n]).then_inc(dve_out, 1)
                else:
                    dve.sem_inc(dve_out, 1)

            def biased_max(u):
                h, q = units[u]
                t, r0, n, m0 = tiles[q]
                dve.wait_ge(scored, u + 1)
                if u >= 2:
                    dve.wait_ge(turned, u - 1)
                if q == 0:
                    dve.wait_ge(bias_ready, h + 1)
                w, L = s.weights[u % 2], local(q)
                mx, nm = s.at_max[:, u % 4:u % 4 + 1], s.at_nm[:, u % 4:u % 4 + 1]
                if n is None:
                    nc.vector.tensor_scalar(w[:, 0:P], scores(u)[:, 0:P], 1.0, None, ALU.mult, ALU.max, accum_out=mx).then_inc(biased, 1)
                else:
                    bias = s.bias_mid[h % 2] if n == 9 else s.bias[h % 2][:, m0:m0 + n, :]
                    m1 = s.at_m1[:, u % 4:u % 4 + 1]
                    nc.vector.tensor_tensor_reduce(out=w[:, 0:L], in0=scores(u)[:, 0:L],
                                                   in1=bias.rearrange("p a b -> p (a b)"), scale=1.0, scalar=NEG,
                                                   op0=ALU.add, op1=ALU.max, accum_out=m1).then_inc(part_max, 1)
                    dve.wait_ge(part_max, h * (Q - 1) + q + 1)
                    nc.vector.tensor_scalar(w[:, L:L + PAST], scores(u)[:, L:L + PAST], 1.0, m1, ALU.mult, ALU.max,
                                            accum_out=mx).then_inc(biased, 1)
                dve.wait_ge(biased, u + 1)
                nc.vector.tensor_scalar(nm, mx, -1.0, None, ALU.mult).then_inc(neg_max, 1)

            def normalise(u):
                w = s.weights[u % 2][:, 0:width(units[u][1])]
                inv = s.at_inv[:, u % 4:u % 4 + 1]
                dve.wait_ge(weighted, u + 1)
                nc.vector.reciprocal(inv, s.at_sum[:, u % 4:u % 4 + 1]).then_inc(inverse, 1)
                dve.wait_ge(inverse, u + 1)
                nc.vector.tensor_scalar(w, w, inv, None, ALU.mult).then_inc(normed, 1)

            biased_max(0)
            biased_max(1)
            normalise(0)
            for u in range(U):
                turned_out(u)
                if u + 1 < U:
                    normalise(u + 1)
                if u + 2 < U:
                    biased_max(u + 2)

        @block.tensor
        def _(pe):
            def score(u):
                h, q = units[u]
                t, r0, n, _ = tiles[q]
                half, hp = slice((h % 2) * HEAD, (h % 2 + 1) * HEAD), h // 2
                if u >= 3:
                    pe.wait_ge(act_out, u - 2)
                    pe.wait_ge(dve_out, u - 2)
                qT = s.qT[half, hp, t * P:(t + 1) * P]
                out = scores(u)
                if n is None:
                    mm = nc.tensor.matmul(out[:, 0:P], qT, s.kT[half, hp, 0:CTX], start=True, stop=True)
                else:
                    L, k0 = local(q), CTX + r0 * GRID
                    nc.tensor.matmul(out[:, 0:512], qT, s.kT[half, hp, k0:k0 + 512], start=True, stop=True)
                    if L > 512:
                        nc.tensor.matmul(out[:, 512:L], qT, s.kT[half, hp, k0 + 512:k0 + L], start=True, stop=True)
                    mm = nc.tensor.matmul(out[:, L:L + PAST], qT, s.kcT[half, hp, :], start=True, stop=True)
                mm.then_inc(scored, 1)

            def turn(u):
                h, q = units[u]
                pe.wait_ge(normed, u + 1)
                for b, (col, n, _, _) in enumerate(blocks(q)):
                    tr = nc.tensor.transpose(s.pair[u % 3][0:n, b * P:(b + 1) * P], s.weights[u % 2][:, col:col + n], s.ident)
                tr.then_inc(turned, 1)

            def mix(u):
                h, q = units[u]
                half = slice((h % 2) * HEAD, (h % 2 + 1) * HEAD)
                pe.wait_ge(act_out, u + 1)
                pe.wait_ge(dve_out, u + 1)
                if u >= 2:
                    pe.wait_ge(mixed_read, u - 1)
                every = blocks(q)
                for b, (_, n, tile, cached) in enumerate(every):
                    v = (s.vc_tm if cached else s.v_tm)[0:n, tile, h * HEAD:(h + 1) * HEAD]
                    mm = nc.tensor.matmul(s.bank[6 + u % 2][half, 0:P], v, s.wT[u % 2][0:n, b * P:(b + 1) * P],
                                          start=(b == 0), stop=(b == len(every) - 1))
                mm.then_inc(mixed, 1)

            score(0)
            score(1)
            for u in range(U):
                turn(u)
                if u + 2 < U:
                    score(u + 2)
                mix(u)


def stage_dn_prepare(nc, s, d):
    sem = s.sem
    small_in, chain, conv_done, silu_done = sem("dn_small_in"), sem("dn_chain"), sem("conv_done"), sem("conv_silu_done")
    turned, act_out, dve_out = sem("dn_turned"), sem("dn_act_out"), sem("dn_dve_out")
    squared, summed, std_done, r_done = sem("dn_squared"), sem("dn_ssq"), sem("dn_std"), sem("dn_r")
    sig_done, pre_done, abs_done, exp_done, ln_done, g_done = [sem("dn_" + n) for n in ("sig", "pre", "abs", "exp", "ln", "g")]
    cum_done, ex_in, ex_done = sem("dn_cum"), sem("dn_ex_in"), sem("dn_ex")
    NJ = CONV_ROW - 3
    G2 = 2 * DN_H
    b_raw = s.zba[:, :, DN_W:DN_W + G2]
    a_raw = s.zba[:, :, DN_W + G2:DN_W + 2 * G2]

    def tile_col(t):
        return 0 if t == 0 else CONV_LAT - 1 + (t - 1) * P

    with nc.Block() as block:
        @block.sync
        def _(sp):
            with nc.allow_non_contiguous_dma(reason="conv taps onto partitions"):
                for k in range(4):
                    sp.dma_start(s.taps[:, :, k], d["dn_conv_w"][0, k].rearrange("(c p) -> p c", p=P)).then_inc(small_in, 16)
            sp.dma_start(s.a_log, d["dn_a_log"].rearrange("a b c -> a (b c)").to_broadcast([P, G2])).then_inc(small_in, 16)
            sp.dma_start(s.dt_bias, d["dn_dt_bias"].rearrange("a b c -> a (b c)").to_broadcast([P, G2])).then_inc(small_in, 16)

        @block.vector
        def _(dve):
            done = [0]

            def link(ins):
                done[0] += 1
                ins.then_inc(chain, 1)
                dve.wait_ge(chain, done[0])

            dve.wait_ge(small_in, 96)
            for c in range(6):
                u, out = s.qkv_fm[:, c], s.conv[:, c]
                link(nc.vector.tensor_scalar(out, u[:, 0:NJ], s.taps[:, c, 0:1], None, ALU.mult))
                for k in range(1, 4):
                    ins = nc.vector.scalar_tensor_tensor(out, u[:, k:k + NJ], s.taps[:, c, k:k + 1], out, ALU.mult, ALU.add)
                    if k < 3:
                        link(ins)
                    else:
                        ins.then_inc(conv_done, 1)
            link(nc.vector.tensor_tensor(s.a_in, a_raw, s.dt_bias.unsqueeze(1).to_broadcast([P, NT, G2]), ALU.add))
            link(nc.vector.tensor_scalar(s.a_abs, s.a_in, -1.0, None, ALU.mult))
            nc.vector.tensor_tensor(s.a_abs, s.a_abs, s.a_in, ALU.min).then_inc(abs_done, 1)
            dve.wait_ge(ln_done, 2)
            link(nc.vector.tensor_scalar(s.a_in, s.a_in, 0.0, None, ALU.max))
            link(nc.vector.tensor_tensor(s.a_in, s.a_in, s.a_abs, ALU.add))
            link(nc.vector.tensor_scalar(s.a_log, s.a_log, -1.0, None, ALU.mult))
            nc.vector.tensor_tensor(s.g, s.a_in, s.a_log.unsqueeze(1).to_broadcast([P, NT, G2]), ALU.mult).then_inc(g_done, 1)
            for t in range(NT):
                dve.wait_ge(turned, t + 1)
                nc.vector.tensor_copy(s.qkv_tm[:, t, 512:768], s.bank[2 * (t % 2) + 1][:, 0:256]).then_inc(dve_out, 1)
                dve.wait_ge(squared, t + 1)
                nc.vector.tensor_reduce(s.dn_ss[:, t, :], s.dn_sq[t % 2].rearrange("p (h d) -> p h d", h=8), AX.X,
                                        ALU.add).then_inc(summed, 1)
            dve.wait_ge(std_done, 1)
            nc.vector.reciprocal(s.dn_ss, s.dn_ss).then_inc(r_done, 1)
            dve.wait_ge(r_done, 1)
            nc.vector.tensor_scalar(s.dn_ss[:, :, 0:4], s.dn_ss[:, :, 0:4], HEAD ** -0.5, None, ALU.mult).then_inc(r_done, 1)
            dve.wait_ge(r_done, 2)
            for t in range(NT):
                qk = s.qkv_tm[:, t, 0:512].rearrange("p (h d) -> p h d", h=8)
                nc.vector.tensor_tensor(qk, qk, s.dn_ss[:, t, :].unsqueeze(2).to_broadcast([P, 8, HEAD]), ALU.mult)
            dve.wait_ge(cum_done, 1)
            ps = s.bank[4]
            for dd in range(2):
                nc.vector.tensor_copy(s.cum[:, :, dd * 4:dd * 4 + 4], ps[:, dd * 36:dd * 36 + 36].rearrange("p (t h) -> p t h", h=4)).then_inc(ex_in, 1)
            dve.wait_ge(ex_in, 2)
            nc.vector.tensor_tensor(s.g_rest, ps[:, 72:144].rearrange("p (t h) -> p t h", h=G2), s.cum, ALU.subtract).then_inc(ex_in, 1)
            dve.wait_ge(ex_done, 2)
            nc.vector.tensor_tensor(s.beta_eg, s.beta, s.beta_eg, ALU.mult)

        @block.scalar
        def _(act):
            for c in range(6):
                act.wait_ge(conv_done, c + 1)
                nc.scalar.activation(s.conv[:, c], s.conv[:, c], ACT.Silu).then_inc(silu_done, 1)
            nc.scalar.activation(s.beta, b_raw, ACT.Sigmoid).then_inc(sig_done, 1)
            act.wait_ge(abs_done, 1)
            nc.scalar.activation(s.a_abs, s.a_abs, ACT.Exp).then_inc(exp_done, 1)
            nc.scalar.activation(s.a_log, s.a_log, ACT.Exp).then_inc(ln_done, 1)
            act.wait_ge(exp_done, 1)
            nc.scalar.activation(s.a_abs, s.a_abs, ACT.Ln, bias=1.0).then_inc(ln_done, 1)
            for t in range(NT):
                act.wait_ge(turned, t + 1)
                nc.scalar.copy(s.qkv_tm[:, t, 0:512], s.bank[2 * (t % 2)]).then_inc(act_out, 1)
                act.wait_ge(act_out, t + 1)
                if t >= 2:
                    act.wait_ge(summed, t - 1)
                nc.scalar.activation(s.dn_sq[t % 2], s.qkv_tm[:, t, 0:512], ACT.Square).then_inc(squared, 1)
            act.wait_ge(summed, NT)
            nc.scalar.activation(s.dn_ss, s.dn_ss, ACT.Sqrt, bias=s.epsc).then_inc(std_done, 1)
            act.wait_ge(ex_in, 3)
            nc.scalar.activation(s.beta_eg, s.cum, ACT.Exp).then_inc(ex_done, 1)
            nc.scalar.activation(s.g_rest, s.g_rest, ACT.Exp).then_inc(ex_done, 1)

        @block.tensor
        def _(pe):
            for t in range(NT):
                if t == 0:
                    pe.wait_ge(silu_done, 6)
                if t >= 2:
                    pe.wait_ge(act_out, t - 1)
                    pe.wait_ge(dve_out, t - 1)
                for c in range(6):
                    bank = s.bank[2 * (t % 2) + c // 4]
                    tr = nc.tensor.transpose(bank[:, (c % 4) * P:(c % 4 + 1) * P], s.conv[:, c, tile_col(t):tile_col(t) + P], s.ident)
                tr.then_inc(turned, 1)
            pe.wait_ge(g_done, 1)
            nc.tensor.matmul(s.bank[4][:, 0:36], s.tri_f, s.g[:, :, 0:4], start=True, stop=True)
            nc.tensor.matmul(s.bank[4][:, 36:72], s.tri_b, s.g[:, :, 4:8], start=True, stop=True)
            nc.tensor.matmul(s.bank[4][:, 72:144], s.block, s.g, start=True, stop=True).then_inc(cum_done, 1)


def stage_dn_scan(nc, s, d):
    sem = s.sem
    both = lambda name: [sem(f"{name}_{x}") for x in "fb"]
    state_in, state_out, start = sem("state_in"), s.out_sem["state_out"], sem("dn_start")
    kb_ready, kv_ready, turned, cast, kbt = both("kb_ready"), both("kv_ready"), both("sc_turned"), both("qk_cast"), both("kbt")
    spread, diff, decay, gram, gram_out = both("spread"), both("diff"), both("decay"), both("gram"), both("gram_out")
    inv_ready, y_done, y_ready, dxz = both("inv_ready"), both("y_done"), both("y_ready"), both("dxz")
    wu_done, wu_ready, qd_ready = both("wu_done"), both("wu_ready"), both("qd_ready")
    ws_done, v_ready, step_done, s_ready, o_ready = both("ws_done"), both("v_ready"), both("step_done"), both("s_ready"), both("o_ready")
    chain = sem("scan_chain")
    tile_of = lambda n, r: 0 if n == 0 else (n if r == 0 else NT - n)
    dirs = (0, 1)
    level = (s.level_f, s.level_b)
    strict = (s.strict_f, s.strict_b)
    tri = (s.tri_f, s.tri_b)
    W = 4 * P

    def heads(v, n=P):
        return v.rearrange("p (h a) -> p h a", h=4)

    def over_heads(m):
        return m.unsqueeze(1).to_broadcast([P, 4, P])

    def chunk_order(r):
        return (0, 1) if r == 0 else (1, 0)

    def end_col(r, c):
        return c * HEAD + (HEAD - 1 if r == 0 else 0)

    with nc.Block() as block:
        @block.sync
        def _(sp):
            for r in dirs:
                sp.dma_start(s.S_lat[0:HEAD, r], d["state_dn"][0, 0, r].rearrange("h k v -> k h v")).then_inc(state_in, 16)
            for r in dirs:
                sp.wait_ge(s_ready[r], 2)
                sp.dma_start(d["out_state"][0, 0, r].rearrange("h k v -> k h v"), s.S_ctx[0:HEAD, r]).then_inc(state_out, 16)
            sp.wait_ge(state_out, 32)

        @block.gpsimd
        def _(pool):
            for n in range(NT):
                for r in dirs:
                    t = tile_of(n, r)
                    if n >= 1:
                        pool.wait_ge(turned[r], n)
                    k = heads(s.qkv_tm[:, t, 256:512])
                    v = heads(s.qkv_tm[:, t, 512:768])
                    col = lambda x: x[:, t, r * 4:r * 4 + 4].unsqueeze(2).to_broadcast([P, 4, HEAD])
                    nc.gpsimd.tensor_tensor(heads(s.kb[r]), k, col(s.beta), ALU.mult).then_inc(kb_ready[r], 1)
                    if n >= 1:
                        pool.wait_ge(step_done[r], 2 * n)
                    nc.gpsimd.tensor_tensor(heads(s.vb[r]), v, col(s.beta), ALU.mult)
                    nc.gpsimd.tensor_tensor(heads(s.kg[r]), k, col(s.beta_eg), ALU.mult)
                    nc.gpsimd.tensor_tensor(heads(s.kd[r]), k, col(s.g_rest), ALU.mult).then_inc(kv_ready[r], 1)

        @block.scalar
        def _(act):
            for n in range(NT):
                for r in dirs:
                    b = s.bank[4 * r:4 * r + 4]
                    act.wait_ge(turned[r], n + 1)
                    if n >= 1:
                        act.wait_ge(qd_ready[r], n)
                    nc.scalar.copy(s.sqT[r], b[0][0:HEAD, :]).then_inc(cast[r], 1)
                    nc.scalar.copy(s.skT[r], b[1][0:HEAD, :]).then_inc(cast[r], 1)
                for r in dirs:
                    b = s.bank[4 * r:4 * r + 4]
                    act.wait_ge(diff[r], n + 1)
                    nc.scalar.activation(s.dec[r], s.pos[r], ACT.Exp, scale=-1.0)
                    nc.scalar.activation(s.decT[r], s.neg[r], ACT.Exp).then_inc(decay[r], 1)
                    if n >= 1:
                        act.wait_ge(s_ready[r], 2 * n)
                    nc.scalar.activation(s.eb[r], b[3], ACT.Exp).then_inc(decay[r], 1)
                for r in dirs:
                    b = s.bank[4 * r:4 * r + 4]
                    act.wait_ge(wu_done[r], n + 1)
                    nc.scalar.copy(s.swT[r], b[0][0:HEAD, :])
                    nc.scalar.copy(s.su[r], b[1][:, 0:4 * HEAD]).then_inc(wu_ready[r], 1)

        @block.vector
        def _(dve):
            done = [0]

            def link(ins):
                done[0] += 1
                ins.then_inc(chain, 1)
                dve.wait_ge(chain, done[0])

            nc.vector.memset(s.o_dn, 0.0)
            nc.vector.memset(s.S_ctx, 0.0).then_inc(start, 1)
            dve.wait_ge(start, 1)
            for n in range(NT):
                for r in dirs:
                    t, b = tile_of(n, r), s.bank[4 * r:4 * r + 4]
                    dve.wait_ge(turned[r], n + 1)
                    nc.vector.tensor_copy(s.skbT[r], b[2][0:HEAD, :]).then_inc(kbt[r], 1)
                    dve.wait_ge(spread[r], n + 1)
                    gc = s.cum[:, t, r * 4:r * 4 + 4].unsqueeze(2).to_broadcast([P, 4, P])
                    link(nc.vector.tensor_tensor(heads(s.pos[r]), heads(b[3]), gc, ALU.subtract))
                    link(nc.vector.tensor_scalar(s.neg[r], s.pos[r], 0.0, None, ALU.min))
                    nc.vector.tensor_scalar(s.pos[r], s.pos[r], 0.0, None, ALU.max).then_inc(diff[r], 1)
                for r in dirs:
                    b = s.bank[4 * r:4 * r + 4]
                    dve.wait_ge(decay[r], 2 * n + 1)
                    dve.wait_ge(gram[r], n + 1)
                    link(nc.vector.tensor_tensor(heads(s.dec[r]), heads(s.dec[r]), over_heads(strict[r]), ALU.mult))
                    link(nc.vector.tensor_tensor(s.L[r], b[0], s.dec[r], ALU.mult))
                    link(nc.vector.tensor_tensor(heads(s.dec[r]), heads(s.decT[r]), over_heads(strict[1 - r]), ALU.mult))
                    link(nc.vector.tensor_tensor(s.LT[r], b[1], s.dec[r], ALU.mult))
                    link(nc.vector.tensor_tensor(heads(s.decT[r]), heads(s.decT[r]), over_heads(tri[r]), ALU.mult))
                    nc.vector.tensor_tensor(s.attT[r], b[2], s.decT[r], ALU.mult)
                    link(nc.vector.tensor_tensor(heads(s.X[r]), heads(s.L[r]), over_heads(level[r][:, 0, :]), ALU.mult))
                    link(nc.vector.tensor_tensor(heads(s.Z[r]), heads(s.LT[r]), over_heads(level[1 - r][:, 0, :]), ALU.mult))
                    nc.vector.scalar_tensor_tensor(heads(s.X[r]), heads(s.X[r]), -1.0, over_heads(s.ident), ALU.mult, ALU.add)
                    nc.vector.scalar_tensor_tensor(heads(s.Z[r]), heads(s.Z[r]), -1.0, over_heads(s.ident), ALU.mult, ALU.add).then_inc(inv_ready[r], 1)
                    dve.wait_ge(decay[r], 2 * n + 2)
                    if n >= 1:
                        dve.wait_ge(step_done[r], 2 * n)
                    nc.vector.tensor_tensor(s.sqd[r], s.sqT[r], s.eb[r][0:HEAD, :], ALU.mult).then_inc(qd_ready[r], 1)
                for m in range(1, 6):
                    for r in dirs:
                        b = s.bank[4 * r:4 * r + 4]
                        dve.wait_ge(y_done[r], 5 * n + m)
                        nc.vector.tensor_tensor(heads(s.Y[r]), heads(b[0]), over_heads(level[r][:, m, :]), ALU.mult).then_inc(y_ready[r], 1)
                    for r in dirs:
                        b = s.bank[4 * r:4 * r + 4]
                        dve.wait_ge(dxz[r], 5 * n + m)
                        if m < 5:
                            nc.vector.tensor_tensor(s.X[r], s.X[r], b[1], ALU.subtract)
                        nc.vector.tensor_tensor(s.Z[r], s.Z[r], b[2], ALU.subtract).then_inc(inv_ready[r], 1)
                for r in dirs:
                    if n == 1 and r == 0:
                        dve.wait_ge(state_in, 32)
                for j in range(2):
                    for r in dirs:
                        c = chunk_order(r)[j]
                        rows, b = slice(c * HEAD, (c + 1) * HEAD), s.bank[4 * r:4 * r + 4]
                        S = (s.S_ctx if n == 0 else s.S_lat)[0:HEAD, r]
                        if j == 0:
                            dve.wait_ge(wu_ready[r], n + 1)
                        dve.wait_ge(ws_done[r], 2 * n + j + 1)
                        nc.vector.tensor_tensor(s.vn[r][rows], s.su[r][rows], b[0][rows, 0:4 * HEAD], ALU.subtract).then_inc(v_ready[r], 1)
                    for r in dirs:
                        t = tile_of(n, r)
                        c = chunk_order(r)[j]
                        rows, b = slice(c * HEAD, (c + 1) * HEAD), s.bank[4 * r:4 * r + 4]
                        S = (s.S_ctx if n == 0 else s.S_lat)[0:HEAD, r]
                        gl = heads(s.eb[r])[0:HEAD, :, end_col(r, c)].unsqueeze(2).to_broadcast([HEAD, 4, HEAD])
                        dve.wait_ge(step_done[r], 2 * n + j + 1)
                        link(nc.vector.tensor_tensor(S, S, gl, ALU.mult))
                        nc.vector.tensor_tensor(S, S, b[3][0:HEAD, 0:4 * HEAD].rearrange("p (h v) -> p h v", h=4), ALU.add).then_inc(s_ready[r], 1)
                        o = s.o_dn[rows, t, :]
                        link(nc.vector.tensor_tensor(o, o, b[2][rows, 0:4 * HEAD], ALU.add))
                        nc.vector.tensor_tensor(o, o, b[1][rows, 0:4 * HEAD], ALU.add).then_inc(o_ready[r], 1)
                        dve.wait_ge(o_ready[r], 2 * n + j + 1)

        @block.tensor
        def _(pe):
            for n in range(NT):
                for r in dirs:
                    t, b = tile_of(n, r), s.bank[4 * r:4 * r + 4]
                    pe.wait_ge(kb_ready[r], n + 1)
                    if n == 0 and r == 0:
                        pe.wait_ge(start, 1)
                    if n >= 1:
                        pe.wait_ge(o_ready[r], 2 * n)
                        pe.wait_ge(s_ready[r], 2 * n)
                    for h in range(4):
                        cols = slice(h * P, (h + 1) * P)
                        nc.tensor.transpose(b[0][0:HEAD, cols], s.qkv_tm[:, t, h * HEAD:(h + 1) * HEAD], s.ident)
                        nc.tensor.transpose(b[1][0:HEAD, cols], s.qkv_tm[:, t, 256 + h * HEAD:256 + (h + 1) * HEAD], s.ident)
                        tr = nc.tensor.transpose(b[2][0:HEAD, cols], s.kb[r][:, h * HEAD:(h + 1) * HEAD], s.ident)
                    tr.then_inc(turned[r], 1)
                    for h in range(4):
                        g = s.g[:, t, r * 4 + h:r * 4 + h + 1].to_broadcast([P, P])
                        mm = nc.tensor.matmul(b[3][:, h * P:(h + 1) * P], g, tri[r], start=True, stop=True)
                    mm.then_inc(spread[r], 1)
                for r in dirs:
                    b = s.bank[4 * r:4 * r + 4]
                    pe.wait_ge(cast[r], 2 * n + 2)
                    pe.wait_ge(kbt[r], n + 1)
                    for h in range(4):
                        cols = slice(h * P, (h + 1) * P)
                        nc.tensor.matmul(b[0][:, cols], s.skbT[r][0:HEAD, cols], s.skT[r][0:HEAD, cols], start=True, stop=True)
                        nc.tensor.matmul(b[1][:, cols], s.skT[r][0:HEAD, cols], s.skbT[r][0:HEAD, cols], start=True, stop=True)
                        mm = nc.tensor.matmul(b[2][:, cols], s.skT[r][0:HEAD, cols], s.sqT[r][0:HEAD, cols], start=True, stop=True)
                    mm.then_inc(gram[r], 1)
                for m in range(1, 6):
                    for r in dirs:
                        b = s.bank[4 * r:4 * r + 4]
                        pe.wait_ge(inv_ready[r], 6 * n + m)
                        for h in range(4):
                            cols = slice(h * P, (h + 1) * P)
                            mm = nc.tensor.matmul(b[0][:, cols], s.LT[r][:, cols], s.X[r][:, cols], start=True, stop=True)
                        mm.then_inc(y_done[r], 1)
                    for r in dirs:
                        b = s.bank[4 * r:4 * r + 4]
                        pe.wait_ge(y_ready[r], 5 * n + m)
                        for h in range(4):
                            cols = slice(h * P, (h + 1) * P)
                            if m < 5:
                                nc.tensor.matmul(b[1][:, cols], s.Z[r][:, cols], s.Y[r][:, cols], start=True, stop=True)
                            mm = nc.tensor.matmul(b[2][:, cols], s.Y[r][:, cols], s.Z[r][:, cols], start=True, stop=True)
                        mm.then_inc(dxz[r], 1)
                for r in dirs:
                    b = s.bank[4 * r:4 * r + 4]
                    pe.wait_ge(kv_ready[r], n + 1)
                    pe.wait_ge(inv_ready[r], 6 * n + 6)
                    for h in range(4):
                        cols, hd = slice(h * P, (h + 1) * P), slice(h * HEAD, (h + 1) * HEAD)
                        nc.tensor.matmul(b[0][0:HEAD, cols], s.kg[r][:, hd], s.Z[r][:, cols], start=True, stop=True)
                        mm = nc.tensor.matmul(b[1][:, hd], s.Z[r][:, cols], s.vb[r][:, hd], start=True, stop=True)
                    mm.then_inc(wu_done[r], 1)
                for j in range(2):
                    for r in dirs:
                        c = chunk_order(r)[j]
                        rows, b = slice(c * HEAD, (c + 1) * HEAD), s.bank[4 * r:4 * r + 4]
                        S = (s.S_ctx if n == 0 else s.S_lat)[0:HEAD, r]
                        if j == 0:
                            pe.wait_ge(wu_ready[r], n + 1)
                        if n == 1 and j == 0:
                            pe.wait_ge(state_in, 32)
                        pe.wait_ge(s_ready[r], 2 * n + j) if 2 * n + j else None
                        for h in range(4):
                            hd = slice(h * HEAD, (h + 1) * HEAD)
                            mm = nc.tensor.matmul(b[0][rows, hd], heads(s.swT[r])[0:HEAD, h, rows], S[:, h, :], start=True, stop=True)
                        mm.then_inc(ws_done[r], 1)
                    for r in dirs:
                        c = chunk_order(r)[j]
                        rows, b = slice(c * HEAD, (c + 1) * HEAD), s.bank[4 * r:4 * r + 4]
                        S = (s.S_ctx if n == 0 else s.S_lat)[0:HEAD, r]
                        pe.wait_ge(v_ready[r], 2 * n + j + 1)
                        if j == 0:
                            pe.wait_ge(qd_ready[r], n + 1)
                        else:
                            pe.wait_ge(o_ready[r], 2 * n + 1)
                        for h in range(4):
                            hd = slice(h * HEAD, (h + 1) * HEAD)
                            nc.tensor.matmul(b[2][rows, hd], heads(s.sqd[r])[0:HEAD, h, rows], S[:, h, :], start=True, stop=True)
                            nc.tensor.matmul(b[1][rows, hd], heads(s.attT[r])[rows, h, rows], s.vn[r][rows, hd], start=True, stop=True)
                            mm = nc.tensor.matmul(b[3][0:HEAD, hd], s.kd[r][rows, hd], s.vn[r][rows, hd], start=True, stop=True)
                        mm.then_inc(step_done[r], 1)


def stage_dn_finish(nc, s, d):
    sem = s.sem
    gain_in, squared, summed, std_done, chain, z_done = [sem("fin_" + n) for n in ("gain", "sq", "sum", "std", "chain", "z")]
    o4 = s.o_dn.rearrange("p t (h d) -> p (t h) d", h=DN_H)
    sq4 = s.big_a.rearrange("p (t d) -> p t d", d=HEAD)
    with nc.Block() as block:
        @block.sync
        def _(sp):
            sp.dma_start(s.dn_gain, d["dn_norm_g"].to_broadcast([P, HEAD])).then_inc(gain_in, 16)

        @block.scalar
        def _(act):
            nc.scalar.activation(s.big_a, s.o_dn.rearrange("p t c -> p (t c)"), ACT.Square).then_inc(squared, 1)
            nc.scalar.activation(s.big_b.rearrange("p (t c) -> p t c", t=NT), s.zba[:, :, 0:DN_W], ACT.Silu).then_inc(z_done, 1)
            act.wait_ge(summed, 1)
            nc.scalar.activation(s.fin_r, s.fin_r, ACT.Sqrt, bias=s.epsc, scale=1.0 / HEAD).then_inc(std_done, 1)

        @block.vector
        def _(dve):
            dve.wait_ge(squared, 1)
            nc.vector.tensor_reduce(s.fin_r, sq4, AX.X, ALU.add).then_inc(summed, 1)
            dve.wait_ge(std_done, 1)
            nc.vector.reciprocal(s.fin_r, s.fin_r).then_inc(chain, 1)
            dve.wait_ge(chain, 1)
            nc.vector.tensor_tensor(o4, o4, s.fin_r.unsqueeze(2).to_broadcast([P, NT * DN_H, HEAD]), ALU.mult).then_inc(chain, 1)
            dve.wait_ge(chain, 2)
            dve.wait_ge(gain_in, 16)
            nc.vector.tensor_tensor(o4, o4, s.dn_gain.unsqueeze(1).to_broadcast([P, NT * DN_H, HEAD]), ALU.mult).then_inc(chain, 1)
            dve.wait_ge(chain, 3)
            dve.wait_ge(z_done, 1)
            o = s.o_dn.rearrange("p t c -> p (t c)")
            nc.vector.tensor_tensor(o, o, s.big_b, ALU.mult)


def stage_pool(nc, s, d):
    sem = s.sem
    counts_in, wp_in, chain, pooled, mapped, out = [sem("pool_" + n) for n in ("counts", "w", "chain", "done", "mapped", "out")]
    A, B, R = s.pool_a, s.pool_b, POOL_ROW
    lo, hi = slice(0, HEAD), slice(HEAD, P)
    spans = [(POOL_CTX, 0, CTX), (POOL_LAT, CTX, 512), (POOL_LAT + 512, CTX + 512, 512)]
    units = [(c, sp_) for c in range(2) for sp_ in spans]
    groups = [(lo, 0, A), (hi, 0, B), (lo, 1, A), (hi, 1, B)]

    with nc.Block() as block:
        @block.sync
        def _(sp):
            sp.dma_start(s.pool_rc, d["pool_counts"]).then_inc(counts_in, 16)
            for g in range(4):
                sp.dma_start(s.w_pool[HEAD * (g % 2):HEAD * (g % 2 + 1), g // 2, :], d["w_pool"][0, g]).then_inc(wp_in, 16)

        @block.vector
        def _(dve):
            done = [0]

            def link(ins):
                done[0] += 1
                ins.then_inc(chain, 1)
                dve.wait_ge(chain, done[0])

            u = s.pool_fm
            add = lambda out_, a, b: link(nc.vector.tensor_tensor(out_, a, b, ALU.add))
            add(A[:, :, 1:R], u[:, :, 0:R - 1], u[:, :, 1:R])
            add(B[:, 0, 2:R - 1], A[:, 0, 1:R - 2], A[:, 0, 3:R])
            add(B[:, 1, 2:R - 1], A[:, 1, 1:R - 2], A[:, 1, 3:R])
            add(A[:, 1, 4:R - 3], B[:, 1, 2:R - 5], B[:, 1, 6:R - 1])
            add(B[hi, 1, 8:R - 7], A[hi, 1, 4:R - 11], A[hi, 1, 12:R - 3])
            dve.wait_ge(counts_in, 16)
            body = slice(POOL_CTX, POOL_LAT + LAT)
            for rows, c, buf in groups:
                link(nc.vector.tensor_tensor(buf[rows, c, body], buf[rows, c, body], s.pool_rc[rows, c, body], ALU.mult))
                ins = nc.vector.tensor_tensor(s.pooled[rows, c, body], buf[rows, c, body], u[rows, c, body], ALU.subtract)
            ins.then_inc(pooled, 1)

        @block.tensor
        def _(pe):
            pe.wait_ge(pooled, 1)
            pe.wait_ge(wp_in, 64)
            for i, (c, (at, _, n)) in enumerate(units):
                for half in range(2):
                    rows = slice(half * HEAD, (half + 1) * HEAD)
                    mm = nc.tensor.matmul(s.bank[i][rows, 0:n], s.w_pool[rows, c, :], s.pooled[rows, c, at:at + n], start=True, stop=True)
                mm.then_inc(mapped, 1)

        @block.scalar
        def _(act):
            for i, (c, (_, t0, n)) in enumerate(units):
                act.wait_ge(mapped, i + 1)
                nc.scalar.activation(s.o_poolT[:, c, t0:t0 + n], s.bank[i][:, 0:n], ACT.Copy, scale=s.pscale[:, c:c + 1])


def stage_turn_mix(nc, s, d):
    sem = s.sem
    turned, out = sem("mix_turned"), sem("mix_out")
    with nc.Block() as block:
        @block.tensor
        def _(pe):
            for t in range(NT):
                if t >= 4:
                    pe.wait_ge(out, t - 3)
                for c in range(2):
                    tr = nc.tensor.transpose(s.bank[t % 4][:, c * P:(c + 1) * P], s.o_dn[:, t, c * P:(c + 1) * P], s.ident)
                tr.then_inc(turned, 1)

        @block.vector
        def _(dve):
            for t in range(NT):
                dve.wait_ge(turned, t + 1)
                nc.vector.tensor_copy(s.o_dnT[:, :, t * P:(t + 1) * P],
                                      s.bank[t % 4][:, 0:256].rearrange("p (a b) -> p a b", a=2)).then_inc(out, 1)


def stage_output(nc, s, d):
    sem = s.sem
    w_in, g_in, x_in = sem("w_out_in"), sem("g1_in"), [sem(f"xr_in{i}") for i in range(2)]
    product, gated, added = sem("out_product"), sem("out_gated"), sem("out_added")
    mix = [s.o_poolT[:, c] for c in range(2)] + [s.o_naT[:, c] for c in range(4)] + [s.o_dnT[:, c] for c in range(2)]
    with nc.Block() as block:
        @block.sync
        def _(sp):
            wv = d["w_out"][0].rearrange("(k p) n -> p k n", p=P)
            for half in range(2):
                sp.dma_start(s.w_out[:, :, half * 512:(half + 1) * 512], wv[:, :, half * 512:(half + 1) * 512]).then_inc(w_in, 16)
            for c in range(2):
                sp.dma_start(s.g1_row[:, c, :], d["mod_rows"][c:c + 1, 2 * D:3 * D].to_broadcast([P, D])).then_inc(g_in, 16)
            for t in range(NT):
                if t >= 2:
                    sp.wait_ge(added, t - 1)
                src = d["x_prompt"][0] if t == 0 else d["x_sample"][0, (t - 1) * P:t * P, :]
                sp.dma_start(s.xr_ring[t % 2], src).then_inc(x_in[t % 2], 16)

        @block.tensor
        def _(pe):
            pe.wait_ge(w_in, 32)
            for t in range(NT):
                if t >= 4:
                    pe.wait_ge(gated, t - 3)
                for half in range(2):
                    for k in range(KD):
                        mm = nc.tensor.matmul(s.bank[2 * (t % 4) + half], mix[k][:, t * P:(t + 1) * P],
                                              s.w_out[:, k, half * 512:(half + 1) * 512], start=(k == 0), stop=(k == KD - 1))
                mm.then_inc(product, 1)

        @block.vector
        def _(dve):
            dve.wait_ge(g_in, 32)
            for t in range(NT):
                dve.wait_ge(product, t + 1)
                nc.vector.tensor_tensor(s.x1[:, t, :], s.pair[t % 4], s.g1_row[:, min(t, 1), :], ALU.mult).then_inc(gated, 1)
                dve.wait_ge(gated, t + 1)
                dve.wait_ge(x_in[t % 2], 16 * (t // 2 + 1))
                nc.vector.tensor_tensor(s.x1[:, t, :], s.x1[:, t, :], s.xr_ring[t % 2], ALU.add).then_inc(added, 1)


def stage_norm2(nc, s, d):
    sem = s.sem
    rows_in, squared, std_done, rstd_done, chain = [sem("n2_" + n) for n in ("in", "sq", "std", "rstd", "chain")]
    a_done, h_half, h_ready, h_stored = sem("n2_a"), sem("n2_half"), sem("h2_ready"), [sem(f"h2_stored{i}") for i in range(3)]
    turned, act_out, dve_out, zeroed = sem("h2_turned"), sem("h2_act_out"), sem("h2_dve_out"), sem("slots_zeroed")
    zero_set = sem("zero_set")
    logits_done = sem("logits_done")
    with nc.Block() as block:
        @block.sync
        def _(sp):
            for c in range(2):
                sp.dma_start(s.b2_row[:, c, :], d["mod_rows"][c:c + 1, 3 * D:4 * D].to_broadcast([P, D])).then_inc(rows_in, 16)
                sp.dma_start(s.a2_row[:, c, :], d["mod_rows"][c:c + 1, 4 * D:5 * D].to_broadcast([P, D])).then_inc(rows_in, 16)
            sp.dma_start(s.n2_row, d["norm2_g"].to_broadcast([P, D])).then_inc(rows_in, 16)
            sp.dma_start(s.w_router, d["w_router"].rearrange("(k p) e -> p k e", p=P)).then_inc(rows_in, 16)
            for j in range(UNIT_X):
                load_unit(sp, s, d, j)
            sp.wait_ge(zero_set, 1)
            sp.dma_start(d["slot_token"].rearrange("(p a) b -> p (a b)", p=P), s.zero_slots).then_inc(zeroed, 16)
            for t in range(NT):
                sp.wait_ge(h_ready, t + 1)
                sp.dma_start(d["h2_rows"][t * P:(t + 1) * P, :], s.h2_ring[t % 3]).then_inc(h_stored[t % 3], 16)
            for i in range(3):
                sp.wait_ge(h_stored[i], 16 * NT // 3)
            sp.wait_ge(zeroed, 16)

        @block.scalar
        def _(act):
            for t in range(NT):
                nc.scalar.activation(s.junk2, s.x1[:, t, :], ACT.Square, accum_out=s.ss[:, t:t + 1]).then_inc(squared, 1)
                act.wait_ge(squared, t + 1)
            nc.scalar.activation(s.rstd, s.ss, ACT.Sqrt, bias=s.epsc, scale=1.0 / D).then_inc(std_done, 1)
            for t in range(NT):
                act.wait_ge(turned, t + 1)
                nc.scalar.copy(s.h2T[:, 0:4, t * P:(t + 1) * P], s.bank[2 * (t % 2)].rearrange("p (a b) -> p a b", a=4)).then_inc(act_out, 1)

        @block.vector
        def _(dve):
            nc.vector.memset(s.zero_slots, 0).then_inc(zero_set, 1)
            dve.wait_ge(rows_in, 96)
            for c in range(2):
                nc.vector.scalar_tensor_tensor(s.a2_row[:, c, :], s.a2_row[:, c, :], 1.0, s.n2_row, ALU.add, ALU.mult).then_inc(a_done, 1)
            dve.wait_ge(a_done, 2)
            dve.wait_ge(std_done, 1)
            nc.vector.reciprocal(s.rstd, s.rstd).then_inc(rstd_done, 1)
            dve.wait_ge(rstd_done, 1)

            def make(t):
                if t >= 3:
                    dve.wait_ge(h_stored[t % 3], 16 * (t // 3))
                    dve.wait_ge(turned, t - 2)
                c = min(t, 1)
                nc.vector.scalar_tensor_tensor(s.h2_ring[t % 3], s.x1[:, t, :], s.rstd[:, t:t + 1], s.a2_row[:, c, :],
                                               ALU.mult, ALU.mult).then_inc(h_half, 1)
                dve.wait_ge(h_half, t + 1)
                nc.vector.tensor_tensor(s.h2_ring[t % 3], s.h2_ring[t % 3], s.b2_row[:, c, :], ALU.add).then_inc(h_ready, 1)

            make(0)
            for t in range(NT):
                if t + 1 < NT:
                    make(t + 1)
                dve.wait_ge(turned, t + 1)
                nc.vector.tensor_copy(s.h2T[:, 4:8, t * P:(t + 1) * P],
                                      s.bank[2 * (t % 2) + 1].rearrange("p (a b) -> p a b", a=4)).then_inc(dve_out, 1)

        @block.tensor
        def _(pe):
            for t in range(NT):
                pe.wait_ge(h_ready, t + 1)
                if t >= 2:
                    pe.wait_ge(act_out, t - 1)
                    pe.wait_ge(dve_out, t - 1)
                for k in range(KD):
                    tr = nc.tensor.transpose(s.bank[2 * (t % 2) + k // 4][:, (k % 4) * P:(k % 4 + 1) * P],
                                             s.h2_ring[t % 3][:, k * P:(k + 1) * P], s.ident)
                tr.then_inc(turned, 1)
            pe.wait_ge(act_out, NT)
            pe.wait_ge(dve_out, NT)
            pe.wait_ge(rows_in, 96)
            for t in range(NT):
                for k in range(KD):
                    mm = nc.tensor.matmul(s.bank[4][:, t * N_EXP:(t + 1) * N_EXP], s.h2T[:, k, t * P:(t + 1) * P],
                                          s.w_router[:, k, :], start=(k == 0), stop=(k == KD - 1))
            mm.then_inc(logits_done, 1)


def stage_route(nc, s, d):
    sem = s.sem
    b_in, sig_done, chain, mask_ready, counted = [sem("rt_" + n) for n in ("bias", "sig", "chain", "mask", "counted")]
    slots_ready, scattered, read_back = sem("slots_ready"), sem("slots_scattered"), sem("slots_read")
    R = s.route
    with nc.Block() as block:
        @block.sync
        def _(sp):
            sp.dma_start(s.b_router, d["b_router"].rearrange("(a e) -> a e", a=1).to_broadcast([P, N_EXP])).then_inc(b_in, 16)
            sp.wait_ge(scattered, 16 * 2 * NT)
            with nc.allow_non_contiguous_dma(reason="one token number per slot"):
                sp.dma_start(s.slot_idx, d["slot_token"].rearrange("(a p) b -> p (a b)", p=P)).then_inc(read_back, 16)
            sp.wait_ge(read_back, 16)

        @block.scalar
        def _(act):
            nc.scalar.activation(R["score"], s.bank[4][:, 0:NT * N_EXP], ACT.Sigmoid).then_inc(sig_done, 1)

        @block.gpsimd
        def _(pool):
            pool.wait_ge(slots_ready, 1)
            for t in range(NT):
                for which in (s.slot_hi, s.slot_lo):
                    nc.gpsimd.indirect_dma_start(out=d["slot_token"], out_offset=bass.IndirectOffsetOnAxis(ap=which[:, t:t + 1], axis=0),
                                                 in_=s.token_id[:, t:t + 1], in_offset=None).then_inc(scattered, 16)
            pool.wait_ge(scattered, 16 * 2 * NT)

        @block.tensor
        def _(pe):
            pe.wait_ge(mask_ready, 1)
            nc.tensor.matmul(s.bank[5][:, 0:NT * N_EXP], s.before, R["mask"], start=True, stop=True)
            nc.tensor.matmul(s.bank[6][:, 0:NT * N_EXP], s.ones, R["mask"], start=True, stop=True).then_inc(counted, 1)

        @block.vector
        def _(dve):
            done = [0]

            def link(ins):
                done[0] += 1
                ins.then_inc(chain, 1)
                dve.wait_ge(chain, done[0])

            def tt(out, a, b, op):
                link(nc.vector.tensor_tensor(out, a, b, op))

            def rank4(rank, x, tmp):
                link(nc.vector.memset(rank, 0.0))
                n = x.shape[1]
                for j in range(4):
                    if j > 0:
                        tt(tmp[:, :, 0:j], x[:, :, 0:j], x[:, :, j:j + 1].to_broadcast([P, n, j]), ALU.is_lt)
                        tt(rank[:, :, 0:j], rank[:, :, 0:j], tmp[:, :, 0:j], ALU.add)
                    if j < 3:
                        tt(tmp[:, :, j + 1:4], x[:, :, j + 1:4], x[:, :, j:j + 1].to_broadcast([P, n, 3 - j]), ALU.is_le)
                        tt(rank[:, :, j + 1:4], rank[:, :, j + 1:4], tmp[:, :, j + 1:4], ALU.add)

            g4 = lambda v: v.rearrange("p (n e) -> p n e", e=4)
            t16 = lambda v: v.rearrange("p (t e) -> p t e", e=N_EXP)
            dve.wait_ge(b_in, 16)
            dve.wait_ge(sig_done, 1)
            tt(t16(R["sel"]), t16(R["score"]), s.b_router.unsqueeze(1).to_broadcast([P, NT, N_EXP]), ALU.add)
            rank4(g4(R["rank"]), g4(R["sel"]), g4(R["tmp"]))
            link(nc.vector.tensor_scalar(R["mask"], R["rank"], 1.5, None, ALU.is_lt))
            tt(R["tmp"], R["sel"], R["mask"], ALU.mult)
            link(nc.vector.tensor_reduce(R["gsum"], g4(R["tmp"]), AX.X, ALU.add))
            rank4(g4(R["grank"]), g4(R["gsum"]), g4(R["gtmp"]))
            link(nc.vector.tensor_scalar(R["gmask"], R["grank"], 0.5, None, ALU.is_lt))
            link(nc.vector.tensor_tensor(g4(R["mask"]), g4(R["mask"]), R["gmask"].unsqueeze(2).to_broadcast([P, 36, 4]), ALU.mult))
            nc.vector.nop().then_inc(mask_ready, 1)
            tt(R["weight"], R["score"], R["mask"], ALU.mult)
            link(nc.vector.tensor_reduce(R["wsum"], t16(R["weight"]), AX.X, ALU.add))
            link(nc.vector.reciprocal(R["wsum"], R["wsum"]))
            tt(t16(R["weight"]), t16(R["weight"]), R["wsum"].unsqueeze(2).to_broadcast([P, NT, N_EXP]), ALU.mult)
            dve.wait_ge(counted, 1)
            count = t16(s.bank[6][:, 0:NT * N_EXP])
            off = t16(R["off"])
            link(nc.vector.memset(off[:, 0, :], 0.0))
            for t in range(1, NT):
                tt(off[:, t, :], off[:, t - 1, :], count[:, t - 1, :], ALU.add)
            tt(R["total"], off[:, NT - 1, :], count[:, NT - 1, :], ALU.add)
            tt(R["slot"], R["off"], s.bank[5][:, 0:NT * N_EXP], ALU.add)
            link(nc.vector.memset(R["over"], 0.0))
            for k in range((N_TOK - CAP + P - 1) // P):
                link(nc.vector.tensor_scalar(R["o16"], R["total"], CAP + k * P + 0.5, None, ALU.is_gt))
                tt(R["over"], R["over"], R["o16"], ALU.add)
            link(nc.vector.tensor_tensor_scan(R["cum"], s.ones[:, 0:N_EXP], R["over"], 0.0, ALU.mult, ALU.add))
            tt(R["o16"], R["cum"], R["over"], ALU.subtract)
            link(nc.vector.tensor_scalar(R["o16"], R["o16"], float(P), float((N_EXP - 1) * CAP), ALU.mult, ALU.add))
            tt(R["o16"], R["o16"], s.grid16, ALU.subtract)
            link(nc.vector.tensor_scalar(R["tmp"], R["slot"], CAP - 0.5, None, ALU.is_gt))
            tt(t16(R["tmp"]), t16(R["tmp"]), R["o16"].unsqueeze(1).to_broadcast([P, NT, N_EXP]), ALU.mult)
            tt(R["slot"], R["slot"], R["tmp"], ALU.add)
            tt(t16(R["slot"]), t16(R["slot"]), s.grid16.unsqueeze(1).to_broadcast([P, NT, N_EXP]), ALU.add)
            tt(R["slot"], R["slot"], R["mask"], ALU.mult)
            link(nc.vector.tensor_reduce(R["hi"], t16(R["slot"]), AX.X, ALU.max))
            link(nc.vector.tensor_reduce(R["lo"], t16(R["slot"]), AX.X, ALU.add))
            tt(R["lo"], R["lo"], R["hi"], ALU.subtract)
            link(nc.vector.tensor_copy(s.slot_hi, R["hi"]))
            link(nc.vector.tensor_copy(s.slot_lo, R["lo"]))
            link(nc.vector.tensor_copy(s.token_id, s.token))
            nc.vector.nop().then_inc(slots_ready, 1)
            tt(t16(R["tmp"]), t16(R["slot"]), R["hi"].unsqueeze(2).to_broadcast([P, NT, N_EXP]), ALU.is_equal)
            tt(R["rank"], R["weight"], R["tmp"], ALU.mult)
            link(nc.vector.tensor_reduce(s.w_hi, t16(R["rank"]), AX.X, ALU.add))
            tt(R["rank"], R["weight"], R["rank"], ALU.subtract)
            link(nc.vector.tensor_reduce(s.w_lo, t16(R["rank"]), AX.X, ALU.add))
            ex = R["rank"][:, 0:OVER].rearrange("p (a b) -> p a b", b=1)
            wide = s.over_cmp
            link(nc.vector.tensor_tensor(wide, R["cum"].unsqueeze(1).to_broadcast([P, OVER, N_EXP]),
                                         s.over_id.unsqueeze(2).to_broadcast([P, OVER, N_EXP]), ALU.is_le))
            link(nc.vector.tensor_reduce(R["tmp"][:, 0:OVER], wide, AX.X, ALU.add))
            link(nc.vector.tensor_scalar(R["tmp"][:, 0:OVER], R["tmp"][:, 0:OVER], float(N_EXP - 1), None, ALU.min))
            nc.vector.tensor_copy(s.over_table[:, 0:OVER], R["tmp"][:, 0:OVER])
            nc.vector.tensor_copy(s.over_table[:, OVER:OVER + 1], R["cum"][:, N_EXP - 1:N_EXP])


def unit_source(d, j):
    e, half = j // UNITS, (j % UNITS) // 2 % 2
    kind = ("w_gate", "w_up", "w_gate", "w_up", "w_down", "w_down")[j % UNITS]
    if kind == "w_down":
        half = j % 2
    src = d[kind][0, e].rearrange("(k p) n -> p k n", p=P)
    k = src.shape[1] // 2
    return src[:, half * k:(half + 1) * k, :]


def load_unit(sp, s, d, j):
    src = unit_source(d, j)
    sp.dma_start(s.unit_x[j % UNIT_X].rearrange("p (k n) -> p k n", n=src.shape[2]), src).then_inc(s.unit_in[j % UNIT_X], 16)


def stage_experts(nc, s, d):
    sem = s.sem
    high_done, low_done, first_half = sem("unit_high"), sem("unit_low"), sem("first_half")
    gathered, turned, rows_high, rows_low = sem("gathered"), sem("hg_turned"), sem("rows_high"), sem("rows_low")
    gate_up, silu_done, hid_done = sem("gate_up"), sem("hid_silu"), sem("hid_done")
    hid_high, hid_low, down_done = sem("hid_high"), sem("hid_low"), sem("down_done")
    y_act, y_dve, y_stored = sem("y_act"), sem("y_dve"), [sem(f"y_stored{i}") for i in range(3)]
    FB, KH = FF // P, KD // 2
    N_UNITS = UNITS * N_EXP

    def high(j, n):
        return s.unit_high[j % UNIT_H].rearrange("p (k n) -> p k n", n=n)

    def low(j, n):
        return s.unit_low[j % UNIT_X].rearrange("p (k n) -> p k n", n=n)

    def multiplied(eng, j):
        e, k = j // UNITS, j % UNITS
        if k < 2:
            eng.wait_ge(first_half, e + 1)
        elif k < 4:
            eng.wait_ge(gate_up, FB * (e + 1))
        else:
            eng.wait_ge(down_done, 2 * (e + 1))

    with nc.Block() as block:
        @block.sync
        def _(sp):
            for j in range(UNIT_X, N_UNITS):
                multiplied(sp, j - UNIT_X)
                load_unit(sp, s, d, j)

        @block.gpsimd
        def _(pool):
            for e in range(N_EXP):
                if e >= 1:
                    pool.wait_ge(turned, 2 * e)
                for i in range(2):
                    nc.gpsimd.indirect_dma_start(out=s.hg_rows[:, i, :], out_offset=None, in_=d["h2_rows"],
                                                 in_offset=bass.IndirectOffsetOnAxis(ap=s.slot_idx[:, 2 * e + i:2 * e + i + 1], axis=0)
                                                 ).then_inc(gathered, 16)

        @block.scalar
        def _(act):
            def split(j):
                if j >= N_UNITS:
                    return
                act.wait_ge(s.unit_in[j % UNIT_X], 16 * (j // UNIT_X + 1))
                if j >= UNIT_H:
                    multiplied(act, j - UNIT_H)
                nc.scalar.copy(s.unit_high[j % UNIT_H], s.unit_x[j % UNIT_X]).then_inc(high_done, 1)

            def turned_out(e):
                for i in range(2):
                    act.wait_ge(turned, 2 * e + i + 1)
                    for b in range(2):
                        nc.scalar.copy(s.hgT_high[:, 4 * b:4 * b + 4, i * P:(i + 1) * P],
                                       s.bank[2 * i + b].rearrange("p (a b) -> p a b", a=4)).then_inc(rows_high, 1)

            def hid_split(u):
                act.wait_ge(hid_done, u + 1)
                nc.scalar.copy(s.hid_high[:, u % FB, :], s.hid_whole[u % 2]).then_inc(hid_high, 1)

            split(0)
            split(1)
            turned_out(0)
            for e in range(N_EXP):
                for j in range(2, UNITS):
                    split(UNITS * e + j)
                for f in range(FB):
                    u = FB * e + f
                    act.wait_ge(gate_up, u + 1)
                    if u >= 2:
                        act.wait_ge(hid_done, u - 1)
                    nc.scalar.activation(s.sg[u % 2], s.bank[4 + f][:, 0:CAP], ACT.Silu).then_inc(silu_done, 1)
                    if f >= 1:
                        hid_split(u - 1)
                hid_split(FB * e + FB - 1)
                if e + 1 < N_EXP:
                    turned_out(e + 1)
                split(UNITS * (e + 1))
                split(UNITS * (e + 1) + 1)
                for i in range(2):
                    v = 2 * e + i
                    act.wait_ge(down_done, v + 1)
                    if v >= 3:
                        act.wait_ge(y_stored[v % 3], 16 * (v // 3))
                    nc.scalar.copy(s.y_rows[v % 3][:, 0:512], s.bank[2 * i]).then_inc(y_act, 1)
                    act.wait_ge(y_act, v + 1)
                    act.wait_ge(y_dve, v + 1)
                    act.dma_start(d["slot_rows"][v * P:(v + 1) * P, :], s.y_rows[v % 3]).then_inc(y_stored[v % 3], 16)
            for i in range(3):
                act.wait_ge(y_stored[i], 16 * len(range(i, 2 * N_EXP, 3)))

        @block.vector
        def _(dve):
            def split(j):
                if j >= N_UNITS:
                    return
                dve.wait_ge(high_done, j + 1)
                nc.vector.tensor_tensor(s.unit_low[j % UNIT_X], s.unit_x[j % UNIT_X], s.unit_high[j % UNIT_H].bitcast(F32), ALU.subtract).then_inc(low_done, 1)

            def turned_out(e):
                for i in range(2):
                    for b in range(2):
                        dve.wait_ge(rows_high, 4 * e + 2 * i + b + 1)
                        cols = slice(i * P, (i + 1) * P)
                        nc.vector.tensor_tensor(s.hgT_low[:, 4 * b:4 * b + 4, cols], s.bank[2 * i + b].rearrange("p (a b) -> p a b", a=4),
                                                s.hgT_high[:, 4 * b:4 * b + 4, cols].bitcast(F32), ALU.subtract).then_inc(rows_low, 1)

            def hid_split(u):
                dve.wait_ge(hid_high, u + 1)
                nc.vector.tensor_tensor(s.hid_low[:, u % FB, :], s.hid_whole[u % 2], s.hid_high[:, u % FB, :].bitcast(F32),
                                        ALU.subtract).then_inc(hid_low, 1)

            split(0)
            split(1)
            turned_out(0)
            for e in range(N_EXP):
                for j in range(2, UNITS):
                    split(UNITS * e + j)
                for f in range(FB):
                    u = FB * e + f
                    dve.wait_ge(silu_done, u + 1)
                    if u >= 2:
                        dve.wait_ge(hid_low, u - 1)
                    nc.vector.tensor_tensor(s.hid_whole[u % 2], s.sg[u % 2], s.bank[4 + f][:, CAP:2 * CAP], ALU.mult).then_inc(hid_done, 1)
                    if f >= 1:
                        hid_split(u - 1)
                hid_split(FB * e + FB - 1)
                if e + 1 < N_EXP:
                    turned_out(e + 1)
                split(UNITS * (e + 1))
                split(UNITS * (e + 1) + 1)
                for i in range(2):
                    v = 2 * e + i
                    dve.wait_ge(down_done, v + 1)
                    if v >= 3:
                        dve.wait_ge(y_stored[v % 3], 16 * (v // 3))
                    nc.vector.tensor_copy(s.y_rows[v % 3][:, 512:1024], s.bank[2 * i + 1]).then_inc(y_dve, 1)

        @block.tensor
        def _(pe):
            def three(out, w, x, first, last):
                nc.tensor.matmul(out, w[0], x[0], start=first, stop=False)
                nc.tensor.matmul(out, w[0], x[1], start=False, stop=False)
                return nc.tensor.matmul(out, w[1], x[0], start=False, stop=last)

            def turn(e):
                pe.wait_ge(gathered, 32 * (e + 1))
                for i in range(2):
                    if e >= 2:
                        pe.wait_ge(y_act, 2 * (e - 2) + i + 1)
                        pe.wait_ge(y_dve, 2 * (e - 2) + i + 1)
                    for k in range(KD):
                        tr = nc.tensor.transpose(s.bank[2 * i + k // 4][:, (k % 4) * P:(k % 4 + 1) * P],
                                                 s.hg_rows[:, i, k * P:(k + 1) * P], s.ident)
                    tr.then_inc(turned, 1)

            def gate_up_half(e, h):
                j = UNITS * e + 2 * h
                pe.wait_ge(low_done, j + 2)
                order = [(k, f) for k in range(KH) for f in range(FB)] if h == 0 else [(k, f) for f in range(FB) for k in range(KH)]
                for k, f in order:
                    for w in range(2):
                        cols = slice(f * P, (f + 1) * P)
                        kk = h * KH + k
                        mm = three(s.bank[4 + f][:, w * CAP:(w + 1) * CAP], (high(j + w, FF)[:, k, cols], low(j + w, FF)[:, k, cols]),
                                   (s.hgT_high[:, kk, :], s.hgT_low[:, kk, :]), (kk, w) == (0, 0), (kk, w) == (KD - 1, 1))
                    if h == 1 and k == KH - 1:
                        mm.then_inc(gate_up, 1)
                if h == 0:
                    mm.then_inc(first_half, 1)

            def down(e):
                j = UNITS * e + 4
                pe.wait_ge(low_done, j + 2)
                for i in range(2):
                    rows = slice(i * P, (i + 1) * P)
                    if e + 1 < N_EXP:
                        pe.wait_ge(rows_low, 4 * (e + 1) + 2 * (i + 1))
                    elif e >= 1:
                        pe.wait_ge(y_act, 2 * (e - 1) + i + 1)
                        pe.wait_ge(y_dve, 2 * (e - 1) + i + 1)
                    for f in range(FB):
                        if i == 0:
                            pe.wait_ge(hid_high, FB * e + f + 1)
                            pe.wait_ge(hid_low, FB * e + f + 1)
                        for half in range(2):
                            cols = slice(half * 512, (half + 1) * 512)
                            mm = three(s.bank[2 * i + half], (s.hid_high[:, f, rows], s.hid_low[:, f, rows]),
                                       (high(j + f // 2, D)[:, f % 2, cols], low(j + f // 2, D)[:, f % 2, cols]), f == 0, f == FB - 1)
                    mm.then_inc(down_done, 1)

            turn(0)
            for e in range(N_EXP):
                pe.wait_ge(rows_high, 4 * (e + 1))
                pe.wait_ge(rows_low, 4 * (e + 1))
                if e >= 1:
                    pe.wait_ge(hid_done, FB * e)
                gate_up_half(e, 0)
                gate_up_half(e, 1)
                if e + 1 < N_EXP:
                    turn(e + 1)
                down(e)


def stage_further(nc, s, d):
    n_over = nc.values_load(s.over_table[0:1, OVER:OVER + 1], min_val=0, max_val=OVER)
    first = N_EXP * CAP
    FB = FF // P
    Wv = [s.we_ring[j].rearrange("p (k n) -> p k n", n=(FF, FF, D)[j]) for j in range(3)]
    kinds = ("w_gate", "w_up", "w_down")
    sem = s.sem
    idx_in, w_in, rows_in, turned, out = sem("fu_idx"), sem("fu_w"), sem("fu_rows"), sem("fu_turned"), sem("fu_out")
    gate_up, silu_done, hid_ready, down, y_ready, stored = [sem("fu_" + n) for n in ("gate_up", "silu", "hid", "down", "y", "stored")]
    counted = [idx_in, w_in, turned, out, gate_up, silu_done, hid_ready, down, y_ready, stored]
    with nc.If(n_over > 0):
        with nc.Fori(0, OVER) as o:
            with nc.Block() as block:
                @block.sync
                def _(sp):
                    with nc.allow_non_contiguous_dma(reason="one token number per slot"):
                        sp.dma_start(s.further_idx, d["slot_token"][bass.ds(first + o * P, P), :]).then_inc(idx_in, 16)
                    e = sp.value_load(s.over_table[0:1, bass.ds(o, 1)], min_val=0, max_val=N_EXP - 1)
                    for j, kind in enumerate(kinds):
                        src = d[kind][0].rearrange("e (k p) n -> p (e k) n", p=P)
                        k = src.shape[1] // N_EXP
                        sp.dma_start(Wv[j], src[:, bass.ds(e * k, k), :]).then_inc(w_in, 16)
                    sp.wait_ge(y_ready, 4)
                    sp.dma_start(d["slot_rows"][bass.ds(first + o * P, P), :], s.y_ring[0]).then_inc(stored, 16)
                    sp.wait_ge(stored, 16)

                @block.gpsimd
                def _(pool):
                    pool.wait_ge(idx_in, 16)
                    nc.gpsimd.indirect_dma_start(out=s.hg[0][:, 0, :], out_offset=None, in_=d["h2_rows"],
                                                 in_offset=bass.IndirectOffsetOnAxis(ap=s.further_idx, axis=0)).then_inc(rows_in, 16)
                    pool.wait_ge(rows_in, o * 16 + 16)

                @block.tensor
                def _(pe):
                    pe.wait_ge(rows_in, o * 16 + 16)
                    for k in range(KD):
                        tr = nc.tensor.transpose(s.bank[k // 4][:, (k % 4) * P:(k % 4 + 1) * P], s.hg[0][:, 0, k * P:(k + 1) * P], s.ident)
                    tr.then_inc(turned, 1)
                    pe.wait_ge(out, 2)
                    pe.wait_ge(w_in, 48)
                    for f in range(FB):
                        for j in range(2):
                            for k in range(KD):
                                mm = nc.tensor.matmul(s.bank[2 + f][:, j * P:(j + 1) * P], Wv[j][:, k, f * P:(f + 1) * P],
                                                      s.hgT[0][:, k, 0:P], start=(k == 0), stop=(k == KD - 1))
                        mm.then_inc(gate_up, 1)
                    pe.wait_ge(hid_ready, FB)
                    for half in range(2):
                        for f in range(FB):
                            mm = nc.tensor.matmul(s.bank[6 + half], s.hid[0][:, f, 0:P], Wv[2][:, f, half * 512:(half + 1) * 512],
                                                  start=(f == 0), stop=(f == FB - 1))
                    mm.then_inc(down, 1)

                @block.scalar
                def _(act):
                    act.wait_ge(turned, 1)
                    for half in range(2):
                        nc.scalar.copy(s.hgT[0][:, 4 * half:4 * half + 4, 0:P], s.bank[half].rearrange("p (a b) -> p a b", a=4)).then_inc(out, 1)
                    for f in range(FB):
                        act.wait_ge(gate_up, f + 1)
                        nc.scalar.activation(s.further_gate[:, f, :], s.bank[2 + f][:, 0:P], ACT.Silu).then_inc(silu_done, 1)

                @block.vector
                def _(dve):
                    for f in range(FB):
                        dve.wait_ge(silu_done, f + 1)
                        nc.vector.tensor_tensor(s.hid[0][:, f, 0:P], s.further_gate[:, f, :], s.bank[2 + f][:, P:2 * P], ALU.mult).then_inc(hid_ready, 1)
                    dve.wait_ge(down, 1)
                    for half in range(2):
                        nc.vector.tensor_copy(s.y_ring[0][:, half * 512:(half + 1) * 512], s.bank[6 + half]).then_inc(y_ready, 2)
            for one in counted:
                nc.sync.sem_clear(one)
            nc.all_engine_barrier()
    nc.end_ifs()


def stage_combine(nc, s, d):
    sem = s.sem
    g_in, in_hi, in_lo = sem("g2_in"), [sem(f"y_hi{i}") for i in range(2)], [sem(f"y_lo{i}") for i in range(2)]
    chain, ready, stored = sem("cb_chain"), sem("y_ready"), s.out_sem["y_out"]
    with nc.Block() as block:
        @block.sync
        def _(sp):
            for c in range(2):
                sp.dma_start(s.g2_row[:, c, :], d["mod_rows"][c:c + 1, 5 * D:6 * D].to_broadcast([P, D])).then_inc(g_in, 16)
            for t in range(NT):
                sp.wait_ge(ready, t + 1)
                dst = d["out_y_prompt"][0] if t == 0 else d["out_y_sample"][0, (t - 1) * P:t * P, :]
                sp.dma_start(dst, s.x1[:, t, :]).then_inc(stored, 16)
            sp.wait_ge(stored, 16 * NT)

        @block.gpsimd
        def _(pool):
            for t in range(NT):
                if t >= 2:
                    pool.wait_ge(ready, t - 1)
                for buf, idx, got in ((s.y_hi, s.slot_hi, in_hi), (s.y_lo, s.slot_lo, in_lo)):
                    nc.gpsimd.indirect_dma_start(out=buf[t % 2], out_offset=None, in_=d["slot_rows"],
                                                 in_offset=bass.IndirectOffsetOnAxis(ap=idx[:, t:t + 1], axis=0)).then_inc(got[t % 2], 16)

        @block.vector
        def _(dve):
            done = [0]

            def link(ins):
                done[0] += 1
                ins.then_inc(chain, 1)
                dve.wait_ge(chain, done[0])

            dve.wait_ge(g_in, 32)
            for t in range(NT):
                a, b = s.y_hi[t % 2], s.y_lo[t % 2]
                dve.wait_ge(in_hi[t % 2], 16 * (t // 2 + 1))
                link(nc.vector.tensor_scalar(a, a, s.w_hi[:, t:t + 1], None, ALU.mult))
                dve.wait_ge(in_lo[t % 2], 16 * (t // 2 + 1))
                link(nc.vector.scalar_tensor_tensor(a, b, s.w_lo[:, t:t + 1], a, ALU.mult, ALU.add))
                link(nc.vector.tensor_tensor(a, a, s.g2_row[:, min(t, 1), :], ALU.mult))
                nc.vector.tensor_tensor(s.x1[:, t, :], s.x1[:, t, :], a, ALU.add).then_inc(ready, 1)


def constants():
    import numpy as np
    i = np.arange(P)
    same = (i[:, None] // HEAD) == (i[None, :] // HEAD)
    out = {
        "ident": np.eye(P),
        "tri_f": same & (i[:, None] <= i[None, :]),
        "tri_b": same & (i[:, None] >= i[None, :]),
        "block": same,
        "strict_f": same & (i[:, None] > i[None, :]),
        "strict_b": same & (i[:, None] < i[None, :]),
        "before": i[:, None] < i[None, :],
        "ones": np.ones((P, P)),
        "grid16": np.tile(np.arange(16) * CAP, (P, 1)),
        "over_id": np.tile(np.arange(OVER), (P, 1)),
        "token": np.arange(NT)[None, :] * P + i[:, None],
    }
    level = []
    for b in range(6):
        size = 1 << b
        bi, bj = i[:, None] // size, i[None, :] // size
        level.append((bi % 2 == 1) & (bj == bi - 1))
    out["level_f"] = np.concatenate(level, axis=1)
    out["level_b"] = np.concatenate([m.T for m in level], axis=1)
    q = (i % GRID)[:, None]
    k = np.arange(GRID)[None, :]
    start = np.clip(q - 8, 0, GRID - 16)
    out["colmask"] = np.where((k >= start) & (k < start + 16), 0.0, NEG)
    return np.concatenate([np.asarray(out[n], np.float32) for n in CST], axis=1)


def pool_counts():
    import numpy as np
    out = np.ones((P, 2, POOL_ROW), np.float32)
    for g, win in enumerate((2, 4, 8, 16)):
        for at, n in ((POOL_CTX, CTX), (POOL_LAT, LAT)):
            t = np.arange(n)
            count = np.clip(t + win - win // 2, 0, n) - np.clip(t - win // 2, 0, n)
            out[HEAD * (g % 2):HEAD * (g % 2 + 1), g // 2, at:at + n] = 1.0 / count
    return out


STAGES = [stage_modulation, stage_norm1, stage_project, stage_heads, stage_attention,
          stage_dn_prepare, stage_dn_scan, stage_dn_finish, stage_pool, stage_turn_mix, stage_output,
          stage_norm2, stage_route, stage_experts, stage_further, stage_combine]

IN_SHAPES = {
    "x_prompt": (1, CTX, D), "x_sample": (1, LAT, D), "cache_na_k": (1, 1, NA_H, PAST, HEAD),
    "cache_na_v": (1, 1, NA_H, PAST, HEAD), "state_dn": (1, 1, 2, DN_H, HEAD, HEAD), "c": (1, D), "c_ctx": (D,),
    "norm1_g": (1, D), "norm2_g": (1, D), "w_ada": (1, D, 6 * D), "b_ada": (1, 6 * D), "w_in": (1, D, IN_W),
    "w_out": (1, D, D), "w_pool": (1, 4, HEAD, HEAD), "pool_scale": (1, POOL_W), "q_norm_g": (1, HEAD),
    "k_norm_g": (1, HEAD), "dn_conv_w": (1, 4, 3 * DN_W), "dn_a_log": (1, 2, DN_H), "dn_dt_bias": (1, 2, DN_H),
    "dn_norm_g": (1, HEAD), "w_router": (D, N_EXP), "b_router": (N_EXP,), "w_gate": (1, N_EXP, D, FF),
    "w_up": (1, N_EXP, D, FF), "w_down": (1, N_EXP, FF, D),
}


def declare(nc, inputs):
    import numpy as np
    arrays, d = {}, {}
    own = {name: inputs[name] for name in IN_SHAPES}
    own["rpb"] = inputs["rpb"]
    own["consts"] = constants()
    own["pool_counts"] = pool_counts()
    for name, a in own.items():
        a = np.ascontiguousarray(a)
        arrays[f"in_{name}"] = a
        d[name] = nc.dram_tensor(f"in_{name}", a.shape, F32, kind="ExternalInput").ap()
    outs = [("out_y_prompt", (1, CTX, D)), ("out_y_sample", (1, LAT, D)), ("out_k", (1, 1, NA_H, CTX, HEAD)),
            ("out_v", (1, 1, NA_H, CTX, HEAD)), ("out_state", (1, 1, 2, DN_H, HEAD, HEAD))]
    for name, shape in outs:
        d[name] = nc.dram_tensor(name, shape, F32, kind="ExternalOutput").ap()
    d["rpb_rows"] = nc.dram_tensor("rpb_rows", (NA_H * 15, RPB_ROW), F32).ap()
    d["mod_rows"] = nc.dram_tensor("mod_rows", (2, 6 * D), F32).ap()
    d["h2_rows"] = nc.dram_tensor("h2_rows", (N_TOK, D), F32).ap()
    d["slot_token"] = nc.dram_tensor("slot_token", (SLOTS, 1), U32).ap()
    d["slot_rows"] = nc.dram_tensor("slot_rows", (SLOTS, D), F32).ap()
    s = Store()
    s.out_sem = {name: nc.alloc_semaphore(name) for name in ("v_stored", "kn_stored", "state_out", "y_out")}
    s.unit_in = [nc.alloc_semaphore(f"unit_in{i}") for i in range(UNIT_X)]
    s.WORDS = 53120
    views(nc, s)
    psum = nc.alloc_psum_tensor("psum", [P, 8 * 512], F32)
    s.bank = [psum[:, 512 * i:512 * (i + 1)] for i in range(8)]
    s.pair = [psum[:, 1024 * i:1024 * (i + 1)] for i in range(4)]
    return arrays, d, [n for n, _ in outs], s


def run_stage(nc, s, d, stage):
    held = []

    def sem(name):
        held.append(nc.alloc_semaphore(name))
        return held[-1]

    s.sem = sem
    stage(nc, s, d)
    nc.clear_and_free_semaphores(held)
    nc.all_engine_barrier()


def kernel(**inputs):
    import concourse.bacc as bacc
    from concourse.bass_utils import run_bass_kernel_spmd

    nc = bacc.Bacc("TRN2", target_bir_lowering=False, num_devices=1)
    arrays, d, outs, s = declare(nc, inputs)
    for stage in STAGES:
        run_stage(nc, s, d, stage)
    r = run_bass_kernel_spmd(nc, [arrays], core_ids=[0])
    return tuple(r.results[0][name] for name in outs)
```

```python
import concourse.bass as bass
from concourse import mybir

F32 = mybir.dt.float32
U32 = mybir.dt.uint32
F32R = mybir.dt.float32r
ALU = mybir.AluOpType
ACT = mybir.ActivationFunctionType
AX = mybir.AxisListType

P = 128
D = 1024
KD = D // P
CTX, LAT = 128, 1024
N_TOK = CTX + LAT
NT = N_TOK // P
POOL_W, NA_W, DN_W = 256, 512, 256
HEAD = 64
NA_H, DN_H = NA_W // HEAD, DN_W // HEAD
IN_W = POOL_W + 3 * NA_W + 3 * DN_W + DN_W + 4 * DN_H
PAST = 256
N_EXP, GRP, TOP = 16, 4, 2
FF = 512
EPS = 1e-6
NEG = -1e30
GRID = 64
RPB_W = 31
RPB_REP = 66
RPB_ROW = RPB_REP * RPB_W

POOL_PAD = 8
POOL_CTX = POOL_PAD
POOL_LAT = POOL_CTX + CTX + POOL_PAD
POOL_ROW = POOL_LAT + LAT + POOL_PAD
CONV_CTX = 1
CONV_LAT = CONV_CTX + CTX + 2 + 1
CONV_ROW = CONV_LAT + LAT + 2

CAP = 256
UNITS = 6
UNIT_X, UNIT_H = 7, 6
OVER = (2 * N_TOK - 2 * CAP) // P
SLOTS = N_EXP * CAP + OVER * P

COL_POOL = 0
COL_Q = COL_POOL + POOL_W
COL_K = COL_Q + NA_W
COL_V = COL_K + NA_W
COL_DN = COL_V + NA_W
COL_Z = COL_DN + 3 * DN_W

ADA_EARLY = 2 * D // 512
ADA_ALL = 6 * D // 512

CST = {}
_at = 0
for _name, _n in (("ident", P), ("tri_f", P), ("tri_b", P), ("block", P), ("strict_f", P), ("strict_b", P),
                  ("level_f", 6 * P), ("level_b", 6 * P), ("colmask", GRID), ("before", P), ("ones", P),
                  ("grid16", 16), ("token", NT), ("over_id", OVER)):
    CST[_name] = (_at, _n)
    _at += _n
CST_W = _at


class Store:
    pass


def views(nc, s):
    base = (nc.sbuf_base + 31) // 32 * 32
    arena = nc.alloc_sbuf_tensor("arena", [P, s.WORDS], F32)
    s.arena = arena

    def view(at, *shape):
        n = 1
        for x in shape:
            n *= x
        assert at + n <= s.WORDS, (at, n)
        v = arena[:, at:at + n]
        if len(shape) == 2:
            v = v.rearrange("p (a b) -> p a b", a=shape[0])
        elif len(shape) == 3:
            v = v.rearrange("p (a b c) -> p a b c", a=shape[0], b=shape[1])
        return v

    def parts(name, at, *shape):
        n = 1
        for x in shape:
            n *= x
        v = nc.alloc_sbuf_tensor_at(name, [P, n], F32R, offset=base + 4 * at)[:, :]
        return v.rearrange("p (a b) -> p a b", a=shape[0]) if len(shape) == 2 else v

    s.view = view
    s.cst = view(0, CST_W)
    cst = lambda name, *shape: view(CST[name][0], *(shape or (CST[name][1],)))
    s.ident, s.tri_f, s.tri_b, s.block = cst("ident"), cst("tri_f"), cst("tri_b"), cst("block")
    s.strict_f, s.strict_b = cst("strict_f"), cst("strict_b")
    s.level_f, s.level_b = cst("level_f", 6, P), cst("level_b", 6, P)
    s.colmask, s.before, s.ones = cst("colmask"), cst("before"), cst("ones")
    s.grid16, s.token, s.over_id = cst("grid16"), cst("token"), cst("over_id")
    at = CST_W
    s.mod_a1 = view(at, KD, 2); at += 16
    s.mod_b1 = view(at, KD, 2); at += 16
    s.gain1 = view(at, KD); at += 8
    s.gain2 = view(at, KD); at += 8
    s.epsc = view(at, 1); at += 1
    s.zero = view(at, 1); at += 1
    s.ss = view(at, NT); at += NT
    s.rstd = view(at, NT); at += NT
    s.qgain = view(at, 1); at += 1
    s.kgain = view(at, 1); at += 1
    s.pscale = view(at, 2); at += 2
    s.taps = view(at, 6, 4); at += 24
    s.silu = view(at, KD, 2); at += 16
    s.cond = view(at, KD, 2); at += 16
    assert at <= 3072, at
    B = 3072
    s.mod = view(B, 2 * D)
    s.ada_ring = [view(B + 2 * D + i * 4096, KD, 512) for i in range(ADA_EARLY)]
    s.b_ada = view(30820, 2 * D)
    s.hT = view(B, KD, N_TOK)
    s.pool_fm = view(12288, 2, POOL_ROW)
    s.qkv_fm = view(14656, 6, CONV_ROW)
    s.q_tm = view(21604, NT, NA_W)
    s.k_tm = view(26212, NT, NA_W)
    s.v_tm = view(30820, NT, NA_W)
    s.zba = view(35428, NT, DN_W + 4 * DN_H)
    s.w_ring = [view(37876 + 4096 * i, KD * 512) for i in range(2)]
    s.x_all = view(21604, NT, D)
    s.xn_ring = [view(46068 + 1024 * i, D) for i in range(3)]
    s.junk = view(49140, D)
    s.zero_rows = view(50164, D)
    s.qT = view(37876, 4, N_TOK)
    s.kT = view(42484, 4, N_TOK)
    s.kcT = view(47092, 4, PAST)
    s.vc_tm = view(48116, 2, NA_W)
    s.kc_tm = view(49140, 2, NA_W)
    s.sq_ring = [view(50164 + 512 * i, 512) for i in range(2)]
    s.qk_ss = view(51188, 2 * NT * NA_H)
    s.qk_r = view(51332, 2 * NT * NA_H)
    s.kgain_row = view(51476, HEAD)
    s.kn_ctx = view(51540, NA_W)
    s.late_ring = [view(at, KD, 512) for at in (7680, 44824, 48920)]
    s.mod_late = [view(34400 + 512 * i, 512) for i in range(2)]
    s.bias = [view(21604 + 896 * i, 14, GRID) for i in range(2)]
    s.bias_mid = [view(23396 + 576 * i, 9, GRID) for i in range(2)]
    s.weights = [view(24548 + 832 * i, 832) for i in range(2)]
    s.wT = [view(26212 + 896 * i, 7 * P) for i in range(2)]
    s.at_m1, s.at_max, s.at_nm, s.at_sum, s.at_inv = [view(28004 + 4 * i, 4) for i in range(5)]
    s.o_naT = view(3072, 4, N_TOK)
    s.o_dn = view(7680, NT, DN_W)
    s.qkv_tm = view(21604, NT, 3 * DN_W)
    at = 28516
    s.a_log = view(at, 8); at += 8
    s.dt_bias = view(at, 8); at += 8
    s.a_in, s.a_abs, s.g, s.cum, s.g_rest, s.beta, s.beta_eg, s.dn_ss = [view(at + NT * 8 * i, NT, 8) for i in range(8)]
    at += 8 * NT * 8
    s.dn_sq = [view(at + 512 * i, 512) for i in range(2)]; at += 1024
    s.S_ctx = view(at, 2, 4, HEAD); at += 512
    s.S_lat = view(at, 2, 4, HEAD); at += 512
    s.fin_r = view(at, NT * DN_H); at += 36
    s.dn_gain = view(at, HEAD); at += 64
    s.kb, s.vb, s.kg, s.kd, s.su, s.vn = [[view(at + 512 * j + 256 * i, 256) for i in range(2)] for j in range(6)]
    at += 6 * 512
    assert at <= 35428, at
    s.conv = [view(46068 + 1160 * i, CONV_ROW - 3) for i in range(2)]
    at = 37876
    (s.sqT, s.skT, s.skbT, s.pos, s.neg, s.dec, s.decT, s.eb, s.L, s.LT, s.attT, s.X, s.Z,
     s.Y) = [[view(at + 1024 * j + 512 * i, 512) for i in range(2)] for j in range(14)]
    at += 14 * 1024
    s.swT = [view(14656 + 512 * i, 512) for i in range(2)]
    s.sqd = [view(15680 + 512 * i, 512) for i in range(2)]
    s.sqT, s.skT, s.skbT, s.swT, s.sqd = [[v[0:HEAD, :] for v in pair] for pair in (s.sqT, s.skT, s.skbT, s.swT, s.sqd)]
    assert at <= 53120, at
    s.o_poolT = view(14656, 2, N_TOK)
    s.o_dnT = view(16960, 2, N_TOK)
    s.pool_a = view(16704, POOL_ROW)
    s.pool_b = view(17888, POOL_ROW)
    s.pool_rc = view(19072, 2, POOL_ROW)
    s.w_pool = view(47348, 2, HEAD)
    s.w_out = view(21604, KD, D)
    s.g1_row = view(31700, 2, D)
    s.xr_ring = [view(19264 + D * i, D) for i in range(2)]
    s.x1 = view(42784, NT, D)
    s.h2T_ring = [view(9984 + D * i, KD, P) for i in range(2)]
    s.a2_row = view(35428, 2, D)
    s.b2_row = view(37476, 2, D)
    s.n2_row = view(39524, D)
    s.w_router = view(40548, KD, N_EXP)
    s.junk2 = view(33748, D)
    s.h2_ring = [view(40676 + D * i, D) for i in range(2)]
    s.g2_ring = [view(17408 + 4096 * i, KD, 512) for i in range(2)]
    s.zero_slots = view(42732, SLOTS // P).bitcast(U32)
    at = 52000
    s.b_router = view(at, N_EXP); at += 16
    s.slot_idx = view(at, SLOTS // P).bitcast(U32); at += SLOTS // P
    s.slot_hi, s.slot_lo, s.token_id = [view(at + NT * i, NT).bitcast(U32) for i in range(3)]; at += 3 * NT
    s.w_hi, s.w_lo = [view(at + NT * i, NT) for i in range(2)]; at += 2 * NT
    s.over_table = view(at, OVER + 1).bitcast(U32); at += OVER + 1
    assert at <= 52736
    at = 27648
    s.route = {}
    for name in ("score", "sel", "rank", "tmp", "mask", "weight", "off", "slot"):
        s.route[name] = view(at, NT * N_EXP); at += NT * N_EXP
    for name in ("gsum", "grank", "gtmp", "gmask"):
        s.route[name] = view(at, NT * 4); at += NT * 4
    for name in ("wsum", "hi", "lo"):
        s.route[name] = view(at, NT); at += NT
    for name in ("total", "over", "o16", "cum"):
        s.route[name] = view(at, N_EXP); at += N_EXP
    s.over_cmp = view(at, OVER, N_EXP)
    s.we_ring = [view(3072 + 4096 * i, 4096) for i in range(6)]
    s.hg = [view(27648 + 2048 * i, 2, D) for i in range(2)]
    s.hgT = [view(31744 + 2048 * i, KD, CAP) for i in range(2)]
    s.hid = [view(35840 + 1024 * i, 4, CAP) for i in range(2)]
    s.sg = [view(37888 + 256 * i, CAP) for i in range(2)]
    s.y_ring = [view(38400 + 1024 * i, D) for i in range(3)]
    s.unit_x = [view(3072 + 2048 * i, 2048) for i in range(UNIT_X)]
    s.unit_low = [parts(f"unit_low{i}", 3072 + 2048 * i, 2048) for i in range(UNIT_X)]
    s.unit_high = [parts(f"unit_high{i}", 17408 + 2048 * i, 2048) for i in range(UNIT_H)]
    s.hg_rows = view(29696, 2, D)
    s.hgT_high = parts("hgT_high", 31744, KD, CAP)
    s.hgT_low = parts("hgT_low", 33792, KD, CAP)
    s.hid_high = parts("hid_high", 35840, 4, CAP)
    s.hid_low = parts("hid_low", 36864, 4, CAP)
    s.hid_whole = [view(38400 + 256 * i, CAP) for i in range(2)]
    s.y_rows = [view(38912 + 1024 * i, D) for i in range(3)]
    s.further_gate = view(41472, 4, P)
    s.further_idx = view(41984, 1).bitcast(U32)
    s.g2_row = view(12288, 2, D)
    s.y_hi = [view(14336 + D * i, D) for i in range(3)]
    s.y_lo = [view(17408 + D * i, D) for i in range(3)]
    s.big_a = view(37876, NT * DN_W)
    s.big_b = view(37876 + NT * DN_W, NT * DN_W)


def stage_modulation(nc, s, d):
    sem = s.sem
    loaded, exp_done = sem("small_loaded"), sem("cond_exp_done")
    ada_in = [sem(f"ada_in{i}") for i in range(ADA_EARLY)]
    silu_done, rows_done, copied = sem("silu_done"), sem("mod_rows_done"), sem("mod_rows_copied")
    squared = sem("n1_squared")
    stored, turned, chain = sem("mod_rows_stored"), sem("mod_turned"), sem("mod_chain")
    eps_set = sem("eps_set")
    w_ada = d["w_ada"][0].rearrange("(k p) n -> p k n", p=P)
    NB = ADA_EARLY
    with nc.Block() as block:
        @block.sync
        def _(sp):
            sp.dma_start(s.cst, d["consts"]).then_inc(loaded, 16)
            with nc.allow_non_contiguous_dma(reason="small vectors onto partitions"):
                sp.dma_start(s.cond[:, :, 0], d["c_ctx"].rearrange("(k p) -> p k", p=P)).then_inc(loaded, 16)
                sp.dma_start(s.cond[:, :, 1], d["c"][0].rearrange("(k p) -> p k", p=P)).then_inc(loaded, 16)
                sp.dma_start(s.gain1, d["norm1_g"][0].rearrange("(k p) -> p k", p=P)).then_inc(loaded, 16)
                for h in range(2):
                    rows = slice(h * HEAD, (h + 1) * HEAD)
                    sp.dma_start(s.qgain[rows, :], d["q_norm_g"].rearrange("a b -> b a")).then_inc(loaded, 16)
                    sp.dma_start(s.kgain[rows, :], d["k_norm_g"].rearrange("a b -> b a")).then_inc(loaded, 16)
                sp.dma_start(s.pscale, d["pool_scale"][0].rearrange("(k p) -> p k", p=P)).then_inc(loaded, 16)
            for i in range(2):
                sp.dma_start(s.b_ada[i:i + 1, :], d["b_ada"][:, 0:2 * D]).then_inc(loaded, 16)
            for n in range(NB):
                sp.dma_start(s.ada_ring[n], w_ada[:, :, n * 512:(n + 1) * 512]).then_inc(ada_in[n], 16)
            for t in range(NT):
                src = d["x_prompt"][0] if t == 0 else d["x_sample"][0, (t - 1) * P:t * P, :]
                sp.dma_start(s.x_all[:, t, :], src).then_inc(s.x_in[t], 16)
            sp.dma_start(d["rpb_rows"].rearrange("r (n w) -> r n w", w=RPB_W),
                         d["rpb"][0].rearrange("h r w -> (h r) w").unsqueeze(1).to_broadcast([NA_H * 15, RPB_REP, RPB_W])).then_inc(stored, 16)
            sp.wait_ge(stored, 16)

        @block.scalar
        def _(act):
            act.wait_ge(loaded, 16 * 11)
            act.wait_ge(eps_set, 1)
            nc.scalar.activation(s.silu, s.cond, ACT.Silu).then_inc(silu_done, 1)
            for t in range(NT):
                act.wait_ge(s.x_in[t], 16)
                nc.scalar.activation(s.junk, s.x_all[:, t, :], ACT.Square, accum_out=s.ss[:, t:t + 1]).then_inc(squared, 1)
                act.wait_ge(squared, t + 1)
            nc.scalar.activation(s.rstd, s.ss, ACT.Sqrt, bias=s.epsc, scale=1.0 / D)

        @block.vector
        def _(dve):
            nc.vector.memset(s.epsc, EPS).then_inc(eps_set, 1)
            for n in range(NB):
                dve.wait_ge(rows_done, n + 1)
                if n == 0:
                    dve.wait_ge(loaded, 16 * 11)
                cols = slice(n * 512, (n + 1) * 512)
                nc.vector.tensor_tensor(s.mod[0:2, cols], s.bank[n % 2][0:2, :], s.b_ada[0:2, cols],
                                        ALU.add).then_inc(copied, 1)
            nc.vector.tensor_scalar(s.qgain, s.qgain, HEAD ** -0.5, None, ALU.mult)
            dve.wait_ge(turned, 1)
            tr = s.bank[2][:, 0:32].rearrange("p (v k c) -> p v k c", v=2, k=KD)
            nc.vector.tensor_copy(s.mod_b1, tr[:, 0])
            for c in range(2):
                nc.vector.scalar_tensor_tensor(s.mod_a1[:, :, c], tr[:, 1, :, c], 1.0, s.gain1, ALU.add, ALU.mult)

        @block.tensor
        def _(pe):
            pe.wait_ge(silu_done, 1)
            for n in range(NB):
                pe.wait_ge(ada_in[n], 16)
                if n >= 2:
                    pe.wait_ge(copied, n - 1)
                for k in range(KD):
                    mm = nc.tensor.matmul(s.bank[n % 2][0:2, :], s.silu[:, k, :], s.ada_ring[n][:, k, :],
                                          start=(k == 0), stop=(k == KD - 1))
                mm.then_inc(rows_done, 1)
            pe.wait_ge(copied, NB)
            for v in range(2):
                for k in range(KD):
                    at = (v * KD + k) * 2
                    tr = nc.tensor.transpose(s.bank[2][:, at:at + 2], s.mod[0:2, v * D + k * P:v * D + (k + 1) * P],
                                             s.ident[0:2, 0:2])
            tr.then_inc(turned, 1)


GROUPS = [(COL_POOL, POOL_W, "fm"), (COL_DN, 384, "fm"), (COL_DN + 384, 384, "fm"), (COL_Q, 512, "q"),
          (COL_K, 512, "k"), (COL_V, 512, "v"), (COL_Z, DN_W + 4 * DN_H, "zba")]


def load_projection(sp, s, d, g):
    col, width, _ = GROUPS[g]
    src = d["w_in"][0].rearrange("(k p) n -> p k n", p=P)[:, :, col:col + width]
    sp.dma_start(s.w_ring[g % 2][:, 0:KD * width].rearrange("p (k n) -> p k n", k=KD), src).then_inc(s.w_loaded[g % 2], 16)


def stage_norm1(nc, s, d):
    sem = s.sem
    rstd_done = sem("n1_rstd_done")
    xn_ready, turned, act_out, dve_out = sem("xn_ready"), sem("xn_turned"), sem("n1_act_out"), sem("n1_dve_out")

    def place(t):
        return [s.bank[2 * (t % 2)], s.bank[2 * (t % 2) + 1]]

    with nc.Block() as block:
        @block.sync
        def _(sp):
            for g in range(2):
                load_projection(sp, s, d, g)

        @block.scalar
        def _(act):
            for t in range(NT):
                act.wait_ge(turned, t + 1)
                c = 0 if t == 0 else 1
                for k in range(KD // 2):
                    ps = place(t)[k // 4][:, (k % 4) * P:(k % 4 + 1) * P]
                    nc.scalar.activation(s.hT[:, k, t * P:(t + 1) * P], ps, ACT.Identity, bias=s.mod_b1[:, k, c:c + 1],
                                         scale=s.mod_a1[:, k, c:c + 1]).then_inc(act_out, 1)

        @block.vector
        def _(dve):
            nc.vector.reciprocal(s.rstd, s.rstd).then_inc(rstd_done, 1)
            dve.wait_ge(rstd_done, 1)

            def scale_rows(t):
                if t >= 3:
                    dve.wait_ge(turned, t - 2)
                nc.vector.tensor_scalar(s.xn_ring[t % 3], s.x_all[:, t, :], s.rstd[:, t:t + 1], None,
                                        ALU.mult).then_inc(xn_ready, 1)

            scale_rows(0)
            scale_rows(1)
            for t in range(NT):
                if t + 2 < NT:
                    scale_rows(t + 2)
                dve.wait_ge(turned, t + 1)
                c = 0 if t == 0 else 1
                for k in range(KD // 2, KD):
                    ps = place(t)[k // 4][:, (k % 4) * P:(k % 4 + 1) * P]
                    nc.vector.tensor_scalar(s.hT[:, k, t * P:(t + 1) * P], ps, s.mod_a1[:, k, c:c + 1],
                                            s.mod_b1[:, k, c:c + 1], ALU.mult, ALU.add).then_inc(dve_out, 1)

        @block.tensor
        def _(pe):
            for t in range(NT):
                pe.wait_ge(xn_ready, t + 1)
                if t >= 2:
                    pe.wait_ge(act_out, 4 * (t - 1))
                    pe.wait_ge(dve_out, 4 * (t - 1))
                for k in range(KD):
                    tr = nc.tensor.transpose(place(t)[k // 4][:, (k % 4) * P:(k % 4 + 1) * P],
                                             s.xn_ring[t % 3][:, k * P:(k + 1) * P], s.ident)
                tr.then_inc(turned, 1)


def stage_project(nc, s, d):
    sem = s.sem
    groups, w_loaded = GROUPS, s.w_loaded
    product, act_out, dve_out, padded, v_stored = sem("proj_product"), sem("proj_act_out"), sem("proj_dve_out"), sem("proj_padded"), s.out_sem["v_stored"]
    rows_zeroed = sem("rows_zeroed")
    taps_in, conv_chain, conv_done, conv_silu = sem("taps_in"), sem("conv_chain"), sem("conv_done"), sem("conv_silu")
    NJ = CONV_ROW - 3
    tm_dst = {"q": s.q_tm, "k": s.k_tm, "v": s.v_tm, "zba": s.zba}

    units = []
    for g, (col, width, kind) in enumerate(groups):
        mine = []
        if kind == "fm":
            for c in range(width // P):
                if g == 0:
                    row, ctx_at, lat_at = s.pool_fm[:, c], POOL_CTX, POOL_LAT
                else:
                    row, ctx_at, lat_at = s.qkv_fm[:, (g - 1) * 3 + c], CONV_CTX, CONV_LAT
                mine.append((g, (c * P, P), (0, P), row[:, ctx_at:ctx_at + CTX]))
                for half in range(2):
                    mine.append((g, (c * P, P), (P + 512 * half, 512), row[:, lat_at + 512 * half:lat_at + 512 * (half + 1)]))
        else:
            for t in range(NT):
                mine.append((g, None, (t * P, P), tm_dst[kind][:, t, :]))
        units += mine
    last_of = {u[0]: i for i, u in enumerate(units)}
    widths = [w for _, w, _ in groups]

    def conv_row(i):
        first = last_of[2] + 3 - last_of[2] % 2
        c = (i - first) // 6
        return c if i >= first and (i - first) % 6 == 0 and c < 6 else None

    def out_of(i):
        g, wc, (t0, n), _ = units[i]
        return s.bank[i % 4][:, 0:(n if wc else widths[g])]

    def w_view(g):
        return s.w_ring[g % 2][:, 0:KD * widths[g]].rearrange("p (k n) -> p k n", k=KD)

    with nc.Block() as block:
        @block.sync
        def _(sp):
            with nc.allow_non_contiguous_dma(reason="conv taps onto partitions"):
                for k in range(4):
                    sp.dma_start(s.taps[:, :, k], d["dn_conv_w"][0, k].rearrange("(c p) -> p c", p=P)).then_inc(taps_in, 16)
            for g in range(2, len(groups)):
                sp.wait_ge(product, last_of[g - 2] + 1)
                load_projection(sp, s, d, g)
            last_v = last_of[5]
            sp.wait_ge(act_out, last_v // 2 + 1)
            sp.wait_ge(dve_out, last_v // 2 + 1)
            sp.dma_start(d["out_v"][0, 0].rearrange("h p d -> p h d"),
                         s.v_tm[:, 0, :].rearrange("p (h d) -> p h d", h=NA_H)).then_inc(v_stored, 16)
            sp.wait_ge(v_stored, 16)

        @block.gpsimd
        def _(pool):
            for at, n in ((0, POOL_PAD), (POOL_CTX + CTX, POOL_PAD), (POOL_LAT + LAT, POOL_PAD)):
                nc.gpsimd.memset(s.pool_fm[:, :, at:at + n], 0.0)
            for at, n in ((0, 1), (CONV_CTX + CTX, 3), (CONV_LAT + LAT, 2)):
                nc.gpsimd.memset(s.qkv_fm[:, :, at:at + n], 0.0).then_inc(padded, 1)
            nc.gpsimd.memset(s.zero_rows, 0.0).then_inc(padded, 1)
            pool.wait_ge(padded, 4)
            for i in range(OVER):
                pool.dma_start(d["slot_rows"][(N_EXP * CAP) + i * P:(N_EXP * CAP) + (i + 1) * P, :], s.zero_rows).then_inc(rows_zeroed, 16)
            pool.wait_ge(rows_zeroed, 16 * OVER)

        @block.scalar
        def _(act):
            for i in range(0, len(units), 2):
                act.wait_ge(product, i + 1)
                nc.scalar.copy(units[i][3], out_of(i)).then_inc(act_out, 1)
                if conv_row(i - 1) is not None:
                    c = conv_row(i - 1)
                    act.wait_ge(conv_done, c + 1)
                    nc.scalar.activation(s.qkv_fm[:, c, 0:NJ], s.conv[c % 2], ACT.Silu).then_inc(conv_silu, 1)

        @block.vector
        def _(dve):
            for i in range(1, len(units), 2):
                dve.wait_ge(product, i + 1)
                nc.vector.tensor_copy(units[i][3], out_of(i)).then_inc(dve_out, 1)
                c = conv_row(i)
                if c is None:
                    continue
                if c == 0:
                    dve.wait_ge(taps_in, 64)
                    dve.wait_ge(padded, 3)
                    dve.wait_ge(act_out, last_of[2] // 2 + 1)
                    dve.wait_ge(dve_out, (last_of[2] + 1) // 2)
                if c >= 2:
                    dve.wait_ge(conv_silu, c - 1)
                u, out = s.qkv_fm[:, c], s.conv[c % 2]
                nc.vector.tensor_scalar(out, u[:, 0:NJ], s.taps[:, c, 0:1], None, ALU.mult).then_inc(conv_chain, 1)
                for k in range(1, 4):
                    dve.wait_ge(conv_chain, 3 * c + k)
                    nc.vector.scalar_tensor_tensor(out, u[:, k:k + NJ], s.taps[:, c, k:k + 1], out, ALU.mult,
                                                   ALU.add).then_inc(conv_chain if k < 3 else conv_done, 1)

        @block.tensor
        def _(pe):
            for i, (g, wc, (t0, n), _) in enumerate(units):
                if i == 0 or units[i - 1][0] != g:
                    pe.wait_ge(w_loaded[g % 2], 16 * (g // 2 + 1))
                if i >= 4:
                    pe.wait_ge(act_out if i % 2 == 0 else dve_out, (i - 4) // 2 + 1)
                w = w_view(g)
                for k in range(KD):
                    if wc:
                        mm = nc.tensor.matmul(out_of(i), w[:, k, wc[0]:wc[0] + wc[1]], s.hT[:, k, t0:t0 + n],
                                              start=(k == 0), stop=(k == KD - 1))
                    else:
                        mm = nc.tensor.matmul(out_of(i), s.hT[:, k, t0:t0 + n], w[:, k, :],
                                              start=(k == 0), stop=(k == KD - 1))
                mm.then_inc(product, 1)


def stage_heads(nc, s, d):
    sem = s.sem
    cache_in, gain_in = sem("cache_in"), sem("kgain_row_in")
    squared, summed, std_done, r_done = sem("qk_squared"), sem("qk_summed"), sem("qk_std_done"), sem("qk_r_done")
    scaled, turned, out = sem("qk_scaled"), sem("qk_turned"), sem("qk_out")
    kc_turned, kc_out, kn_done, kn_stored = sem("kc_turned"), sem("kc_out"), sem("kn_done"), s.out_sem["kn_stored"]
    tiles = [(t, w) for t in range(NT) for w in range(2)]
    tm = [s.q_tm, s.k_tm]

    with nc.Block() as block:
        @block.sync
        def _(sp):
            for i in range(2):
                rows = slice(i * P, (i + 1) * P)
                sp.dma_start(s.kc_tm[:, i, :].rearrange("p (h d) -> p h d", h=NA_H),
                             d["cache_na_k"][0, 0, :, rows, :].rearrange("h p d -> p h d")).then_inc(cache_in, 16)
                sp.dma_start(s.vc_tm[:, i, :].rearrange("p (h d) -> p h d", h=NA_H),
                             d["cache_na_v"][0, 0, :, rows, :].rearrange("h p d -> p h d")).then_inc(cache_in, 16)
            sp.dma_start(s.kgain_row, d["k_norm_g"].to_broadcast([P, HEAD])).then_inc(gain_in, 16)
            sp.wait_ge(kn_done, 1)
            sp.dma_start(d["out_k"][0, 0].rearrange("h p d -> p h d"),
                         s.kn_ctx.rearrange("p (h d) -> p h d", h=NA_H)).then_inc(kn_stored, 16)
            sp.wait_ge(kn_stored, 16)

        @block.scalar
        def _(act):
            for j, (t, w) in enumerate(tiles):
                if j >= 2:
                    act.wait_ge(summed, j - 1)
                nc.scalar.activation(s.sq_ring[j % 2], tm[w][:, t, :], ACT.Square).then_inc(squared, 1)
            act.wait_ge(summed, len(tiles))
            nc.scalar.activation(s.qk_r, s.qk_ss, ACT.Sqrt, bias=s.epsc, scale=1.0 / HEAD).then_inc(std_done, 1)
            for i in range(2):
                act.wait_ge(kc_turned, i + 1)
                nc.scalar.copy(s.kcT[:, :, i * P:(i + 1) * P], s.bank[4 + i].rearrange("p (a b) -> p a b", a=4)).then_inc(kc_out, 1)
            for j, (t, w) in enumerate(tiles):
                act.wait_ge(turned, j + 1)
                dst = (s.qT, s.kT)[w][:, :, t * P:(t + 1) * P]
                nc.scalar.activation(dst, s.bank[j % 4].rearrange("p (a b) -> p a b", a=4), ACT.Copy,
                                     scale=(s.qgain, s.kgain)[w]).then_inc(out, 1)

        @block.vector
        def _(dve):
            for j, (t, w) in enumerate(tiles):
                dve.wait_ge(squared, j + 1)
                nc.vector.tensor_reduce(s.qk_ss[:, j * NA_H:(j + 1) * NA_H],
                                        s.sq_ring[j % 2].rearrange("p (h d) -> p h d", h=NA_H), AX.X, ALU.add).then_inc(summed, 1)
            dve.wait_ge(std_done, 1)
            nc.vector.reciprocal(s.qk_r, s.qk_r).then_inc(r_done, 1)
            dve.wait_ge(r_done, 1)
            for j, (t, w) in enumerate(tiles):
                x = tm[w][:, t, :].rearrange("p (h d) -> p h d", h=NA_H)
                r = s.qk_r[:, j * NA_H:(j + 1) * NA_H].unsqueeze(2).to_broadcast([P, NA_H, HEAD])
                nc.vector.tensor_tensor(x, x, r, ALU.mult).then_inc(scaled, 1)
                if j == 1:
                    dve.wait_ge(scaled, 2)
                    dve.wait_ge(gain_in, 16)
                    nc.vector.tensor_tensor(s.kn_ctx.rearrange("p (h d) -> p h d", h=NA_H), x,
                                            s.kgain_row.unsqueeze(1).to_broadcast([P, NA_H, HEAD]), ALU.mult).then_inc(kn_done, 1)

        @block.tensor
        def _(pe):
            pe.wait_ge(cache_in, 64)
            for i in range(2):
                for hp in range(4):
                    tr = nc.tensor.transpose(s.bank[4 + i][:, hp * P:(hp + 1) * P], s.kc_tm[:, i, hp * P:(hp + 1) * P], s.ident)
                tr.then_inc(kc_turned, 1)
            for j, (t, w) in enumerate(tiles):
                pe.wait_ge(scaled, j + 1)
                if j >= 4:
                    pe.wait_ge(out, j - 3)
                for hp in range(4):
                    tr = nc.tensor.transpose(s.bank[j % 4][:, hp * P:(hp + 1) * P], tm[w][:, t, hp * P:(hp + 1) * P], s.ident)
                tr.then_inc(turned, 1)


def query_tiles():
    out = []
    rows, kh = LAT // GRID, 8
    for i in range(rows // 2):
        first = [min(max(r - kh // 2, 0), rows - kh) for r in (2 * i, 2 * i + 1)]
        n = first[1] + kh - first[0]
        out.append((1 + i, first[0], n, first[0] - 2 * i + 6))
    out.append((0, None, None, None))
    return out


def stage_attention(nc, s, d):
    sem = s.sem
    bias_in, bias_ready = [sem(f"bias_in{i}") for i in range(2)], sem("bias_ready")
    scored, biased, neg_max, weighted = sem("at_scored"), sem("at_biased"), sem("at_neg_max"), sem("at_weighted")
    turned, act_out, dve_out = sem("at_turned"), sem("at_act_out"), sem("at_dve_out")
    part_max = sem("at_part_max")
    inverse, normed, mixed, mixed_read, chain = [sem("at_" + n) for n in ("inverse", "normed", "mixed", "mixed_read", "chain")]
    tiles = query_tiles()
    units = [(h, q) for h in range(NA_H) for q in range(len(tiles))]
    U, Q = len(units), len(tiles)

    def local(q):
        return 0 if tiles[q][2] is None else tiles[q][2] * GRID

    def width(q):
        return P if tiles[q][2] is None else local(q) + PAST

    def blocks(q):
        t, r0, n, _ = tiles[q]
        if n is None:
            return [(0, P, 0, False)]
        full = [(b * P, min(P, local(q) - b * P), 1 + r0 // 2 + b, False) for b in range((n + 1) // 2)]
        return full + [(local(q) + b * P, P, b, True) for b in range(PAST // P)]

    def scores(u):
        return s.pair[u % 3]

    with nc.Block() as block:
        @block.sync
        def _(sp):
            load_late(sp, s, d, 0)
            for h in range(NA_H):
                if h >= 2:
                    sp.wait_ge(biased, Q * (h - 1))
                    sp.wait_ge(bias_ready, h - 1)
                for a in range(2):
                    src = bass.AP(tensor=d["rpb_rows"].tensor, offset=(h * 15 + 1 - a) * RPB_ROW + 15,
                                  ap=[[RPB_W - 1, GRID], [RPB_ROW, 14], [1, GRID]])
                    sp.dma_start(s.bias[h % 2][a * GRID:(a + 1) * GRID], src).then_inc(bias_in[h % 2], 16)

        @block.gpsimd
        def _(pool):
            for h in range(NA_H):
                b, m = s.bias[h % 2], s.bias_mid[h % 2]
                pool.wait_ge(bias_in[h % 2], 32 * (h // 2 + 1))
                nc.gpsimd.tensor_tensor(b, b, s.colmask.unsqueeze(1).to_broadcast([P, 14, GRID]), ALU.add).then_inc(chain, 1)
                pool.wait_ge(chain, 3 * h + 1)
                nc.gpsimd.tensor_copy(m, b[:, 2:11, :]).then_inc(chain, 1)
                pool.wait_ge(chain, 3 * h + 2)
                nc.gpsimd.memset(m[0:GRID, 8, :], NEG)
                nc.gpsimd.memset(m[GRID:P, 0, :], NEG).then_inc(chain, 1)
                pool.wait_ge(chain, 3 * h + 3)
                nc.gpsimd.nop().then_inc(bias_ready, 1)

        @block.scalar
        def _(act):
            def turned_out(u):
                h, q = units[u]
                n = min(len(blocks(q)), 4) * P
                act.wait_ge(turned, u + 1)
                if u >= 2:
                    act.wait_ge(mixed, u - 1)
                nc.scalar.copy(s.wT[u % 2][:, 0:n], s.pair[u % 3][:, 0:n]).then_inc(act_out, 1)

            def weigh(u):
                h, q = units[u]
                act.wait_ge(neg_max, u + 1)
                w = s.weights[u % 2][:, 0:width(q)]
                nc.scalar.activation(w, w, ACT.Exp, bias=s.at_nm[:, u % 4:u % 4 + 1],
                                     accum_out=s.at_sum[:, u % 4:u % 4 + 1]).then_inc(weighted, 1)

            def mixed_out(u):
                h, q = units[u]
                half, t = slice((h % 2) * HEAD, (h % 2 + 1) * HEAD), tiles[q][0]
                act.wait_ge(mixed, u + 1)
                nc.scalar.copy(s.o_naT[half, h // 2, t * P:(t + 1) * P], s.bank[6 + u % 2][half, 0:P]).then_inc(mixed_read, 1)

            weigh(0)
            weigh(1)
            for u in range(U):
                turned_out(u)
                if u + 2 < U:
                    weigh(u + 2)
                mixed_out(u)

        @block.vector
        def _(dve):
            def turned_out(u):
                h, q = units[u]
                n = (len(blocks(q)) - 4) * P
                dve.wait_ge(turned, u + 1)
                if u >= 2:
                    dve.wait_ge(mixed, u - 1)
                if n > 0:
                    nc.vector.tensor_copy(s.wT[u % 2][:, 512:512 + n], s.pair[u % 3][:, 512:512 + n]).then_inc(dve_out, 1)
                else:
                    dve.sem_inc(dve_out, 1)

            def biased_max(u):
                h, q = units[u]
                t, r0, n, m0 = tiles[q]
                dve.wait_ge(scored, u + 1)
                if u >= 2:
                    dve.wait_ge(turned, u - 1)
                if q == 0:
                    dve.wait_ge(bias_ready, h + 1)
                w, L = s.weights[u % 2], local(q)
                mx, nm = s.at_max[:, u % 4:u % 4 + 1], s.at_nm[:, u % 4:u % 4 + 1]
                if n is None:
                    nc.vector.tensor_scalar(w[:, 0:P], scores(u)[:, 0:P], 1.0, None, ALU.mult, ALU.max, accum_out=mx).then_inc(biased, 1)
                else:
                    bias = s.bias_mid[h % 2] if n == 9 else s.bias[h % 2][:, m0:m0 + n, :]
                    m1 = s.at_m1[:, u % 4:u % 4 + 1]
                    nc.vector.tensor_tensor_reduce(out=w[:, 0:L], in0=scores(u)[:, 0:L],
                                                   in1=bias.rearrange("p a b -> p (a b)"), scale=1.0, scalar=NEG,
                                                   op0=ALU.add, op1=ALU.max, accum_out=m1).then_inc(part_max, 1)
                    dve.wait_ge(part_max, h * (Q - 1) + q + 1)
                    nc.vector.tensor_scalar(w[:, L:L + PAST], scores(u)[:, L:L + PAST], 1.0, m1, ALU.mult, ALU.max,
                                            accum_out=mx).then_inc(biased, 1)
                dve.wait_ge(biased, u + 1)
                nc.vector.tensor_scalar(nm, mx, -1.0, None, ALU.mult).then_inc(neg_max, 1)

            def normalise(u):
                w = s.weights[u % 2][:, 0:width(units[u][1])]
                inv = s.at_inv[:, u % 4:u % 4 + 1]
                dve.wait_ge(weighted, u + 1)
                nc.vector.reciprocal(inv, s.at_sum[:, u % 4:u % 4 + 1]).then_inc(inverse, 1)
                dve.wait_ge(inverse, u + 1)
                nc.vector.tensor_scalar(w, w, inv, None, ALU.mult).then_inc(normed, 1)

            biased_max(0)
            biased_max(1)
            normalise(0)
            for u in range(U):
                turned_out(u)
                if u + 1 < U:
                    normalise(u + 1)
                if u + 2 < U:
                    biased_max(u + 2)

        @block.tensor
        def _(pe):
            def score(u):
                h, q = units[u]
                t, r0, n, _ = tiles[q]
                half, hp = slice((h % 2) * HEAD, (h % 2 + 1) * HEAD), h // 2
                if u >= 3:
                    pe.wait_ge(act_out, u - 2)
                    pe.wait_ge(dve_out, u - 2)
                qT = s.qT[half, hp, t * P:(t + 1) * P]
                out = scores(u)
                if n is None:
                    mm = nc.tensor.matmul(out[:, 0:P], qT, s.kT[half, hp, 0:CTX], start=True, stop=True)
                else:
                    L, k0 = local(q), CTX + r0 * GRID
                    nc.tensor.matmul(out[:, 0:512], qT, s.kT[half, hp, k0:k0 + 512], start=True, stop=True)
                    if L > 512:
                        nc.tensor.matmul(out[:, 512:L], qT, s.kT[half, hp, k0 + 512:k0 + L], start=True, stop=True)
                    mm = nc.tensor.matmul(out[:, L:L + PAST], qT, s.kcT[half, hp, :], start=True, stop=True)
                mm.then_inc(scored, 1)

            def turn(u):
                h, q = units[u]
                pe.wait_ge(normed, u + 1)
                for b, (col, n, _, _) in enumerate(blocks(q)):
                    tr = nc.tensor.transpose(s.pair[u % 3][0:n, b * P:(b + 1) * P], s.weights[u % 2][:, col:col + n], s.ident)
                tr.then_inc(turned, 1)

            def mix(u):
                h, q = units[u]
                half = slice((h % 2) * HEAD, (h % 2 + 1) * HEAD)
                pe.wait_ge(act_out, u + 1)
                pe.wait_ge(dve_out, u + 1)
                if u >= 2:
                    pe.wait_ge(mixed_read, u - 1)
                every = blocks(q)
                for b, (_, n, tile, cached) in enumerate(every):
                    v = (s.vc_tm if cached else s.v_tm)[0:n, tile, h * HEAD:(h + 1) * HEAD]
                    mm = nc.tensor.matmul(s.bank[6 + u % 2][half, 0:P], v, s.wT[u % 2][0:n, b * P:(b + 1) * P],
                                          start=(b == 0), stop=(b == len(every) - 1))
                mm.then_inc(mixed, 1)

            score(0)
            score(1)
            for u in range(U):
                turn(u)
                if u + 2 < U:
                    score(u + 2)
                mix(u)


LATE = list(range(ADA_EARLY, 5 * D // 512))


def load_late(sp, s, d, i):
    src = d["w_ada"][0].rearrange("(k p) n -> p k n", p=P)[:, :, LATE[i] * 512:(LATE[i] + 1) * 512]
    sp.dma_start(s.late_ring[i % 3], src).then_inc(s.late_in[i % 3], 16)


def stage_dn_prepare(nc, s, d):
    b_in, rows_stored = [[s.sem(f"{n}{i}") for i in range(2)] for n in ("late_b_in", "late_stored")]
    rows_done, rows_ready = s.sem("late_rows_done"), s.sem("late_rows_ready")
    sem = s.sem
    small_in, chain = sem("dn_small_in"), sem("dn_chain")
    turned, act_out, dve_out = sem("dn_turned"), sem("dn_act_out"), sem("dn_dve_out")
    squared, summed, std_done, r_done = sem("dn_squared"), sem("dn_ssq"), sem("dn_std"), sem("dn_r")
    sig_done, pre_done, abs_done, exp_done, ln_done, g_done = [sem("dn_" + n) for n in ("sig", "pre", "abs", "exp", "ln", "g")]
    cum_done, ex_in, ex_done = sem("dn_cum"), sem("dn_ex_in"), sem("dn_ex")
    G2 = 2 * DN_H
    b_raw = s.zba[:, :, DN_W:DN_W + G2]
    a_raw = s.zba[:, :, DN_W + G2:DN_W + 2 * G2]

    def tile_col(t):
        return 0 if t == 0 else CONV_LAT - 1 + (t - 1) * P

    with nc.Block() as block:
        @block.sync
        def _(sp):
            sp.dma_start(s.a_log, d["dn_a_log"].rearrange("a b c -> a (b c)").to_broadcast([P, G2])).then_inc(small_in, 16)
            sp.dma_start(s.dt_bias, d["dn_dt_bias"].rearrange("a b c -> a (b c)").to_broadcast([P, G2])).then_inc(small_in, 16)

            def store_rows(i):
                sp.wait_ge(rows_ready, i + 1)
                sp.dma_start(d["mod_rows"][:, LATE[i] * 512:(LATE[i] + 1) * 512], s.mod_late[i % 2][0:2, :]).then_inc(rows_stored[i % 2], 16)

            load_late(sp, s, d, 1)
            load_late(sp, s, d, 2)
            for i, n in enumerate(LATE):
                if i >= 2:
                    sp.wait_ge(rows_stored[i % 2], 16 * (i // 2))
                sp.dma_start(s.mod_late[i % 2][0:2, :], d["b_ada"][:, n * 512:(n + 1) * 512].to_broadcast([2, 512])).then_inc(b_in[i % 2], 16)
                if i >= 1:
                    store_rows(i - 1)
                    if i + 2 < len(LATE):
                        load_late(sp, s, d, i + 2)
            store_rows(len(LATE) - 1)
            for i in range(2):
                sp.wait_ge(rows_stored[i], 16 * len(LATE) // 2)

        @block.vector
        def _(dve):
            done = [0]

            def link(ins):
                done[0] += 1
                ins.then_inc(chain, 1)
                dve.wait_ge(chain, done[0])

            def late_rows(i):
                dve.wait_ge(rows_done, i + 1)
                dve.wait_ge(b_in[i % 2], 16 * (i // 2 + 1))
                nc.vector.tensor_tensor(s.mod_late[i % 2][0:2, :], s.bank[6 + i % 2][0:2, :], s.mod_late[i % 2][0:2, :],
                                        ALU.add).then_inc(rows_ready, 1)

            dve.wait_ge(small_in, 32)
            link(nc.vector.tensor_tensor(s.a_in, a_raw, s.dt_bias.unsqueeze(1).to_broadcast([P, NT, G2]), ALU.add))
            link(nc.vector.tensor_scalar(s.a_abs, s.a_in, -1.0, None, ALU.mult))
            nc.vector.tensor_tensor(s.a_abs, s.a_abs, s.a_in, ALU.min).then_inc(abs_done, 1)
            dve.wait_ge(ln_done, 2)
            link(nc.vector.tensor_scalar(s.a_in, s.a_in, 0.0, None, ALU.max))
            link(nc.vector.tensor_tensor(s.a_in, s.a_in, s.a_abs, ALU.add))
            link(nc.vector.tensor_scalar(s.a_log, s.a_log, -1.0, None, ALU.mult))
            nc.vector.tensor_tensor(s.g, s.a_in, s.a_log.unsqueeze(1).to_broadcast([P, NT, G2]), ALU.mult).then_inc(g_done, 1)
            for t in range(NT):
                dve.wait_ge(turned, t + 1)
                nc.vector.tensor_copy(s.qkv_tm[:, t, 512:768], s.bank[2 * (t % 2) + 1][:, 0:256]).then_inc(dve_out, 1)
                dve.wait_ge(squared, t + 1)
                nc.vector.tensor_reduce(s.dn_ss[:, t, :], s.dn_sq[t % 2].rearrange("p (h d) -> p h d", h=8), AX.X,
                                        ALU.add).then_inc(summed, 1)
                if t % 4 == 3:
                    late_rows(t // 4)
            dve.wait_ge(std_done, 1)
            nc.vector.reciprocal(s.dn_ss, s.dn_ss).then_inc(r_done, 1)
            dve.wait_ge(r_done, 1)
            nc.vector.tensor_scalar(s.dn_ss[:, :, 0:4], s.dn_ss[:, :, 0:4], HEAD ** -0.5, None, ALU.mult).then_inc(r_done, 1)
            dve.wait_ge(r_done, 2)
            for t in range(NT):
                qk = s.qkv_tm[:, t, 0:512].rearrange("p (h d) -> p h d", h=8)
                nc.vector.tensor_tensor(qk, qk, s.dn_ss[:, t, :].unsqueeze(2).to_broadcast([P, 8, HEAD]), ALU.mult)
            dve.wait_ge(cum_done, 1)
            ps = s.bank[4]
            for dd in range(2):
                nc.vector.tensor_copy(s.cum[:, :, dd * 4:dd * 4 + 4], ps[:, dd * 36:dd * 36 + 36].rearrange("p (t h) -> p t h", h=4)).then_inc(ex_in, 1)
            dve.wait_ge(ex_in, 2)
            nc.vector.tensor_tensor(s.g_rest, ps[:, 72:144].rearrange("p (t h) -> p t h", h=G2), s.cum, ALU.subtract).then_inc(ex_in, 1)
            dve.wait_ge(ex_done, 2)
            nc.vector.tensor_tensor(s.beta_eg, s.beta, s.beta_eg, ALU.mult)
            for i in range(2, len(LATE)):
                late_rows(i)

        @block.scalar
        def _(act):
            nc.scalar.activation(s.beta, b_raw, ACT.Sigmoid).then_inc(sig_done, 1)
            act.wait_ge(abs_done, 1)
            nc.scalar.activation(s.a_abs, s.a_abs, ACT.Exp).then_inc(exp_done, 1)
            nc.scalar.activation(s.a_log, s.a_log, ACT.Exp).then_inc(ln_done, 1)
            act.wait_ge(exp_done, 1)
            nc.scalar.activation(s.a_abs, s.a_abs, ACT.Ln, bias=1.0).then_inc(ln_done, 1)
            for t in range(NT):
                act.wait_ge(turned, t + 1)
                nc.scalar.copy(s.qkv_tm[:, t, 0:512], s.bank[2 * (t % 2)]).then_inc(act_out, 1)
                act.wait_ge(act_out, t + 1)
                if t >= 2:
                    act.wait_ge(summed, t - 1)
                nc.scalar.activation(s.dn_sq[t % 2], s.qkv_tm[:, t, 0:512], ACT.Square).then_inc(squared, 1)
            act.wait_ge(summed, NT)
            nc.scalar.activation(s.dn_ss, s.dn_ss, ACT.Sqrt, bias=s.epsc).then_inc(std_done, 1)
            act.wait_ge(ex_in, 3)
            nc.scalar.activation(s.beta_eg, s.cum, ACT.Exp).then_inc(ex_done, 1)
            nc.scalar.activation(s.g_rest, s.g_rest, ACT.Exp).then_inc(ex_done, 1)

        @block.tensor
        def _(pe):
            def late_rows(i):
                pe.wait_ge(s.late_in[i % 3], 16 * (i // 3 + 1))
                if i >= 2:
                    pe.wait_ge(rows_ready, i - 1)
                for k in range(KD):
                    mm = nc.tensor.matmul(s.bank[6 + i % 2][0:2, :], s.silu[:, k, :], s.late_ring[i % 3][:, k, :],
                                          start=(k == 0), stop=(k == KD - 1))
                mm.then_inc(rows_done, 1)

            for t in range(NT):
                if t >= 2:
                    pe.wait_ge(act_out, t - 1)
                    pe.wait_ge(dve_out, t - 1)
                for c in range(6):
                    bank = s.bank[2 * (t % 2) + c // 4]
                    tr = nc.tensor.transpose(bank[:, (c % 4) * P:(c % 4 + 1) * P], s.qkv_fm[:, c, tile_col(t):tile_col(t) + P], s.ident)
                tr.then_inc(turned, 1)
                if t % 4 == 3:
                    late_rows(t // 4)
            pe.wait_ge(g_done, 1)
            nc.tensor.matmul(s.bank[4][:, 0:36], s.tri_f, s.g[:, :, 0:4], start=True, stop=True)
            nc.tensor.matmul(s.bank[4][:, 36:72], s.tri_b, s.g[:, :, 4:8], start=True, stop=True)
            nc.tensor.matmul(s.bank[4][:, 72:144], s.block, s.g, start=True, stop=True).then_inc(cum_done, 1)
            for i in range(2, len(LATE)):
                late_rows(i)


def stage_dn_scan(nc, s, d):
    sem = s.sem
    both = lambda name: [sem(f"{name}_{x}") for x in "fb"]
    state_in, state_out, start = sem("state_in"), s.out_sem["state_out"], sem("dn_start")
    kb_ready, kv_ready, turned, cast, kbt = both("kb_ready"), both("kv_ready"), both("sc_turned"), both("qk_cast"), both("kbt")
    spread, diff, decay, gram, gram_out = both("spread"), both("diff"), both("decay"), both("gram"), both("gram_out")
    l_ready, l_turned, lt_ready, x_ready, x_turned, z_ready = [both(n) for n in ("l_ready", "l_turned", "lt_ready", "x_ready", "x_turned", "z_ready")]
    y_done, y_ready, dx = both("y_done"), both("y_ready"), both("dx")
    wu_done, wu_ready, qd_ready = both("wu_done"), both("wu_ready"), both("qd_ready")
    ws_done, v_ready, step_done, s_ready, o_ready = both("ws_done"), both("v_ready"), both("step_done"), both("s_ready"), both("o_ready")
    chain, pool_chain, counts_in = sem("scan_chain"), sem("windows_chain"), [sem(f"counts_in{c}") for c in range(2)]
    tile_of = lambda n, r: 0 if n == 0 else (n if r == 0 else NT - n)
    dirs = (0, 1)
    level = (s.level_f, s.level_b)
    strict = (s.strict_f, s.strict_b)
    tri = (s.tri_f, s.tri_b)
    W = 4 * P

    def heads(v, n=P):
        return v.rearrange("p (h a) -> p h a", h=4)

    def over_heads(m):
        return m.unsqueeze(1).to_broadcast([P, 4, P])

    def chunk_order(r):
        return (0, 1) if r == 0 else (1, 0)

    def end_col(r, c):
        return c * HEAD + (HEAD - 1 if r == 0 else 0)

    with nc.Block() as block:
        @block.sync
        def _(sp):
            for r in dirs:
                sp.dma_start(s.S_lat[0:HEAD, r], d["state_dn"][0, 0, r].rearrange("h k v -> k h v")).then_inc(state_in, 16)
            for c in range(2):
                sp.dma_start(s.pool_rc[:, c], d["pool_counts"][:, c]).then_inc(counts_in[c], 16)
            for r in dirs:
                sp.wait_ge(s_ready[r], 2)
                sp.dma_start(d["out_state"][0, 0, r].rearrange("h k v -> k h v"), s.S_ctx[0:HEAD, r]).then_inc(state_out, 16)
            sp.wait_ge(state_out, 32)

        @block.gpsimd
        def _(pool):
            linked = [0]

            def link(ins):
                linked[0] += 1
                ins.then_inc(pool_chain, 1)
                pool.wait_ge(pool_chain, linked[0])

            def windows(pool, c):
                u, A, B, R = s.pool_fm[:, c], s.pool_a, s.pool_b, POOL_ROW
                lo, hi = slice(0, HEAD), slice(HEAD, P)
                add = lambda out_, a, b: link(nc.gpsimd.tensor_tensor(out_, a, b, ALU.add))
                add(A[:, 1:R], u[:, 0:R - 1], u[:, 1:R])
                add(B[:, 2:R - 1], A[:, 1:R - 2], A[:, 3:R])
                if c == 1:
                    add(A[:, 4:R - 3], B[:, 2:R - 5], B[:, 6:R - 1])
                    add(B[hi, 8:R - 7], A[hi, 4:R - 11], A[hi, 12:R - 3])
                pool.wait_ge(counts_in[c], 16)
                body = slice(POOL_CTX, POOL_LAT + LAT)
                for rows, buf in ((lo, A), (hi, B)):
                    link(nc.gpsimd.tensor_tensor(buf[rows, body], buf[rows, body], s.pool_rc[rows, c, body], ALU.mult))
                    link(nc.gpsimd.tensor_tensor(u[rows, body], buf[rows, body], u[rows, body], ALU.subtract))

            for n in range(NT):
                for r in dirs:
                    t = tile_of(n, r)
                    if n >= 1:
                        pool.wait_ge(turned[r], n)
                    k = heads(s.qkv_tm[:, t, 256:512])
                    v = heads(s.qkv_tm[:, t, 512:768])
                    col = lambda x: x[:, t, r * 4:r * 4 + 4].unsqueeze(2).to_broadcast([P, 4, HEAD])
                    nc.gpsimd.tensor_tensor(heads(s.kb[r]), k, col(s.beta), ALU.mult).then_inc(kb_ready[r], 1)
                    if n >= 1:
                        pool.wait_ge(step_done[r], 2 * n)
                    nc.gpsimd.tensor_tensor(heads(s.vb[r]), v, col(s.beta), ALU.mult)
                    nc.gpsimd.tensor_tensor(heads(s.kg[r]), k, col(s.beta_eg), ALU.mult)
                    nc.gpsimd.tensor_tensor(heads(s.kd[r]), k, col(s.g_rest), ALU.mult).then_inc(kv_ready[r], 1)
                if n == 1:
                    windows(pool, 0)
                if n == 4:
                    windows(pool, 1)

        @block.scalar
        def _(act):
            for n in range(NT):
                for r in dirs:
                    b = s.bank[4 * r:4 * r + 4]
                    act.wait_ge(turned[r], n + 1)
                    if n >= 1:
                        act.wait_ge(qd_ready[r], n)
                    nc.scalar.copy(s.sqT[r], b[0][0:HEAD, :]).then_inc(cast[r], 1)
                    nc.scalar.copy(s.skT[r], b[1][0:HEAD, :]).then_inc(cast[r], 1)
                for r in dirs:
                    b = s.bank[4 * r:4 * r + 4]
                    act.wait_ge(diff[r], n + 1)
                    nc.scalar.activation(s.dec[r], s.pos[r], ACT.Exp, scale=-1.0)
                    nc.scalar.activation(s.decT[r], s.neg[r], ACT.Exp).then_inc(decay[r], 1)
                    if n >= 1:
                        act.wait_ge(s_ready[r], 2 * n)
                    nc.scalar.activation(s.eb[r], b[3], ACT.Exp).then_inc(decay[r], 1)
                for r in dirs:
                    act.wait_ge(l_turned[r], n + 1)
                    nc.scalar.copy(s.LT[r], s.bank[4 * r + 1]).then_inc(lt_ready[r], 1)
                for m in range(1, 7):
                    for r in dirs:
                        act.wait_ge(x_turned[r], 6 * n + m)
                        nc.scalar.copy(s.Z[r], s.bank[4 * r + 3]).then_inc(z_ready[r], 1)
                for r in dirs:
                    b = s.bank[4 * r:4 * r + 4]
                    act.wait_ge(wu_done[r], n + 1)
                    nc.scalar.copy(s.swT[r], b[0][0:HEAD, :])
                    nc.scalar.copy(s.su[r], b[1][:, 0:4 * HEAD]).then_inc(wu_ready[r], 1)

        @block.vector
        def _(dve):
            done = [0]

            def link(ins):
                done[0] += 1
                ins.then_inc(chain, 1)
                dve.wait_ge(chain, done[0])

            nc.vector.memset(s.o_dn, 0.0)
            nc.vector.memset(s.S_ctx, 0.0).then_inc(start, 1)
            dve.wait_ge(start, 1)
            for n in range(NT):
                for r in dirs:
                    t, b = tile_of(n, r), s.bank[4 * r:4 * r + 4]
                    dve.wait_ge(turned[r], n + 1)
                    nc.vector.tensor_copy(s.skbT[r], b[2][0:HEAD, :]).then_inc(kbt[r], 1)
                    dve.wait_ge(spread[r], n + 1)
                    gc = s.cum[:, t, r * 4:r * 4 + 4].unsqueeze(2).to_broadcast([P, 4, P])
                    link(nc.vector.tensor_tensor(heads(s.pos[r]), heads(b[3]), gc, ALU.subtract))
                    link(nc.vector.tensor_scalar(s.neg[r], s.pos[r], 0.0, None, ALU.min))
                    nc.vector.tensor_scalar(s.pos[r], s.pos[r], 0.0, None, ALU.max).then_inc(diff[r], 1)
                for r in dirs:
                    b = s.bank[4 * r:4 * r + 4]
                    dve.wait_ge(decay[r], 2 * n + 1)
                    dve.wait_ge(gram[r], n + 1)
                    link(nc.vector.tensor_tensor(heads(s.dec[r]), heads(s.dec[r]), over_heads(strict[r]), ALU.mult))
                    nc.vector.tensor_tensor(s.L[r], b[0], s.dec[r], ALU.mult).then_inc(l_ready[r], 1)
                    dve.wait_ge(l_ready[r], n + 1)
                    link(nc.vector.tensor_tensor(heads(s.X[r]), heads(s.L[r]), over_heads(level[r][:, 0, :]), ALU.mult))
                    nc.vector.scalar_tensor_tensor(heads(s.X[r]), heads(s.X[r]), -1.0, over_heads(s.ident), ALU.mult, ALU.add).then_inc(x_ready[r], 1)
                for r in dirs:
                    b = s.bank[4 * r:4 * r + 4]
                    link(nc.vector.tensor_tensor(heads(s.decT[r]), heads(s.decT[r]), over_heads(tri[r]), ALU.mult))
                    nc.vector.tensor_tensor(s.attT[r], b[2], s.decT[r], ALU.mult)
                    dve.wait_ge(decay[r], 2 * n + 2)
                    if n >= 1:
                        dve.wait_ge(step_done[r], 2 * n)
                    nc.vector.tensor_tensor(s.sqd[r], s.sqT[r], s.eb[r][0:HEAD, :], ALU.mult).then_inc(qd_ready[r], 1)
                for m in range(1, 6):
                    for r in dirs:
                        b = s.bank[4 * r:4 * r + 4]
                        dve.wait_ge(y_done[r], 5 * n + m)
                        nc.vector.tensor_tensor(heads(s.Y[r]), heads(b[0]), over_heads(level[r][:, m, :]), ALU.mult).then_inc(y_ready[r], 1)
                    for r in dirs:
                        b = s.bank[4 * r:4 * r + 4]
                        dve.wait_ge(dx[r], 5 * n + m)
                        nc.vector.tensor_tensor(s.X[r], s.X[r], b[1], ALU.subtract).then_inc(x_ready[r], 1)
                for r in dirs:
                    if n == 1 and r == 0:
                        dve.wait_ge(state_in, 32)
                for j in range(2):
                    for r in dirs:
                        c = chunk_order(r)[j]
                        rows, b = slice(c * HEAD, (c + 1) * HEAD), s.bank[4 * r:4 * r + 4]
                        S = (s.S_ctx if n == 0 else s.S_lat)[0:HEAD, r]
                        if j == 0:
                            dve.wait_ge(wu_ready[r], n + 1)
                        dve.wait_ge(ws_done[r], 2 * n + j + 1)
                        nc.vector.tensor_tensor(s.vn[r][rows], s.su[r][rows], b[0][rows, 0:4 * HEAD], ALU.subtract).then_inc(v_ready[r], 1)
                    for r in dirs:
                        t = tile_of(n, r)
                        c = chunk_order(r)[j]
                        rows, b = slice(c * HEAD, (c + 1) * HEAD), s.bank[4 * r:4 * r + 4]
                        S = (s.S_ctx if n == 0 else s.S_lat)[0:HEAD, r]
                        gl = heads(s.eb[r])[0:HEAD, :, end_col(r, c)].unsqueeze(2).to_broadcast([HEAD, 4, HEAD])
                        dve.wait_ge(step_done[r], 2 * n + j + 1)
                        link(nc.vector.tensor_tensor(S, S, gl, ALU.mult))
                        nc.vector.tensor_tensor(S, S, b[3][0:HEAD, 0:4 * HEAD].rearrange("p (h v) -> p h v", h=4), ALU.add).then_inc(s_ready[r], 1)
                        o = s.o_dn[rows, t, :]
                        link(nc.vector.tensor_tensor(o, o, b[2][rows, 0:4 * HEAD], ALU.add))
                        nc.vector.tensor_tensor(o, o, b[1][rows, 0:4 * HEAD], ALU.add).then_inc(o_ready[r], 1)
                        dve.wait_ge(o_ready[r], 2 * n + j + 1)

        @block.tensor
        def _(pe):
            for n in range(NT):
                for r in dirs:
                    t, b = tile_of(n, r), s.bank[4 * r:4 * r + 4]
                    pe.wait_ge(kb_ready[r], n + 1)
                    if n == 0 and r == 0:
                        pe.wait_ge(start, 1)
                    if n >= 1:
                        pe.wait_ge(o_ready[r], 2 * n)
                        pe.wait_ge(s_ready[r], 2 * n)
                    for h in range(4):
                        cols = slice(h * P, (h + 1) * P)
                        nc.tensor.transpose(b[0][0:HEAD, cols], s.qkv_tm[:, t, h * HEAD:(h + 1) * HEAD], s.ident)
                        nc.tensor.transpose(b[1][0:HEAD, cols], s.qkv_tm[:, t, 256 + h * HEAD:256 + (h + 1) * HEAD], s.ident)
                        tr = nc.tensor.transpose(b[2][0:HEAD, cols], s.kb[r][:, h * HEAD:(h + 1) * HEAD], s.ident)
                    tr.then_inc(turned[r], 1)
                    for h in range(4):
                        g = s.g[:, t, r * 4 + h:r * 4 + h + 1].to_broadcast([P, P])
                        mm = nc.tensor.matmul(b[3][:, h * P:(h + 1) * P], g, tri[r], start=True, stop=True)
                    mm.then_inc(spread[r], 1)
                for r in dirs:
                    b = s.bank[4 * r:4 * r + 4]
                    pe.wait_ge(cast[r], 2 * n + 2)
                    pe.wait_ge(kbt[r], n + 1)
                    for h in range(4):
                        cols = slice(h * P, (h + 1) * P)
                        nc.tensor.matmul(b[0][:, cols], s.skbT[r][0:HEAD, cols], s.skT[r][0:HEAD, cols], start=True, stop=True)
                        mm = nc.tensor.matmul(b[2][:, cols], s.skT[r][0:HEAD, cols], s.sqT[r][0:HEAD, cols], start=True, stop=True)
                    mm.then_inc(gram[r], 1)
                for r in dirs:
                    pe.wait_ge(l_ready[r], n + 1)
                    for h in range(4):
                        cols = slice(h * P, (h + 1) * P)
                        tr = nc.tensor.transpose(s.bank[4 * r + 1][:, cols], s.L[r][:, cols], s.ident)
                    tr.then_inc(l_turned[r], 1)

                def turn_x(r, m):
                    pe.wait_ge(x_ready[r], 6 * n + m)
                    if m == 1:
                        pe.wait_ge(decay[r], 2 * n + 2)
                    for h in range(4):
                        cols = slice(h * P, (h + 1) * P)
                        tr = nc.tensor.transpose(s.bank[4 * r + 3][:, cols], s.X[r][:, cols], s.ident)
                    tr.then_inc(x_turned[r], 1)

                for m in range(1, 6):
                    for r in dirs:
                        b = s.bank[4 * r:4 * r + 4]
                        turn_x(r, m)
                        if m == 1:
                            pe.wait_ge(lt_ready[r], n + 1)
                        for h in range(4):
                            cols = slice(h * P, (h + 1) * P)
                            mm = nc.tensor.matmul(b[0][:, cols], s.LT[r][:, cols], s.X[r][:, cols], start=True, stop=True)
                        mm.then_inc(y_done[r], 1)
                    for r in dirs:
                        b = s.bank[4 * r:4 * r + 4]
                        pe.wait_ge(z_ready[r], 6 * n + m)
                        pe.wait_ge(y_ready[r], 5 * n + m)
                        for h in range(4):
                            cols = slice(h * P, (h + 1) * P)
                            mm = nc.tensor.matmul(b[1][:, cols], s.Z[r][:, cols], s.Y[r][:, cols], start=True, stop=True)
                        mm.then_inc(dx[r], 1)
                for r in dirs:
                    turn_x(r, 6)
                for r in dirs:
                    b = s.bank[4 * r:4 * r + 4]
                    pe.wait_ge(kv_ready[r], n + 1)
                    pe.wait_ge(z_ready[r], 6 * n + 6)
                    for h in range(4):
                        cols, hd = slice(h * P, (h + 1) * P), slice(h * HEAD, (h + 1) * HEAD)
                        nc.tensor.matmul(b[0][0:HEAD, cols], s.kg[r][:, hd], s.Z[r][:, cols], start=True, stop=True)
                        mm = nc.tensor.matmul(b[1][:, hd], s.Z[r][:, cols], s.vb[r][:, hd], start=True, stop=True)
                    mm.then_inc(wu_done[r], 1)
                for j in range(2):
                    for r in dirs:
                        c = chunk_order(r)[j]
                        rows, b = slice(c * HEAD, (c + 1) * HEAD), s.bank[4 * r:4 * r + 4]
                        S = (s.S_ctx if n == 0 else s.S_lat)[0:HEAD, r]
                        if j == 0:
                            pe.wait_ge(wu_ready[r], n + 1)
                        if n == 1 and j == 0:
                            pe.wait_ge(state_in, 32)
                        pe.wait_ge(s_ready[r], 2 * n + j) if 2 * n + j else None
                        for h in range(4):
                            hd = slice(h * HEAD, (h + 1) * HEAD)
                            mm = nc.tensor.matmul(b[0][rows, hd], heads(s.swT[r])[0:HEAD, h, rows], S[:, h, :], start=True, stop=True)
                        mm.then_inc(ws_done[r], 1)
                    for r in dirs:
                        c = chunk_order(r)[j]
                        rows, b = slice(c * HEAD, (c + 1) * HEAD), s.bank[4 * r:4 * r + 4]
                        S = (s.S_ctx if n == 0 else s.S_lat)[0:HEAD, r]
                        pe.wait_ge(v_ready[r], 2 * n + j + 1)
                        if j == 0:
                            pe.wait_ge(qd_ready[r], n + 1)
                        else:
                            pe.wait_ge(o_ready[r], 2 * n + 1)
                        for h in range(4):
                            hd = slice(h * HEAD, (h + 1) * HEAD)
                            nc.tensor.matmul(b[2][rows, hd], heads(s.sqd[r])[0:HEAD, h, rows], S[:, h, :], start=True, stop=True)
                            nc.tensor.matmul(b[1][rows, hd], heads(s.attT[r])[rows, h, rows], s.vn[r][rows, hd], start=True, stop=True)
                            mm = nc.tensor.matmul(b[3][0:HEAD, hd], s.kd[r][rows, hd], s.vn[r][rows, hd], start=True, stop=True)
                        mm.then_inc(step_done[r], 1)


def stage_output(nc, s, d):
    sem = s.sem
    wp_in, mapped, pool_out = sem("w_pool_in"), sem("pool_mapped"), sem("pool_out")
    gain_in, squared, summed, std_done, chain, z_done = [sem("fin_" + n) for n in ("gain", "sq", "sum", "std", "chain", "z")]
    finished, turned, dn_out = sem("dn_finished"), sem("mix_turned"), sem("mix_out")
    w_in, g_in, x_in = sem("w_out_in"), sem("g1_in"), [sem(f"xr_in{i}") for i in range(2)]
    product, gated, added = sem("out_product"), sem("out_gated"), sem("out_added")
    rows_in, n2_squared, n2_std, n2_rstd, a_done, h_half, h_ready = [sem("n2_" + n) for n in ("in", "sq", "std", "rstd", "a", "half", "ready")]
    h_stored, zero_set, zeroed = [sem(f"h2_stored{i}") for i in range(2)], sem("zero_set"), sem("slots_zeroed")
    h_turned, h_act, h_dve, logits_done = sem("h2_turned"), sem("h2_act_out"), sem("h2_dve_out"), sem("logits_done")
    o4 = s.o_dn.rearrange("p t (h d) -> p (t h) d", h=DN_H)
    sq4 = s.big_a.rearrange("p (t d) -> p t d", d=HEAD)
    spans = [(POOL_CTX, 0, CTX), (POOL_LAT, CTX, 512), (POOL_LAT + 512, CTX + 512, 512)]
    maps = [(c, span) for c in range(2) for span in spans]
    mix = [s.o_poolT[:, c] for c in range(2)] + [s.o_naT[:, c] for c in range(4)] + [s.o_dnT[:, c] for c in range(2)]
    EARLY = 6

    with nc.Block() as block:
        @block.sync
        def _(sp):
            for g in range(4):
                sp.dma_start(s.w_pool[HEAD * (g % 2):HEAD * (g % 2 + 1), g // 2, :], d["w_pool"][0, g]).then_inc(wp_in, 16)
            sp.dma_start(s.dn_gain, d["dn_norm_g"].to_broadcast([P, HEAD])).then_inc(gain_in, 16)
            wv = d["w_out"][0].rearrange("(k p) n -> p k n", p=P)
            for half in range(2):
                sp.dma_start(s.w_out[:, :, half * 512:(half + 1) * 512], wv[:, :, half * 512:(half + 1) * 512]).then_inc(w_in, 16)
            for c in range(2):
                sp.dma_start(s.g1_row[:, c, :], d["mod_rows"][c:c + 1, 2 * D:3 * D].to_broadcast([P, D])).then_inc(g_in, 16)

            def store_h2(t):
                sp.wait_ge(h_ready, t + 1)
                sp.dma_start(d["h2_rows"][t * P:(t + 1) * P, :], s.h2_ring[t % 2]).then_inc(h_stored[t % 2], 16)

            for t in range(NT):
                if t >= 2:
                    sp.wait_ge(added, t - 1)
                src = d["x_prompt"][0] if t == 0 else d["x_sample"][0, (t - 1) * P:t * P, :]
                sp.dma_start(s.xr_ring[t % 2], src).then_inc(x_in[t % 2], 16)
                if t == 1:
                    sp.wait_ge(finished, 1)
                    for c in range(2):
                        sp.dma_start(s.b2_row[:, c, :], d["mod_rows"][c:c + 1, 3 * D:4 * D].to_broadcast([P, D])).then_inc(rows_in, 16)
                        sp.dma_start(s.a2_row[:, c, :], d["mod_rows"][c:c + 1, 4 * D:5 * D].to_broadcast([P, D])).then_inc(rows_in, 16)
                    sp.dma_start(s.n2_row, d["norm2_g"].to_broadcast([P, D])).then_inc(rows_in, 16)
                    sp.dma_start(s.w_router, d["w_router"].rearrange("(k p) e -> p k e", p=P)).then_inc(rows_in, 16)
                    sp.wait_ge(zero_set, 1)
                    sp.dma_start(d["slot_token"].rearrange("(p a) b -> p (a b)", p=P), s.zero_slots).then_inc(zeroed, 16)
                if t >= 3:
                    store_h2(t - 3)
            for t in range(NT - 3, NT):
                store_h2(t)
            for i in range(2):
                sp.wait_ge(h_stored[i], 16 * len(range(i, NT, 2)))
            sp.wait_ge(zeroed, 16)

        @block.scalar
        def _(act):
            nc.scalar.activation(s.big_a, s.o_dn.rearrange("p t c -> p (t c)"), ACT.Square).then_inc(squared, 1)
            act.wait_ge(summed, 1)
            nc.scalar.activation(s.fin_r, s.fin_r, ACT.Sqrt, bias=s.epsc, scale=1.0 / HEAD).then_inc(std_done, 1)
            nc.scalar.activation(s.big_b.rearrange("p (t c) -> p t c", t=NT), s.zba[:, :, 0:DN_W], ACT.Silu).then_inc(z_done, 1)
            for i, (c, (_, t0, n)) in enumerate(maps):
                act.wait_ge(mapped, i + 1)
                nc.scalar.activation(s.o_poolT[:, c, t0:t0 + n], s.bank[i][:, 0:n], ACT.Copy, scale=s.pscale[:, c:c + 1]).then_inc(pool_out, 1)

            def h2_out(t):
                act.wait_ge(h_turned, t + 1)
                if t >= 2:
                    act.wait_ge(logits_done, t - 1)
                nc.scalar.copy(s.h2T_ring[t % 2][:, 0:4], s.bank[5].rearrange("p (a b) -> p a b", a=4)).then_inc(h_act, 1)

            for t in range(NT):
                if t >= 1:
                    h2_out(t - 1)
                act.wait_ge(added, t + 1)
                nc.scalar.activation(s.junk2, s.x1[:, t, :], ACT.Square, accum_out=s.ss[:, t:t + 1]).then_inc(n2_squared, 1)
                act.wait_ge(n2_squared, t + 1)
                nc.scalar.activation(s.rstd[:, t:t + 1], s.ss[:, t:t + 1], ACT.Sqrt, bias=s.epsc, scale=1.0 / D).then_inc(n2_std, 1)
            h2_out(NT - 1)

        @block.tensor
        def _(pe):
            def turn(t):
                if t >= 1:
                    pe.wait_ge(dn_out, t)
                for c in range(2):
                    tr = nc.tensor.transpose(s.bank[4][:, c * P:(c + 1) * P], s.o_dn[:, t, c * P:(c + 1) * P], s.ident)
                tr.then_inc(turned, 1)

            def products(t, chunks):
                for half in range(2):
                    for k in chunks:
                        mm = nc.tensor.matmul(s.bank[2 * (t % 2) + half], mix[k][:, t * P:(t + 1) * P],
                                              s.w_out[:, k, half * 512:(half + 1) * 512], start=(k == 0), stop=(k == KD - 1))
                return mm

            def early(t):
                if t >= 2:
                    pe.wait_ge(gated, t - 1)
                products(t, range(EARLY))

            def turn_h2(t):
                pe.wait_ge(h_ready, t + 1)
                if t >= 1:
                    pe.wait_ge(h_act, t)
                    pe.wait_ge(h_dve, t)
                for k in range(KD):
                    tr = nc.tensor.transpose(s.bank[5 + k // 4][:, (k % 4) * P:(k % 4 + 1) * P],
                                             s.h2_ring[t % 2][:, k * P:(k + 1) * P], s.ident)
                tr.then_inc(h_turned, 1)

            def logits(t):
                pe.wait_ge(h_act, t + 1)
                pe.wait_ge(h_dve, t + 1)
                if t == 0:
                    pe.wait_ge(rows_in, 96)
                for k in range(KD):
                    mm = nc.tensor.matmul(s.bank[7][:, t * N_EXP:(t + 1) * N_EXP], s.h2T_ring[t % 2][:, k, :],
                                          s.w_router[:, k, :], start=(k == 0), stop=(k == KD - 1))
                mm.then_inc(logits_done, 1)

            pe.wait_ge(wp_in, 64)
            for i, (c, (at, _, n)) in enumerate(maps):
                for half in range(2):
                    rows = slice(half * HEAD, (half + 1) * HEAD)
                    mm = nc.tensor.matmul(s.bank[i][rows, 0:n], s.w_pool[rows, c, :], s.pool_fm[rows, c, at:at + n], start=True, stop=True)
                mm.then_inc(mapped, 1)
            pe.wait_ge(w_in, 32)
            pe.wait_ge(pool_out, len(maps))
            early(0)
            pe.wait_ge(finished, 1)
            turn(0)
            for t in range(NT):
                if t + 1 < NT:
                    early(t + 1)
                    turn(t + 1)
                pe.wait_ge(dn_out, t + 1)
                products(t, range(EARLY, KD)).then_inc(product, 1)
                if t >= 1:
                    turn_h2(t - 1)
                if t >= 2:
                    logits(t - 2)
            logits(NT - 2)
            turn_h2(NT - 1)
            logits(NT - 1)

        @block.vector
        def _(dve):
            dve.wait_ge(squared, 1)
            nc.vector.tensor_reduce(s.fin_r, sq4, AX.X, ALU.add).then_inc(summed, 1)
            dve.wait_ge(std_done, 1)
            nc.vector.reciprocal(s.fin_r, s.fin_r).then_inc(chain, 1)
            dve.wait_ge(chain, 1)
            nc.vector.tensor_tensor(o4, o4, s.fin_r.unsqueeze(2).to_broadcast([P, NT * DN_H, HEAD]), ALU.mult).then_inc(chain, 1)
            dve.wait_ge(chain, 2)
            dve.wait_ge(gain_in, 16)
            nc.vector.tensor_tensor(o4, o4, s.dn_gain.unsqueeze(1).to_broadcast([P, NT * DN_H, HEAD]), ALU.mult).then_inc(chain, 1)
            dve.wait_ge(chain, 3)
            dve.wait_ge(z_done, 1)
            o = s.o_dn.rearrange("p t c -> p (t c)")
            nc.vector.tensor_tensor(o, o, s.big_b, ALU.mult).then_inc(finished, 1)

            def turned_out(t):
                dve.wait_ge(turned, t + 1)
                nc.vector.tensor_copy(s.o_dnT[:, :, t * P:(t + 1) * P],
                                      s.bank[4][:, 0:256].rearrange("p (a b) -> p a b", a=2)).then_inc(dn_out, 1)

            nc.vector.memset(s.zero_slots, 0).then_inc(zero_set, 1)

            def norm(t):
                c = min(t, 1)
                dve.wait_ge(n2_std, t + 1)
                nc.vector.reciprocal(s.rstd[:, t:t + 1], s.rstd[:, t:t + 1]).then_inc(n2_rstd, 1)
                if t == 0:
                    dve.wait_ge(rows_in, 96)
                    for i in range(2):
                        nc.vector.scalar_tensor_tensor(s.a2_row[:, i, :], s.a2_row[:, i, :], 1.0, s.n2_row, ALU.add, ALU.mult).then_inc(a_done, 1)
                    dve.wait_ge(a_done, 2)
                if t >= 2:
                    dve.wait_ge(h_stored[t % 2], 16 * (t // 2))
                    dve.wait_ge(h_turned, t - 1)
                dve.wait_ge(n2_rstd, t + 1)
                nc.vector.scalar_tensor_tensor(s.h2_ring[t % 2], s.x1[:, t, :], s.rstd[:, t:t + 1], s.a2_row[:, c, :],
                                               ALU.mult, ALU.mult).then_inc(h_half, 1)
                dve.wait_ge(h_half, t + 1)
                nc.vector.tensor_tensor(s.h2_ring[t % 2], s.h2_ring[t % 2], s.b2_row[:, c, :], ALU.add).then_inc(h_ready, 1)

            def h2_out(t):
                dve.wait_ge(h_turned, t + 1)
                if t >= 2:
                    dve.wait_ge(logits_done, t - 1)
                nc.vector.tensor_copy(s.h2T_ring[t % 2][:, 4:8], s.bank[6].rearrange("p (a b) -> p a b", a=4)).then_inc(h_dve, 1)

            turned_out(0)
            dve.wait_ge(g_in, 32)
            for t in range(NT):
                if t >= 1:
                    norm(t - 1)
                if t + 1 < NT:
                    turned_out(t + 1)
                dve.wait_ge(product, t + 1)
                nc.vector.tensor_tensor(s.x1[:, t, :], s.pair[t % 2], s.g1_row[:, min(t, 1), :], ALU.mult).then_inc(gated, 1)
                dve.wait_ge(gated, t + 1)
                dve.wait_ge(x_in[t % 2], 16 * (t // 2 + 1))
                nc.vector.tensor_tensor(s.x1[:, t, :], s.x1[:, t, :], s.xr_ring[t % 2], ALU.add).then_inc(added, 1)
                if t >= 1:
                    h2_out(t - 1)
            norm(NT - 1)
            h2_out(NT - 1)


def stage_route(nc, s, d):
    sem = s.sem
    b_in, sig_done, chain, mask_ready, counted = [sem("rt_" + n) for n in ("bias", "sig", "chain", "mask", "counted")]
    slots_ready, scattered, read_back = sem("slots_ready"), sem("slots_scattered"), sem("slots_read")
    g2_in, b_in2, g2_done, g2_ready, g2_stored = sem("g2_ada_in"), sem("g2_bias_in"), sem("g2_done"), sem("g2_ready"), sem("g2_stored")
    R = s.route
    with nc.Block() as block:
        @block.sync
        def _(sp):
            sp.dma_start(s.b_router, d["b_router"].rearrange("(a e) -> a e", a=1).to_broadcast([P, N_EXP])).then_inc(b_in, 16)
            for i in range(2):
                cols = slice(5 * D + i * 512, 5 * D + (i + 1) * 512)
                sp.dma_start(s.g2_ring[i], d["w_ada"][0].rearrange("(k p) n -> p k n", p=P)[:, :, cols]).then_inc(g2_in, 16)
                sp.dma_start(s.mod_late[i][0:2, :], d["b_ada"][:, cols].to_broadcast([2, 512])).then_inc(b_in2, 16)
            for j in range(UNIT_X):
                load_unit(sp, s, d, j)
            sp.wait_ge(scattered, 16 * 2 * NT)
            with nc.allow_non_contiguous_dma(reason="one token number per slot"):
                sp.dma_start(s.slot_idx, d["slot_token"].rearrange("(a p) b -> p (a b)", p=P)).then_inc(read_back, 16)
            sp.wait_ge(read_back, 16)
            sp.wait_ge(g2_ready, 2)
            for i in range(2):
                sp.dma_start(d["mod_rows"][:, 5 * D + i * 512:5 * D + (i + 1) * 512], s.mod_late[i][0:2, :]).then_inc(g2_stored, 16)
            sp.wait_ge(g2_stored, 32)

        @block.scalar
        def _(act):
            nc.scalar.activation(R["score"], s.bank[7][:, 0:NT * N_EXP], ACT.Sigmoid).then_inc(sig_done, 1)

        @block.gpsimd
        def _(pool):
            pool.wait_ge(slots_ready, 1)
            for t in range(NT):
                for which in (s.slot_hi, s.slot_lo):
                    nc.gpsimd.indirect_dma_start(out=d["slot_token"], out_offset=bass.IndirectOffsetOnAxis(ap=which[:, t:t + 1], axis=0),
                                                 in_=s.token_id[:, t:t + 1], in_offset=None).then_inc(scattered, 16)
            pool.wait_ge(scattered, 16 * 2 * NT)

        @block.tensor
        def _(pe):
            pe.wait_ge(mask_ready, 1)
            nc.tensor.matmul(s.bank[5][:, 0:NT * N_EXP], s.before, R["mask"], start=True, stop=True)
            nc.tensor.matmul(s.bank[6][:, 0:NT * N_EXP], s.ones, R["mask"], start=True, stop=True).then_inc(counted, 1)
            pe.wait_ge(g2_in, 32)
            for i in range(2):
                for k in range(KD):
                    mm = nc.tensor.matmul(s.bank[i][0:2, :], s.silu[:, k, :], s.g2_ring[i][:, k, :], start=(k == 0), stop=(k == KD - 1))
            mm.then_inc(g2_done, 1)

        @block.vector
        def _(dve):
            done = [0]

            def link(ins):
                done[0] += 1
                ins.then_inc(chain, 1)
                dve.wait_ge(chain, done[0])

            def tt(out, a, b, op):
                link(nc.vector.tensor_tensor(out, a, b, op))

            def rank4(rank, x, tmp):
                link(nc.vector.memset(rank, 0.0))
                n = x.shape[1]
                for j in range(4):
                    if j > 0:
                        tt(tmp[:, :, 0:j], x[:, :, 0:j], x[:, :, j:j + 1].to_broadcast([P, n, j]), ALU.is_lt)
                        tt(rank[:, :, 0:j], rank[:, :, 0:j], tmp[:, :, 0:j], ALU.add)
                    if j < 3:
                        tt(tmp[:, :, j + 1:4], x[:, :, j + 1:4], x[:, :, j:j + 1].to_broadcast([P, n, 3 - j]), ALU.is_le)
                        tt(rank[:, :, j + 1:4], rank[:, :, j + 1:4], tmp[:, :, j + 1:4], ALU.add)

            g4 = lambda v: v.rearrange("p (n e) -> p n e", e=4)
            t16 = lambda v: v.rearrange("p (t e) -> p t e", e=N_EXP)
            dve.wait_ge(b_in, 16)
            dve.wait_ge(sig_done, 1)
            tt(t16(R["sel"]), t16(R["score"]), s.b_router.unsqueeze(1).to_broadcast([P, NT, N_EXP]), ALU.add)
            rank4(g4(R["rank"]), g4(R["sel"]), g4(R["tmp"]))
            link(nc.vector.tensor_scalar(R["mask"], R["rank"], 1.5, None, ALU.is_lt))
            tt(R["tmp"], R["sel"], R["mask"], ALU.mult)
            link(nc.vector.tensor_reduce(R["gsum"], g4(R["tmp"]), AX.X, ALU.add))
            rank4(g4(R["grank"]), g4(R["gsum"]), g4(R["gtmp"]))
            link(nc.vector.tensor_scalar(R["gmask"], R["grank"], 0.5, None, ALU.is_lt))
            link(nc.vector.tensor_tensor(g4(R["mask"]), g4(R["mask"]), R["gmask"].unsqueeze(2).to_broadcast([P, 36, 4]), ALU.mult))
            nc.vector.nop().then_inc(mask_ready, 1)
            tt(R["weight"], R["score"], R["mask"], ALU.mult)
            link(nc.vector.tensor_reduce(R["wsum"], t16(R["weight"]), AX.X, ALU.add))
            link(nc.vector.reciprocal(R["wsum"], R["wsum"]))
            tt(t16(R["weight"]), t16(R["weight"]), R["wsum"].unsqueeze(2).to_broadcast([P, NT, N_EXP]), ALU.mult)
            dve.wait_ge(counted, 1)
            count = t16(s.bank[6][:, 0:NT * N_EXP])
            off = t16(R["off"])
            link(nc.vector.memset(off[:, 0, :], 0.0))
            for t in range(1, NT):
                tt(off[:, t, :], off[:, t - 1, :], count[:, t - 1, :], ALU.add)
            tt(R["total"], off[:, NT - 1, :], count[:, NT - 1, :], ALU.add)
            tt(R["slot"], R["off"], s.bank[5][:, 0:NT * N_EXP], ALU.add)
            link(nc.vector.memset(R["over"], 0.0))
            for k in range((N_TOK - CAP + P - 1) // P):
                link(nc.vector.tensor_scalar(R["o16"], R["total"], CAP + k * P + 0.5, None, ALU.is_gt))
                tt(R["over"], R["over"], R["o16"], ALU.add)
            link(nc.vector.tensor_tensor_scan(R["cum"], s.ones[:, 0:N_EXP], R["over"], 0.0, ALU.mult, ALU.add))
            tt(R["o16"], R["cum"], R["over"], ALU.subtract)
            link(nc.vector.tensor_scalar(R["o16"], R["o16"], float(P), float((N_EXP - 1) * CAP), ALU.mult, ALU.add))
            tt(R["o16"], R["o16"], s.grid16, ALU.subtract)
            link(nc.vector.tensor_scalar(R["tmp"], R["slot"], CAP - 0.5, None, ALU.is_gt))
            tt(t16(R["tmp"]), t16(R["tmp"]), R["o16"].unsqueeze(1).to_broadcast([P, NT, N_EXP]), ALU.mult)
            tt(R["slot"], R["slot"], R["tmp"], ALU.add)
            tt(t16(R["slot"]), t16(R["slot"]), s.grid16.unsqueeze(1).to_broadcast([P, NT, N_EXP]), ALU.add)
            tt(R["slot"], R["slot"], R["mask"], ALU.mult)
            link(nc.vector.tensor_reduce(R["hi"], t16(R["slot"]), AX.X, ALU.max))
            link(nc.vector.tensor_reduce(R["lo"], t16(R["slot"]), AX.X, ALU.add))
            tt(R["lo"], R["lo"], R["hi"], ALU.subtract)
            link(nc.vector.tensor_copy(s.slot_hi, R["hi"]))
            link(nc.vector.tensor_copy(s.slot_lo, R["lo"]))
            link(nc.vector.tensor_copy(s.token_id, s.token))
            nc.vector.nop().then_inc(slots_ready, 1)
            tt(t16(R["tmp"]), t16(R["slot"]), R["hi"].unsqueeze(2).to_broadcast([P, NT, N_EXP]), ALU.is_equal)
            tt(R["rank"], R["weight"], R["tmp"], ALU.mult)
            link(nc.vector.tensor_reduce(s.w_hi, t16(R["rank"]), AX.X, ALU.add))
            tt(R["rank"], R["weight"], R["rank"], ALU.subtract)
            link(nc.vector.tensor_reduce(s.w_lo, t16(R["rank"]), AX.X, ALU.add))
            ex = R["rank"][:, 0:OVER].rearrange("p (a b) -> p a b", b=1)
            wide = s.over_cmp
            link(nc.vector.tensor_tensor(wide, R["cum"].unsqueeze(1).to_broadcast([P, OVER, N_EXP]),
                                         s.over_id.unsqueeze(2).to_broadcast([P, OVER, N_EXP]), ALU.is_le))
            link(nc.vector.tensor_reduce(R["tmp"][:, 0:OVER], wide, AX.X, ALU.add))
            link(nc.vector.tensor_scalar(R["tmp"][:, 0:OVER], R["tmp"][:, 0:OVER], float(N_EXP - 1), None, ALU.min))
            nc.vector.tensor_copy(s.over_table[:, 0:OVER], R["tmp"][:, 0:OVER])
            nc.vector.tensor_copy(s.over_table[:, OVER:OVER + 1], R["cum"][:, N_EXP - 1:N_EXP])
            dve.wait_ge(g2_done, 1)
            dve.wait_ge(b_in2, 32)
            for i in range(2):
                nc.vector.tensor_tensor(s.mod_late[i][0:2, :], s.bank[i][0:2, :], s.mod_late[i][0:2, :], ALU.add).then_inc(g2_ready, 1)


def unit_source(d, j):
    e, half = j // UNITS, (j % UNITS) // 2 % 2
    kind = ("w_gate", "w_up", "w_gate", "w_up", "w_down", "w_down")[j % UNITS]
    if kind == "w_down":
        half = j % 2
    src = d[kind][0, e].rearrange("(k p) n -> p k n", p=P)
    k = src.shape[1] // 2
    return src[:, half * k:(half + 1) * k, :]


def load_unit(sp, s, d, j):
    src = unit_source(d, j)
    sp.dma_start(s.unit_x[j % UNIT_X].rearrange("p (k n) -> p k n", n=src.shape[2]), src).then_inc(s.unit_in[j % UNIT_X], 16)


def stage_experts(nc, s, d):
    sem = s.sem
    high_done, low_done, first_half = sem("unit_high"), sem("unit_low"), sem("first_half")
    gathered, turned, rows_high, rows_low = sem("gathered"), sem("hg_turned"), sem("rows_high"), sem("rows_low")
    gate_up, silu_done, hid_done = sem("gate_up"), sem("hid_silu"), sem("hid_done")
    hid_high, hid_low, down_done = sem("hid_high"), sem("hid_low"), sem("down_done")
    y_act, y_dve, y_stored = sem("y_act"), sem("y_dve"), [sem(f"y_stored{i}") for i in range(3)]
    FB, KH = FF // P, KD // 2
    N_UNITS = UNITS * N_EXP

    def high(j, n):
        return s.unit_high[j % UNIT_H].rearrange("p (k n) -> p k n", n=n)

    def low(j, n):
        return s.unit_low[j % UNIT_X].rearrange("p (k n) -> p k n", n=n)

    def multiplied(eng, j):
        e, k = j // UNITS, j % UNITS
        if k < 2:
            eng.wait_ge(first_half, e + 1)
        elif k < 4:
            eng.wait_ge(gate_up, FB * (e + 1))
        else:
            eng.wait_ge(down_done, 2 * (e + 1))

    with nc.Block() as block:
        @block.sync
        def _(sp):
            for j in range(UNIT_X, N_UNITS):
                multiplied(sp, j - UNIT_X)
                load_unit(sp, s, d, j)

        @block.gpsimd
        def _(pool):
            for e in range(N_EXP):
                if e >= 1:
                    pool.wait_ge(turned, 2 * e)
                for i in range(2):
                    nc.gpsimd.indirect_dma_start(out=s.hg_rows[:, i, :], out_offset=None, in_=d["h2_rows"],
                                                 in_offset=bass.IndirectOffsetOnAxis(ap=s.slot_idx[:, 2 * e + i:2 * e + i + 1], axis=0)
                                                 ).then_inc(gathered, 16)

        @block.scalar
        def _(act):
            def split(j):
                if j >= N_UNITS:
                    return
                act.wait_ge(s.unit_in[j % UNIT_X], 16 * (j // UNIT_X + 1))
                if j >= UNIT_H:
                    multiplied(act, j - UNIT_H)
                nc.scalar.copy(s.unit_high[j % UNIT_H], s.unit_x[j % UNIT_X]).then_inc(high_done, 1)

            def turned_out(e):
                for i in range(2):
                    act.wait_ge(turned, 2 * e + i + 1)
                    for b in range(2):
                        nc.scalar.copy(s.hgT_high[:, 4 * b:4 * b + 4, i * P:(i + 1) * P],
                                       s.bank[2 * i + b].rearrange("p (a b) -> p a b", a=4)).then_inc(rows_high, 1)

            def hid_split(u):
                act.wait_ge(hid_done, u + 1)
                nc.scalar.copy(s.hid_high[:, u % FB, :], s.hid_whole[u % 2]).then_inc(hid_high, 1)

            split(0)
            split(1)
            turned_out(0)
            for e in range(N_EXP):
                for j in range(2, UNITS):
                    split(UNITS * e + j)
                for f in range(FB):
                    u = FB * e + f
                    act.wait_ge(gate_up, u + 1)
                    if u >= 2:
                        act.wait_ge(hid_done, u - 1)
                    nc.scalar.activation(s.sg[u % 2], s.bank[4 + f][:, 0:CAP], ACT.Silu).then_inc(silu_done, 1)
                    if f >= 1:
                        hid_split(u - 1)
                hid_split(FB * e + FB - 1)
                if e + 1 < N_EXP:
                    turned_out(e + 1)
                split(UNITS * (e + 1))
                split(UNITS * (e + 1) + 1)
                for i in range(2):
                    v = 2 * e + i
                    act.wait_ge(down_done, v + 1)
                    if v >= 3:
                        act.wait_ge(y_stored[v % 3], 16 * (v // 3))
                    nc.scalar.copy(s.y_rows[v % 3][:, 0:512], s.bank[2 * i]).then_inc(y_act, 1)
                    act.wait_ge(y_act, v + 1)
                    act.wait_ge(y_dve, v + 1)
                    act.dma_start(d["slot_rows"][v * P:(v + 1) * P, :], s.y_rows[v % 3]).then_inc(y_stored[v % 3], 16)
            for i in range(3):
                act.wait_ge(y_stored[i], 16 * len(range(i, 2 * N_EXP, 3)))

        @block.vector
        def _(dve):
            def split(j):
                if j >= N_UNITS:
                    return
                dve.wait_ge(high_done, j + 1)
                nc.vector.tensor_tensor(s.unit_low[j % UNIT_X], s.unit_x[j % UNIT_X], s.unit_high[j % UNIT_H].bitcast(F32), ALU.subtract).then_inc(low_done, 1)

            def turned_out(e):
                for i in range(2):
                    for b in range(2):
                        dve.wait_ge(rows_high, 4 * e + 2 * i + b + 1)
                        cols = slice(i * P, (i + 1) * P)
                        nc.vector.tensor_tensor(s.hgT_low[:, 4 * b:4 * b + 4, cols], s.bank[2 * i + b].rearrange("p (a b) -> p a b", a=4),
                                                s.hgT_high[:, 4 * b:4 * b + 4, cols].bitcast(F32), ALU.subtract).then_inc(rows_low, 1)

            def hid_split(u):
                dve.wait_ge(hid_high, u + 1)
                nc.vector.tensor_tensor(s.hid_low[:, u % FB, :], s.hid_whole[u % 2], s.hid_high[:, u % FB, :].bitcast(F32),
                                        ALU.subtract).then_inc(hid_low, 1)

            split(0)
            split(1)
            turned_out(0)
            for e in range(N_EXP):
                for j in range(2, UNITS):
                    split(UNITS * e + j)
                for f in range(FB):
                    u = FB * e + f
                    dve.wait_ge(silu_done, u + 1)
                    if u >= 2:
                        dve.wait_ge(hid_low, u - 1)
                    nc.vector.tensor_tensor(s.hid_whole[u % 2], s.sg[u % 2], s.bank[4 + f][:, CAP:2 * CAP], ALU.mult).then_inc(hid_done, 1)
                    if f >= 1:
                        hid_split(u - 1)
                hid_split(FB * e + FB - 1)
                if e + 1 < N_EXP:
                    turned_out(e + 1)
                split(UNITS * (e + 1))
                split(UNITS * (e + 1) + 1)
                for i in range(2):
                    v = 2 * e + i
                    dve.wait_ge(down_done, v + 1)
                    if v >= 3:
                        dve.wait_ge(y_stored[v % 3], 16 * (v // 3))
                    nc.vector.tensor_copy(s.y_rows[v % 3][:, 512:1024], s.bank[2 * i + 1]).then_inc(y_dve, 1)

        @block.tensor
        def _(pe):
            def three(out, w, x, first, last):
                nc.tensor.matmul(out, w[0], x[0], start=first, stop=False)
                nc.tensor.matmul(out, w[0], x[1], start=False, stop=False)
                return nc.tensor.matmul(out, w[1], x[0], start=False, stop=last)

            def turn(e):
                pe.wait_ge(gathered, 32 * (e + 1))
                for i in range(2):
                    if e >= 2:
                        pe.wait_ge(y_act, 2 * (e - 2) + i + 1)
                        pe.wait_ge(y_dve, 2 * (e - 2) + i + 1)
                    for k in range(KD):
                        tr = nc.tensor.transpose(s.bank[2 * i + k // 4][:, (k % 4) * P:(k % 4 + 1) * P],
                                                 s.hg_rows[:, i, k * P:(k + 1) * P], s.ident)
                    tr.then_inc(turned, 1)

            def gate_up_half(e, h):
                j = UNITS * e + 2 * h
                pe.wait_ge(low_done, j + 2)
                order = [(k, f) for k in range(KH) for f in range(FB)] if h == 0 else [(k, f) for f in range(FB) for k in range(KH)]
                for k, f in order:
                    for w in range(2):
                        cols = slice(f * P, (f + 1) * P)
                        kk = h * KH + k
                        mm = three(s.bank[4 + f][:, w * CAP:(w + 1) * CAP], (high(j + w, FF)[:, k, cols], low(j + w, FF)[:, k, cols]),
                                   (s.hgT_high[:, kk, :], s.hgT_low[:, kk, :]), (kk, w) == (0, 0), (kk, w) == (KD - 1, 1))
                    if h == 1 and k == KH - 1:
                        mm.then_inc(gate_up, 1)
                if h == 0:
                    mm.then_inc(first_half, 1)

            def down(e):
                j = UNITS * e + 4
                pe.wait_ge(low_done, j + 2)
                for i in range(2):
                    rows = slice(i * P, (i + 1) * P)
                    if e + 1 < N_EXP:
                        pe.wait_ge(rows_low, 4 * (e + 1) + 2 * (i + 1))
                    elif e >= 1:
                        pe.wait_ge(y_act, 2 * (e - 1) + i + 1)
                        pe.wait_ge(y_dve, 2 * (e - 1) + i + 1)
                    for f in range(FB):
                        if i == 0:
                            pe.wait_ge(hid_high, FB * e + f + 1)
                            pe.wait_ge(hid_low, FB * e + f + 1)
                        for half in range(2):
                            cols = slice(half * 512, (half + 1) * 512)
                            mm = three(s.bank[2 * i + half], (s.hid_high[:, f, rows], s.hid_low[:, f, rows]),
                                       (high(j + f // 2, D)[:, f % 2, cols], low(j + f // 2, D)[:, f % 2, cols]), f == 0, f == FB - 1)
                    mm.then_inc(down_done, 1)

            turn(0)
            for e in range(N_EXP):
                pe.wait_ge(rows_high, 4 * (e + 1))
                pe.wait_ge(rows_low, 4 * (e + 1))
                if e >= 1:
                    pe.wait_ge(hid_done, FB * e)
                gate_up_half(e, 0)
                gate_up_half(e, 1)
                if e + 1 < N_EXP:
                    turn(e + 1)
                down(e)


def stage_further(nc, s, d):
    n_over = nc.values_load(s.over_table[0:1, OVER:OVER + 1], min_val=0, max_val=OVER)
    first = N_EXP * CAP
    FB = FF // P
    Wv = [s.we_ring[j].rearrange("p (k n) -> p k n", n=(FF, FF, D)[j]) for j in range(3)]
    kinds = ("w_gate", "w_up", "w_down")
    sem = s.sem
    idx_in, w_in, rows_in, turned, out = sem("fu_idx"), sem("fu_w"), sem("fu_rows"), sem("fu_turned"), sem("fu_out")
    gate_up, silu_done, hid_ready, down, y_ready, stored = [sem("fu_" + n) for n in ("gate_up", "silu", "hid", "down", "y", "stored")]
    counted = [idx_in, w_in, turned, out, gate_up, silu_done, hid_ready, down, y_ready, stored]
    with nc.If(n_over > 0):
        with nc.Fori(0, OVER) as o:
            with nc.Block() as block:
                @block.sync
                def _(sp):
                    with nc.allow_non_contiguous_dma(reason="one token number per slot"):
                        sp.dma_start(s.further_idx, d["slot_token"][bass.ds(first + o * P, P), :]).then_inc(idx_in, 16)
                    e = sp.value_load(s.over_table[0:1, bass.ds(o, 1)], min_val=0, max_val=N_EXP - 1)
                    for j, kind in enumerate(kinds):
                        src = d[kind][0].rearrange("e (k p) n -> p (e k) n", p=P)
                        k = src.shape[1] // N_EXP
                        sp.dma_start(Wv[j], src[:, bass.ds(e * k, k), :]).then_inc(w_in, 16)
                    sp.wait_ge(y_ready, 4)
                    sp.dma_start(d["slot_rows"][bass.ds(first + o * P, P), :], s.y_ring[0]).then_inc(stored, 16)
                    sp.wait_ge(stored, 16)

                @block.gpsimd
                def _(pool):
                    pool.wait_ge(idx_in, 16)
                    nc.gpsimd.indirect_dma_start(out=s.hg[0][:, 0, :], out_offset=None, in_=d["h2_rows"],
                                                 in_offset=bass.IndirectOffsetOnAxis(ap=s.further_idx, axis=0)).then_inc(rows_in, 16)
                    pool.wait_ge(rows_in, o * 16 + 16)

                @block.tensor
                def _(pe):
                    pe.wait_ge(rows_in, o * 16 + 16)
                    for k in range(KD):
                        tr = nc.tensor.transpose(s.bank[k // 4][:, (k % 4) * P:(k % 4 + 1) * P], s.hg[0][:, 0, k * P:(k + 1) * P], s.ident)
                    tr.then_inc(turned, 1)
                    pe.wait_ge(out, 2)
                    pe.wait_ge(w_in, 48)
                    for f in range(FB):
                        for j in range(2):
                            for k in range(KD):
                                mm = nc.tensor.matmul(s.bank[2 + f][:, j * P:(j + 1) * P], Wv[j][:, k, f * P:(f + 1) * P],
                                                      s.hgT[0][:, k, 0:P], start=(k == 0), stop=(k == KD - 1))
                        mm.then_inc(gate_up, 1)
                    pe.wait_ge(hid_ready, FB)
                    for half in range(2):
                        for f in range(FB):
                            mm = nc.tensor.matmul(s.bank[6 + half], s.hid[0][:, f, 0:P], Wv[2][:, f, half * 512:(half + 1) * 512],
                                                  start=(f == 0), stop=(f == FB - 1))
                    mm.then_inc(down, 1)

                @block.scalar
                def _(act):
                    act.wait_ge(turned, 1)
                    for half in range(2):
                        nc.scalar.copy(s.hgT[0][:, 4 * half:4 * half + 4, 0:P], s.bank[half].rearrange("p (a b) -> p a b", a=4)).then_inc(out, 1)
                    for f in range(FB):
                        act.wait_ge(gate_up, f + 1)
                        nc.scalar.activation(s.further_gate[:, f, :], s.bank[2 + f][:, 0:P], ACT.Silu).then_inc(silu_done, 1)

                @block.vector
                def _(dve):
                    for f in range(FB):
                        dve.wait_ge(silu_done, f + 1)
                        nc.vector.tensor_tensor(s.hid[0][:, f, 0:P], s.further_gate[:, f, :], s.bank[2 + f][:, P:2 * P], ALU.mult).then_inc(hid_ready, 1)
                    dve.wait_ge(down, 1)
                    for half in range(2):
                        nc.vector.tensor_copy(s.y_ring[0][:, half * 512:(half + 1) * 512], s.bank[6 + half]).then_inc(y_ready, 2)
            for one in counted:
                nc.sync.sem_clear(one)
            nc.all_engine_barrier()
    nc.end_ifs()


def stage_combine(nc, s, d):
    sem = s.sem
    g_in, in_hi, in_lo = sem("g2_in"), [sem(f"y_hi{i}") for i in range(3)], [sem(f"y_lo{i}") for i in range(3)]
    weighted, summed, gated, ready, stored = sem("y_weighted"), sem("y_summed"), sem("y_gated"), sem("y_ready"), s.out_sem["y_out"]
    with nc.Block() as block:
        @block.sync
        def _(sp):
            for c in range(2):
                sp.dma_start(s.g2_row[:, c, :], d["mod_rows"][c:c + 1, 5 * D:6 * D].to_broadcast([P, D])).then_inc(g_in, 16)
            for t in range(NT):
                sp.wait_ge(ready, t + 1)
                dst = d["out_y_prompt"][0] if t == 0 else d["out_y_sample"][0, (t - 1) * P:t * P, :]
                sp.dma_start(dst, s.x1[:, t, :]).then_inc(stored, 16)
            sp.wait_ge(stored, 16 * NT)

        @block.gpsimd
        def _(pool):
            for t in range(NT):
                if t >= 3:
                    pool.wait_ge(ready, t - 2)
                for buf, idx, got in ((s.y_hi, s.slot_hi, in_hi), (s.y_lo, s.slot_lo, in_lo)):
                    nc.gpsimd.indirect_dma_start(out=buf[t % 3], out_offset=None, in_=d["slot_rows"],
                                                 in_offset=bass.IndirectOffsetOnAxis(ap=idx[:, t:t + 1], axis=0)).then_inc(got[t % 3], 16)

        @block.scalar
        def _(act):
            for t in range(NT):
                a = s.y_hi[t % 3]
                act.wait_ge(in_hi[t % 3], 16 * (t // 3 + 1))
                nc.scalar.activation(a, a, ACT.Copy, scale=s.w_hi[:, t:t + 1]).then_inc(weighted, 1)

        @block.vector
        def _(dve):
            dve.wait_ge(g_in, 32)

            def mixed(t):
                a, b = s.y_hi[t % 3], s.y_lo[t % 3]
                dve.wait_ge(weighted, t + 1)
                dve.wait_ge(in_lo[t % 3], 16 * (t // 3 + 1))
                nc.vector.scalar_tensor_tensor(a, b, s.w_lo[:, t:t + 1], a, ALU.mult, ALU.add).then_inc(summed, 1)
                dve.wait_ge(summed, t + 1)
                nc.vector.tensor_tensor(a, a, s.g2_row[:, min(t, 1), :], ALU.mult).then_inc(gated, 1)

            mixed(0)
            for t in range(NT):
                if t + 1 < NT:
                    mixed(t + 1)
                dve.wait_ge(gated, t + 1)
                nc.vector.tensor_tensor(s.x1[:, t, :], s.x1[:, t, :], s.y_hi[t % 3], ALU.add).then_inc(ready, 1)


def constants():
    import numpy as np
    i = np.arange(P)
    same = (i[:, None] // HEAD) == (i[None, :] // HEAD)
    out = {
        "ident": np.eye(P),
        "tri_f": same & (i[:, None] <= i[None, :]),
        "tri_b": same & (i[:, None] >= i[None, :]),
        "block": same,
        "strict_f": same & (i[:, None] > i[None, :]),
        "strict_b": same & (i[:, None] < i[None, :]),
        "before": i[:, None] < i[None, :],
        "ones": np.ones((P, P)),
        "grid16": np.tile(np.arange(16) * CAP, (P, 1)),
        "over_id": np.tile(np.arange(OVER), (P, 1)),
        "token": np.arange(NT)[None, :] * P + i[:, None],
    }
    level = []
    for b in range(6):
        size = 1 << b
        bi, bj = i[:, None] // size, i[None, :] // size
        level.append((bi % 2 == 1) & (bj == bi - 1))
    out["level_f"] = np.concatenate(level, axis=1)
    out["level_b"] = np.concatenate([m.T for m in level], axis=1)
    q = (i % GRID)[:, None]
    k = np.arange(GRID)[None, :]
    start = np.clip(q - 8, 0, GRID - 16)
    out["colmask"] = np.where((k >= start) & (k < start + 16), 0.0, NEG)
    return np.concatenate([np.asarray(out[n], np.float32) for n in CST], axis=1)


def pool_counts():
    import numpy as np
    out = np.ones((P, 2, POOL_ROW), np.float32)
    for g, win in enumerate((2, 4, 8, 16)):
        for at, n in ((POOL_CTX, CTX), (POOL_LAT, LAT)):
            t = np.arange(n)
            count = np.clip(t + win - win // 2, 0, n) - np.clip(t - win // 2, 0, n)
            out[HEAD * (g % 2):HEAD * (g % 2 + 1), g // 2, at:at + n] = 1.0 / count
    return out


STAGES = [stage_modulation, stage_norm1, stage_project, stage_heads, stage_attention,
          stage_dn_prepare, stage_dn_scan, stage_output, stage_route, stage_experts, stage_further, stage_combine]

IN_SHAPES = {
    "x_prompt": (1, CTX, D), "x_sample": (1, LAT, D), "cache_na_k": (1, 1, NA_H, PAST, HEAD),
    "cache_na_v": (1, 1, NA_H, PAST, HEAD), "state_dn": (1, 1, 2, DN_H, HEAD, HEAD), "c": (1, D), "c_ctx": (D,),
    "norm1_g": (1, D), "norm2_g": (1, D), "w_ada": (1, D, 6 * D), "b_ada": (1, 6 * D), "w_in": (1, D, IN_W),
    "w_out": (1, D, D), "w_pool": (1, 4, HEAD, HEAD), "pool_scale": (1, POOL_W), "q_norm_g": (1, HEAD),
    "k_norm_g": (1, HEAD), "dn_conv_w": (1, 4, 3 * DN_W), "dn_a_log": (1, 2, DN_H), "dn_dt_bias": (1, 2, DN_H),
    "dn_norm_g": (1, HEAD), "w_router": (D, N_EXP), "b_router": (N_EXP,), "w_gate": (1, N_EXP, D, FF),
    "w_up": (1, N_EXP, D, FF), "w_down": (1, N_EXP, FF, D),
}


def declare(nc, inputs):
    import numpy as np
    arrays, d = {}, {}
    own = {name: inputs[name] for name in IN_SHAPES}
    own["rpb"] = inputs["rpb"]
    own["consts"] = constants()
    own["pool_counts"] = pool_counts()
    for name, a in own.items():
        a = np.ascontiguousarray(a)
        arrays[f"in_{name}"] = a
        d[name] = nc.dram_tensor(f"in_{name}", a.shape, F32, kind="ExternalInput").ap()
    outs = [("out_y_prompt", (1, CTX, D)), ("out_y_sample", (1, LAT, D)), ("out_k", (1, 1, NA_H, CTX, HEAD)),
            ("out_v", (1, 1, NA_H, CTX, HEAD)), ("out_state", (1, 1, 2, DN_H, HEAD, HEAD))]
    for name, shape in outs:
        d[name] = nc.dram_tensor(name, shape, F32, kind="ExternalOutput").ap()
    d["rpb_rows"] = nc.dram_tensor("rpb_rows", (NA_H * 15, RPB_ROW), F32).ap()
    d["mod_rows"] = nc.dram_tensor("mod_rows", (2, 6 * D), F32).ap()
    d["h2_rows"] = nc.dram_tensor("h2_rows", (N_TOK, D), F32).ap()
    d["slot_token"] = nc.dram_tensor("slot_token", (SLOTS, 1), U32).ap()
    d["slot_rows"] = nc.dram_tensor("slot_rows", (SLOTS, D), F32).ap()
    s = Store()
    s.out_sem = {name: nc.alloc_semaphore(name) for name in ("v_stored", "kn_stored", "state_out", "y_out")}
    s.x_in = [nc.alloc_semaphore(f"x_in{i}") for i in range(NT)]
    s.late_in = [nc.alloc_semaphore(f"late_in{i}") for i in range(3)]
    s.w_loaded = [nc.alloc_semaphore(f"w_in_loaded{i}") for i in range(2)]
    s.unit_in = [nc.alloc_semaphore(f"unit_in{i}") for i in range(UNIT_X)]
    s.WORDS = 53120
    views(nc, s)
    psum = nc.alloc_psum_tensor("psum", [P, 8 * 512], F32)
    s.bank = [psum[:, 512 * i:512 * (i + 1)] for i in range(8)]
    s.pair = [psum[:, 1024 * i:1024 * (i + 1)] for i in range(4)]
    return arrays, d, [n for n, _ in outs], s


def run_stage(nc, s, d, stage):
    held = []

    def sem(name):
        held.append(nc.alloc_semaphore(name))
        return held[-1]

    s.sem = sem
    stage(nc, s, d)
    nc.clear_and_free_semaphores(held)
    nc.all_engine_barrier()


def kernel(**inputs):
    import concourse.bacc as bacc
    from concourse.bass_utils import run_bass_kernel_spmd

    nc = bacc.Bacc("TRN2", target_bir_lowering=False, num_devices=1)
    arrays, d, outs, s = declare(nc, inputs)
    for stage in STAGES:
        run_stage(nc, s, d, stage)
    r = run_bass_kernel_spmd(nc, [arrays], core_ids=[0])
    return tuple(r.results[0][name] for name in outs)
```
